# Optimizing a Trainium2 kernel written in Bass

```python
import jax, jax.numpy as jnp
from jax import lax
import numpy as np

D_MODEL = 2048
BATCH = 1
SEQ = 512
DEPTH = 1

CHUNK = 64
N_MIXERS = 2
EPS = 1e-6

SSM_EXPAND = 2
D_INNER = SSM_EXPAND * D_MODEL
SSM_HEADDIM = 64
SSM_HEADS = D_INNER // SSM_HEADDIM
SSM_GROUPS = 8
SSM_HEADS_PER_GROUP = SSM_HEADS // SSM_GROUPS
SSM_STATE = 128
SSM_CONV = 4
SSD_CHUNK = CHUNK
CONV_DIM = D_INNER + 2 * SSM_GROUPS * SSM_STATE
SSM_IN = D_INNER + CONV_DIM + SSM_HEADS
DT_MIN = 1e-3
DT_MAX = 1e-1

POOL_EXPAND = 2
D_POOL = POOL_EXPAND * D_MODEL
POOL_WINDOWS = (2, 4, 8, 16)
POOL_GROUPS = len(POOL_WINDOWS)
POOL_GROUP_DIM = D_POOL // POOL_GROUPS


def rmsnorm(x, g):
    xf = x.astype(jnp.float32)
    y = xf * lax.rsqrt(jnp.mean(xf * xf, axis=-1, keepdims=True) + EPS)
    return (y * g.astype(jnp.float32)).astype(x.dtype)

def causal_depthwise_conv(x, w, b):
    k_taps = w.shape[0]
    length = x.shape[1]
    xp = jnp.pad(x, ((0, 0), (k_taps - 1, 0), (0, 0)))
    y = b
    for k in range(k_taps):
        y = y + xp[:, k:k + length] * w[k]
    return y

def ssd_chunked_scan(xdt, a_dt, bm, cm):
    bsz, length, g, r, p = xdt.shape
    n = bm.shape[-1]
    n_chunks = length // SSD_CHUNK

    def to_chunks(t):
        t = t.reshape((bsz, n_chunks, SSD_CHUNK) + t.shape[2:])
        return jnp.moveaxis(t, 1, 0)

    mask = jnp.tril(jnp.ones((SSD_CHUNK, SSD_CHUNK), dtype=bool))[None, :, :, None, None]

    def step(state, inp):
        xc, ac, bc, cc = inp
        cs = jnp.cumsum(ac, axis=1)
        seg = cs[:, :, None] - cs[:, None, :]
        decay = jnp.exp(jnp.where(mask, seg, -jnp.inf))
        cb = jnp.einsum("blgn,bsgn->blsg", cc, bc)
        y_diag = jnp.einsum("blsg,blsgr,bsgrp->blgrp", cb, decay, xc)
        y_off = jnp.einsum("blgn,bgrpn,blgr->blgrp", cc, state, jnp.exp(cs))
        last = cs[:, -1]
        w_in = jnp.exp(last[:, None] - cs)
        new_state = state * jnp.exp(last)[..., None, None] + jnp.einsum(
            "bsgn,bsgr,bsgrp->bgrpn", bc, w_in, xc)
        return new_state, y_diag + y_off

    state0 = jnp.zeros((bsz, g, r, p, n), jnp.float32)
    _, ys = lax.scan(step, state0, (to_chunks(xdt), to_chunks(a_dt), to_chunks(bm), to_chunks(cm)))
    return jnp.moveaxis(ys, 0, 1).reshape(bsz, length, g, r, p)

def ssm_mixer(h, w_in, conv_w, conv_b, dt_bias, a_log, d_skip, norm_g, w_out):
    bsz, length, _ = h.shape
    g, r, p, n = SSM_GROUPS, SSM_HEADS_PER_GROUP, SSM_HEADDIM, SSM_STATE
    proj = h @ w_in
    z = proj[..., :D_INNER]
    xbc = proj[..., D_INNER:D_INNER + CONV_DIM]
    dt = proj[..., D_INNER + CONV_DIM:]
    xbc = jax.nn.silu(causal_depthwise_conv(xbc, conv_w, conv_b)).astype(jnp.float32)
    xs = xbc[..., :D_INNER].reshape(bsz, length, g, r, p)
    bm = xbc[..., D_INNER:D_INNER + g * n].reshape(bsz, length, g, n)
    cm = xbc[..., D_INNER + g * n:].reshape(bsz, length, g, n)
    dt = jax.nn.softplus(dt.astype(jnp.float32) + dt_bias.astype(jnp.float32))
    dt = dt.reshape(bsz, length, g, r)
    a = -jnp.exp(a_log.astype(jnp.float32)).reshape(g, r)
    y = ssd_chunked_scan(xs * dt[..., None], dt * a, bm, cm)
    y = y + d_skip.astype(jnp.float32).reshape(g, r, 1) * xs
    y = y.reshape(bsz, length, D_INNER) * jax.nn.silu(z.astype(jnp.float32))
    y = rmsnorm(y, norm_g)
    return y.astype(h.dtype) @ w_out

def pool_mixer(h, w_in, w_group, scale, w_out):
    bsz, length, _ = h.shape
    proj = h @ w_in
    u = proj[..., :D_POOL].astype(jnp.float32).reshape(bsz, length, POOL_GROUPS, POOL_GROUP_DIM)
    gate = proj[..., D_POOL:].astype(jnp.float32)
    cs = jnp.cumsum(u, axis=1)
    pos = jnp.arange(1, length + 1, dtype=jnp.int32)
    means = []
    for gi, win in enumerate(POOL_WINDOWS):
        c = cs[:, :, gi]
        shifted = jnp.pad(c, ((0, 0), (win, 0), (0, 0)))[:, :length]
        cnt = jnp.minimum(pos, win).astype(jnp.float32)[None, :, None]
        means.append((c - shifted) / cnt)
    mixed = jnp.stack(means, axis=2) - u
    mixed = jnp.einsum("blgc,gcd->blgd", mixed, w_group.astype(jnp.float32))
    mixed = mixed.reshape(bsz, length, D_POOL) * scale.astype(jnp.float32)
    y = mixed * jax.nn.silu(gate)
    return y.astype(h.dtype) @ w_out

def first_inputs(seed: int = 0) -> dict:
    key = jax.random.key(seed)
    ks = jax.random.split(key, 20)
    n_a = (DEPTH + N_MIXERS - 1) // N_MIXERS
    n_b = DEPTH // N_MIXERS
    f32 = jnp.float32
    x = jax.random.normal(ks[0], (BATCH, SEQ, D_MODEL), f32)
    ln_g = 1.0 + 0.05 * jax.random.normal(ks[1], (DEPTH, D_MODEL), f32)
    final_g = 1.0 + 0.05 * jax.random.normal(ks[2], (D_MODEL,), f32)
    ssm_w_in = jax.random.normal(ks[3], (n_a, D_MODEL, SSM_IN), f32) * D_MODEL ** -0.5
    ssm_conv_w = jax.random.normal(ks[4], (n_a, SSM_CONV, CONV_DIM), f32) * SSM_CONV ** -0.5
    ssm_conv_b = 0.01 * jax.random.normal(ks[5], (n_a, CONV_DIM), f32)
    u_dt = jax.random.uniform(ks[6], (n_a, SSM_HEADS), f32)
    dt0 = jnp.exp(u_dt * (np.log(DT_MAX) - np.log(DT_MIN)) + np.log(DT_MIN))
    ssm_dt_bias = dt0 + jnp.log(-jnp.expm1(-dt0))
    ssm_a_log = jnp.log(jax.random.uniform(ks[7], (n_a, SSM_HEADS), f32, 1.0, 16.0))
    ssm_d = 1.0 + 0.1 * jax.random.normal(ks[8], (n_a, SSM_HEADS), f32)
    ssm_norm_g = 1.0 + 0.05 * jax.random.normal(ks[9], (n_a, D_INNER), f32)
    ssm_w_out = jax.random.normal(ks[10], (n_a, D_INNER, D_MODEL), f32) * D_INNER ** -0.5
    pool_w_in = jax.random.normal(ks[11], (n_b, D_MODEL, 2 * D_POOL), f32) * D_MODEL ** -0.5
    pool_w_group = jax.random.normal(ks[12], (n_b, POOL_GROUPS, POOL_GROUP_DIM, POOL_GROUP_DIM), f32) * POOL_GROUP_DIM ** -0.5
    pool_scale = 1.0 + 0.1 * jax.random.normal(ks[13], (n_b, D_POOL), f32)
    pool_w_out = jax.random.normal(ks[14], (n_b, D_POOL, D_MODEL), f32) * D_POOL ** -0.5
    return {"x": x, "ln_g": ln_g, "final_g": final_g,
            "ssm_w_in": ssm_w_in, "ssm_conv_w": ssm_conv_w, "ssm_conv_b": ssm_conv_b,
            "ssm_dt_bias": ssm_dt_bias, "ssm_a_log": ssm_a_log, "ssm_d": ssm_d,
            "ssm_norm_g": ssm_norm_g, "ssm_w_out": ssm_w_out,
            "pool_w_in": pool_w_in, "pool_w_group": pool_w_group,
            "pool_scale": pool_scale, "pool_w_out": pool_w_out}

def first_block(x, ln_g, final_g, ssm_w_in, ssm_conv_w, ssm_conv_b, ssm_dt_bias, ssm_a_log,
              ssm_d, ssm_norm_g, ssm_w_out, pool_w_in, pool_w_group, pool_scale, pool_w_out):
    for i in range(DEPTH):
        j = i // N_MIXERS
        hn = rmsnorm(x, ln_g[i])
        if i % N_MIXERS == 0:
            x = x + ssm_mixer(hn, ssm_w_in[j], ssm_conv_w[j], ssm_conv_b[j], ssm_dt_bias[j],
                              ssm_a_log[j], ssm_d[j], ssm_norm_g[j], ssm_w_out[j])
        else:
            x = x + pool_mixer(hn, pool_w_in[j], pool_w_group[j], pool_scale[j], pool_w_out[j])
    return rmsnorm(x, final_g)


D_MIX = D_MODEL
D_RNN = D_MIX // 2
RNN_BLOCKS = 16
RNN_BLOCK = D_RNN // RNN_BLOCKS
CONV_WIDTH = 4
LRU_C = 8.0
MLA_HEADS = 8
QK_NOPE = 128
QK_ROPE = 64
V_HEAD = 128
D_ATT = MLA_HEADS * V_HEAD
Q_LORA = 512
KV_LORA = 512
ROPE_THETA = 10000.0
Q_BLOCK = 128
IN_SPLITS = (D_RNN, D_RNN, Q_LORA, KV_LORA, QK_ROPE, D_ATT)
D_IN = D_RNN + D_RNN + Q_LORA + KV_LORA + QK_ROPE + D_ATT
ADA_SCALE = 0.5


def rms_norm(x, gain=None):
    xf = x.astype(jnp.float32)
    y = xf * lax.rsqrt(jnp.mean(xf * xf, axis=-1, keepdims=True) + EPS)
    if gain is not None:
        y = y * gain.astype(jnp.float32)
    return y.astype(x.dtype)

def apply_rope(x, cos, sin):
    half = x.shape[-1] // 2
    x1, x2 = x[..., :half], x[..., half:]
    return jnp.concatenate([x1 * cos - x2 * sin, x1 * sin + x2 * cos], axis=-1).astype(x.dtype)

def split_points(sizes):
    pts, acc = [], 0
    for s in sizes[:-1]:
        acc += s
        pts.append(acc)
    return pts

def _lin_rec_combine(e1, e2):
    a1, b1 = e1
    a2, b2 = e2
    return a1 * a2, a2 * b1 + b2

def rg_lru_branch(xr, conv_w, conv_b, w_rg_a, b_rg_a, w_rg_x, b_rg_x, lru_lambda):
    B, S, C = xr.shape
    xc = lax.conv_general_dilated(
        xr, conv_w[:, None, :].astype(xr.dtype), window_strides=(1,),
        padding=[(CONV_WIDTH - 1, 0)], dimension_numbers=('NWC', 'WIO', 'NWC'),
        feature_group_count=C) + conv_b
    xb = xc.reshape(B, S, RNN_BLOCKS, RNN_BLOCK)
    r = jax.nn.sigmoid(jnp.einsum('bshi,hij->bshj', xb, w_rg_a).reshape(B, S, C) + b_rg_a)
    i = jax.nn.sigmoid(jnp.einsum('bshi,hij->bshj', xb, w_rg_x).reshape(B, S, C) + b_rg_x)
    log_a = -LRU_C * r.astype(jnp.float32) * jax.nn.softplus(-lru_lambda.astype(jnp.float32))
    a = jnp.exp(log_a)
    b = jnp.sqrt(-jnp.expm1(2.0 * log_a)) * (i * xc).astype(jnp.float32)
    _, h = lax.associative_scan(_lin_rec_combine, (a, b), axis=1)
    return h.astype(xr.dtype)

def mla_branch(q_comp, kv_comp, k_rope_raw, positions, q_a_norm, w_uq, kv_a_norm, w_ukv,
               q_norm_nope, q_norm_rope, k_norm_nope, k_norm_rope):
    B, S, _ = q_comp.shape
    q = (rms_norm(q_comp, q_a_norm) @ w_uq).reshape(B, S, MLA_HEADS, QK_NOPE + QK_ROPE)
    kv = (rms_norm(kv_comp, kv_a_norm) @ w_ukv).reshape(B, S, MLA_HEADS, QK_NOPE + V_HEAD)
    q_nope, q_pe = q[..., :QK_NOPE], q[..., QK_NOPE:]
    k_nope, v = kv[..., :QK_NOPE], kv[..., QK_NOPE:]

    inv_freq = 1.0 / (ROPE_THETA ** (jnp.arange(0, QK_ROPE, 2, dtype=jnp.float32) / QK_ROPE))
    ang = positions.astype(jnp.float32)[..., None] * inv_freq
    cos, sin = jnp.cos(ang), jnp.sin(ang)

    q_nope = rms_norm(q_nope, q_norm_nope)
    q_pe = apply_rope(rms_norm(q_pe, q_norm_rope), cos[:, :, None], sin[:, :, None])
    k_nope = rms_norm(k_nope, k_norm_nope)
    k_pe = apply_rope(rms_norm(k_rope_raw, k_norm_rope), cos, sin)

    sm_scale = (QK_NOPE + QK_ROPE) ** -0.5
    n_blk = S // Q_BLOCK
    qn_b = q_nope.reshape(B, n_blk, Q_BLOCK, MLA_HEADS, QK_NOPE).transpose(1, 0, 2, 3, 4)
    qr_b = q_pe.reshape(B, n_blk, Q_BLOCK, MLA_HEADS, QK_ROPE).transpose(1, 0, 2, 3, 4)
    k_idx = jnp.arange(S)

    def attend_block(args):
        qn, qr, blk = args
        s = (jnp.einsum('bqhd,bkhd->bhqk', qn, k_nope)
             + jnp.einsum('bqhr,bkr->bhqk', qr, k_pe)).astype(jnp.float32) * sm_scale
        q_idx = blk * Q_BLOCK + jnp.arange(Q_BLOCK)
        s = jnp.where(q_idx[:, None] >= k_idx[None, :], s, -jnp.inf)
        p = jax.nn.softmax(s, axis=-1).astype(v.dtype)
        return jnp.einsum('bhqk,bkhd->bqhd', p, v)

    o = lax.map(attend_block, (qn_b, qr_b, jnp.arange(n_blk)))
    return o.transpose(1, 0, 2, 3, 4).reshape(B, S, D_ATT)

def second_inputs(seed: int = 0) -> dict:
    key = jax.random.key(seed)
    ks = jax.random.split(key, 24)
    f32 = jnp.float32
    nrm = lambda k, shape, s: jax.random.normal(k, shape, f32) * s
    gain = lambda k, n: 1.0 + 0.02 * jax.random.normal(k, (DEPTH, n), f32)

    x = jax.random.normal(ks[0], (BATCH, SEQ, D_MODEL), f32)
    c = jax.random.normal(ks[1], (BATCH, D_MODEL), f32)
    offsets = jax.random.randint(ks[2], (BATCH, 1), 0, 1024, dtype=jnp.int32)
    positions = offsets + jnp.arange(SEQ, dtype=jnp.int32)[None, :]

    u = jax.random.uniform(ks[3], (DEPTH, D_RNN), f32, 0.9, 0.999)
    sl = u ** (1.0 / LRU_C)
    lru_lambda = jnp.log(sl) - jnp.log1p(-sl)

    return {
        "x": x,
        "c": c,
        "positions": positions,
        "w_ada": nrm(ks[4], (DEPTH, D_MODEL, 3 * D_MODEL), ADA_SCALE * D_MODEL ** -0.5),
        "b_ada": nrm(ks[5], (DEPTH, 3 * D_MODEL), 0.01),
        "w_in": nrm(ks[6], (DEPTH, D_MODEL, D_IN), D_MODEL ** -0.5),
        "conv_w": nrm(ks[7], (DEPTH, CONV_WIDTH, D_RNN), CONV_WIDTH ** -0.5),
        "conv_b": nrm(ks[8], (DEPTH, D_RNN), 0.01),
        "w_rg_a": nrm(ks[9], (DEPTH, RNN_BLOCKS, RNN_BLOCK, RNN_BLOCK), RNN_BLOCK ** -0.5),
        "b_rg_a": nrm(ks[10], (DEPTH, D_RNN), 0.01),
        "w_rg_x": nrm(ks[11], (DEPTH, RNN_BLOCKS, RNN_BLOCK, RNN_BLOCK), RNN_BLOCK ** -0.5),
        "b_rg_x": nrm(ks[12], (DEPTH, D_RNN), 0.01),
        "lru_lambda": lru_lambda,
        "q_a_norm": gain(ks[13], Q_LORA),
        "w_uq": nrm(ks[14], (DEPTH, Q_LORA, MLA_HEADS * (QK_NOPE + QK_ROPE)), Q_LORA ** -0.5),
        "kv_a_norm": gain(ks[15], KV_LORA),
        "w_ukv": nrm(ks[16], (DEPTH, KV_LORA, MLA_HEADS * (QK_NOPE + V_HEAD)), KV_LORA ** -0.5),
        "q_norm_nope": gain(ks[17], QK_NOPE),
        "q_norm_rope": gain(ks[18], QK_ROPE),
        "k_norm_nope": gain(ks[19], QK_NOPE),
        "k_norm_rope": gain(ks[20], QK_ROPE),
        "w_out": nrm(ks[21], (DEPTH, D_MIX, D_MODEL), D_MIX ** -0.5),
    }

def second_block(x, c, positions, w_ada, b_ada, w_in, conv_w, conv_b, w_rg_a, b_rg_a, w_rg_x,
              b_rg_x, lru_lambda, q_a_norm, w_uq, kv_a_norm, w_ukv, q_norm_nope, q_norm_rope,
              k_norm_nope, k_norm_rope, w_out):
    c_act = jax.nn.silu(c)
    for l in range(DEPTH):
        mod = c_act @ w_ada[l] + b_ada[l]
        shift, scale, gate = jnp.split(mod, 3, axis=-1)
        h = rms_norm(x) * (1.0 + scale[:, None, :]) + shift[:, None, :]

        proj = h @ w_in[l]
        xr, gr, qc, kvc, kr, ga = jnp.split(proj, split_points(IN_SPLITS), axis=-1)

        y_rnn = rg_lru_branch(xr, conv_w[l], conv_b[l], w_rg_a[l], b_rg_a[l], w_rg_x[l],
                              b_rg_x[l], lru_lambda[l]) * jax.nn.silu(gr)
        y_att = mla_branch(qc, kvc, kr, positions, q_a_norm[l], w_uq[l], kv_a_norm[l], w_ukv[l],
                           q_norm_nope[l], q_norm_rope[l], k_norm_nope[l],
                           k_norm_rope[l]) * jax.nn.silu(ga)

        y = jnp.concatenate([y_rnn, y_att], axis=-1) @ w_out[l]
        x = x + gate[:, None, :] * y
    return x


def setup_inputs(seed=0):
    out = dict(first_inputs(seed))
    for name, value in second_inputs(seed + 1).items():
        if name != "x":
            out[name + "_2"] = value
    return out


def reference(
    x, ln_g, final_g, ssm_w_in, ssm_conv_w, ssm_conv_b, ssm_dt_bias, ssm_a_log, ssm_d,
    ssm_norm_g, ssm_w_out, pool_w_in, pool_w_group, pool_scale, pool_w_out, c_2, positions_2,
    w_ada_2, b_ada_2, w_in_2, conv_w_2, conv_b_2, w_rg_a_2, b_rg_a_2, w_rg_x_2, b_rg_x_2,
    lru_lambda_2, q_a_norm_2, w_uq_2, kv_a_norm_2, w_ukv_2, q_norm_nope_2, q_norm_rope_2,
    k_norm_nope_2, k_norm_rope_2, w_out_2,
):
    x = first_block(
        x, ln_g, final_g, ssm_w_in, ssm_conv_w, ssm_conv_b, ssm_dt_bias, ssm_a_log, ssm_d,
        ssm_norm_g, ssm_w_out, pool_w_in, pool_w_group, pool_scale, pool_w_out,
    )
    return second_block(
        x, c_2, positions_2, w_ada_2, b_ada_2, w_in_2, conv_w_2, conv_b_2, w_rg_a_2, b_rg_a_2,
        w_rg_x_2, b_rg_x_2, lru_lambda_2, q_a_norm_2, w_uq_2, kv_a_norm_2, w_ukv_2,
        q_norm_nope_2, q_norm_rope_2, k_norm_nope_2, k_norm_rope_2, w_out_2,
    )


_drawn_inputs = setup_inputs


def setup_inputs(seed=0):
    import zlib

    import numpy as np

    out = dict(_drawn_inputs(seed))
    spreads = {}
    factors = {'ssm_conv_b': 5.634,
     'b_ada_2': 5.668,
     'conv_b_2': 8.0,
     'b_rg_a_2': 200.0,
     'b_rg_x_2': 64.0,
     'q_a_norm_2': 8.0,
     'w_uq_2': 3.723,
     'kv_a_norm_2': 8.0,
     'q_norm_nope_2': 8.0,
     'q_norm_rope_2': 8.0,
     'k_norm_nope_2': 8.0,
     'k_norm_rope_2': 8.0,
     'w_rg_a_2': 2.772}
    for name, (base, spread) in spreads.items():
        noise = np.random.default_rng([zlib.crc32(name.encode()), seed]).standard_normal(out[name].shape)
        drawn = base * np.exp(spread * noise) if base else spread * noise
        out[name] = __import__('jax').numpy.asarray(drawn.astype(out[name].dtype))
    for name, factor in factors.items():
        out[name] = (out[name] * factor).astype(out[name].dtype)
    return out
```

```python
from contextlib import ExitStack

import numpy as np
import concourse.bass as bass
from concourse import mybir

F32 = mybir.dt.float32
F32R = mybir.dt.float32r
I32 = mybir.dt.int32
ALU = mybir.AluOpType
ACT = mybir.ActivationFunctionType
AX_X = mybir.AxisListType.X

P = 128
SEQ = 512
NT = SEQ // P
D = 2048
KB = D // P
EPS = 1e-6

D_INNER = 4096
GROUPS = 8
HPG = 8
HD = 64
HEADS = GROUPS * HPG
STATE = 128
TAPS = 4
CONV_DIM = D_INNER + 2 * GROUPS * STATE
CONV_BLOCKS = CONV_DIM // P
GB = D_INNER // GROUPS // P
Q = P
NQ = SEQ // Q

RING = 4
UKT = 4
UCOL = 256
UNIT = UKT * UCOL
UPP = KB // UKT
PANELS = 5
GU = PANELS * UPP
DT_UNITS = KB // UKT
ADA = 3 * D
ADA_COLS = ADA // GROUPS

ROW_CONV_W = (0, 48, 128, 176)
ROW_LN, ROW_QA, ROW_KVA = 96, 112, 116
ROW_NORM = 224
ROW_CONV_B = 256
ROW_SHIFT_B, ROW_SCALE_B = 304, 320
ROW_CONV2_W, ROW_CONV2_B, ROW_LRU = 336, 368, 376
ROW_RG_A, ROW_RG_X, ROW_C = 384, 392, 400


RNN_BLOCKS = 8
ATT_HEADS = 8
NOPE, ROPE, VH = 128, 64, 128
QH = NOPE + ROPE
PAIRS = ATT_HEADS // 2
LORA_KB = 4
COL_QKV, COL_KR, COL_GA = 2048, 3072, 3136
LRU_C = 8.0
SM_SCALE = float(QH) ** -0.5
SERIES_TO = 0.25
NEG = -1.0e30

TKT, TCOL = 2, 512
OUT1_UPP = D_INNER // P // TKT
OUT2_UPP = KB // TKT
OUT_PANELS = D // TCOL
U_OUT1 = DT_UNITS + GROUPS * GU
L_OUT1 = 1 + GROUPS * (GU // RING + 2)
U_RNN = U_OUT1 + OUT_PANELS * OUT1_UPP
RNN_PANELS, QKV_PANELS, GA_PANELS = 8, 4, 4
U_QKV = U_RNN + RNN_PANELS * UPP
U_GA = U_QKV + QKV_PANELS * UPP
U_KR = U_GA + GA_PANELS * UPP
U_PAIR = U_KR + DT_UNITS
U_OUT2 = U_PAIR + PAIRS * 4
U_END = U_OUT2 + OUT_PANELS * OUT2_UPP


def landed_before(unit):
    return L_OUT1 + (unit - U_OUT1) // RING


LRU_STEPS = 18
PAIR_STEPS = 35
ROUND = 1.5 * 2 ** 23
PI32 = 3.1415925
TURN = (6.28125, 2.0 ** -9 - 2.0 ** -16, 2 * np.pi - 6.28125 - 2.0 ** -9 + 2.0 ** -16)


class Steps:

    def __init__(self, eng, sem):
        self.eng, self.sem, self.n, self.base = eng, sem, 0, 0

    def done(self, instruction):
        instruction.then_inc(self.sem, 1)
        self.n += 1

    def wait(self, behind=0):
        self.eng.wait_ge(self.sem, self.base + (self.n - behind))

    def enter(self, g, per):
        self.base = (g - 1) * per
        self.first = self.n

    def leave(self, times, per):
        assert self.n - self.first == per, (self.n - self.first, per)
        self.n = self.first + times * per
        self.base = 0


def columns(ap, start, size):
    return ap[:, bass.ds(start, size)]


def build_program(nc, x, ln_g, final_g, ssm_w_in, ssm_conv_w, ssm_conv_b, ssm_dt_bias, ssm_a_log, ssm_d,
                  ssm_norm_g, ssm_w_out, c_2, positions_2, w_ada_2, b_ada_2, w_in_2, conv_w_2, conv_b_2,
                  w_rg_a_2, b_rg_a_2, w_rg_x_2, b_rg_x_2, lru_lambda_2, q_a_norm_2, w_uq_2, kv_a_norm_2,
                  w_ukv_2, q_norm_nope_2, q_norm_rope_2, k_norm_nope_2, k_norm_rope_2, w_out_2, inv_freq, out):
    ctx = ExitStack()
    with ctx:
        sem_names = {}

        def sem(name):
            assert name not in sem_names
            sem_names[name] = ctx.enter_context(nc.semaphore(name))
            return sem_names[name]

        def sb(name, shape, dt=F32, scope=ctx):
            return scope.enter_context(nc.sbuf_tensor(name, shape, dt))

        cs_rows = nc.dram_tensor("cs_rows", (HEADS, SEQ), F32).ap()
        y_rows = nc.dram_tensor("y_rows", (D_INNER, SEQ), F32).ap()
        x1_rows = nc.dram_tensor("x1_rows", (SEQ, D), F32).ap()
        x1n_rows = nc.dram_tensor("x1n_rows", (SEQ, D), F32).ap()
        ada_part = nc.dram_tensor("ada_part", (P, ADA), F32).ap()

        ps = ctx.enter_context(nc.psum_tensor("ps", [P, 8, 512], F32))

        w_raw = sb("w_raw", [P, RING, UNIT])
        w_hi = sb("w_hi", [P, RING, UNIT], F32R)
        w_lo = sb("w_lo", [P, RING, UNIT], F32R)
        ident = sb("ident", [P, P])
        ones = sb("ones", [P, P])
        cols = sb("cols", [P, 4 * P])
        ysq = sb("ysq", [P, SEQ])

        small = sb("small", [P, 64])
        yrs, x1ss, x1rs = small[:, 0:4], small[:, 4:8], small[:, 8:12]
        rsq, rskv, krs = small[:, 12:16], small[:, 16:20], small[:, 20:24]
        shc, scc = small[:, 24:40], small[:, 40:56]

        scope1 = ExitStack()
        hn_hi = sb("hn_hi", [P, KB, SEQ], F32R, scope1)
        hn_lo = sb("hn_lo", [P, KB, SEQ], F32R, scope1)
        tri = sb("tri", [P, P], F32, scope1)
        halves = sb("halves", [2, P], F32, scope1)
        d2 = sb("d_pairs", [2, HEADS // 2], F32, scope1)
        dcol = sb("dcol", [P, HEADS // 2], F32, scope1)
        convc = sb("convc", [P, TAPS + 1, CONV_BLOCKS], F32, scope1)
        prep = sb("prep", [P, 3 * NT, HEADS], F32, scope1)
        silu_c = sb("silu_c", [P, KB], F32, scope1)
        th_c = sb("th_c", [P, KB], F32, scope1)

        scope_x = ExitStack()
        xt = sb("xt", [P, NT, D], F32, scope_x)
        xjunk = sb("xjunk", [P, D], F32, scope_x)
        vrows = sb("vrows", [P, 4, P], F32, scope_x)
        xss = sb("xss", [P, NT], F32, scope_x)
        xrs = sb("xrs", [P, NT], F32, scope_x)
        bias_b = sb("bias_b", [P, HEADS], F32, scope_x)
        alog_b = sb("alog_b", [P, HEADS], F32, scope_x)
        dtv = [sb(f"dtv{i}", [P, NT, HEADS], F32, scope_x) for i in range(6)]
        cs_t = sb("cs_t", [HEADS, SEQ], F32, scope_x)
        scope_x.close()

        scope_g = ExitStack()
        ada_raw = sb("ada_raw", [P, 2, ADA_COLS], F32, scope_g)
        ada_acc = sb("ada_acc", [P, ADA_COLS], F32, scope_g)
        xraw = sb("xraw", [P, 6, 3 + SEQ], F32, scope_g)
        bct = sb("bct", [P, 2, SEQ], F32, scope_g)
        xst = sb("xst", [P, GB, SEQ], F32, scope_g)
        gz = sb("gz", [P, GB, SEQ], F32, scope_g)
        th = sb("th", [P, 2, 2, SEQ], F32, scope_g)
        csb = sb("csb", [P, 2, HPG, Q], F32, scope_g)
        seg = sb("seg", [P, HPG, Q], F32, scope_g)
        xdt = sb("xdt", [P, HPG, HD], F32, scope_g)
        xw = sb("xw", [P, HPG, HD], F32, scope_g)
        ytok = sb("ytok", [P, GB, P], F32, scope_g)
        state = sb("state", [P, HPG, HD], F32, scope_g)
        btok = sb("btok", [P, P], F32, scope_g)
        cbm = sb("cbm", [P, P], F32, scope_g)
        yt = sb("yt", [P, GB, SEQ], F32, scope_g)
        ytmp = sb("ytmp", [P, SEQ], F32, scope_g)
        gprep = sb("gprep", [P, 3 * NT, HPG], F32, scope_g)
        gconv = sb("gconv", [P, TAPS + 1, 6], F32, scope_g)
        gd = sb("gd", [P, GB], F32, scope_g)
        wa = sb("wa", [P, 2 * HPG], F32, scope_g)
        we = sb("we", [P, 2 * HPG], F32, scope_g)
        scope_g.close()
        scope1.close()

        gateb = sb("gateb", [P, D])
        rope_t = sb("rope_t", [P, 2, NT, ROPE // 2])
        lconst = sb("lconst", [P, 8, RNN_BLOCKS])

        scope_o = ExitStack()
        y_hi = sb("y_hi", [P, D_INNER // P, SEQ], F32R, scope_o)
        y_lo = sb("y_lo", [P, D_INNER // P, SEQ], F32R, scope_o)
        y_in = sb("y_in", [P, 2, 2, SEQ], F32, scope_o)
        x1p = sb("x1p", [P, NT, TCOL], F32, scope_o)
        scope_o.close()

        scope2 = ExitStack()
        xr = sb("xr", [P, RNN_BLOCKS, SEQ], F32, scope2)
        ga = sb("ga", [P, RNN_BLOCKS, SEQ], F32, scope2)
        qkvc = sb("qkvc", [P, 2 * LORA_KB, SEQ], F32, scope2)
        scope_f = ExitStack()
        gr = sb("gr", [P, RNN_BLOCKS, SEQ], F32, scope_f)
        h_hi = sb("h_hi", [P, KB, SEQ], F32R, scope_f)
        h_lo = sb("h_lo", [P, KB, SEQ], F32R, scope_f)
        lt = [sb(f"lt{i}", [P, SEQ], F32, scope_f) for i in range(6)]
        wblk = sb("wblk", [P, 2, P], F32, scope_f)
        lc = sb("lc", [P, 8], F32, scope_f)
        scope_f.close()
        scope_a = ExitStack()
        c_hi = sb("c_hi", [P, 2 * LORA_KB, SEQ], F32R, scope_a)
        c_lo = sb("c_lo", [P, 2 * LORA_KB, SEQ], F32R, scope_a)
        q_tok = sb("q_tok", [P, NT, 2, QH], F32, scope_a)
        kv_tok = sb("kv_tok", [P, NT, 2, NOPE + VH], F32, scope_a)
        sqt = sb("sqt", [P, NT, 2, QH], F32, scope_a)
        prob = sb("prob", [P, 2, SEQ], F32, scope_a)
        pt = sb("pt", [P, NT, SEQ], F32, scope_a)
        qt = sb("qt", [P, 2, SEQ], F32, scope_a)
        kt = sb("kt", [P, 2, SEQ], F32, scope_a)
        qpt = sb("qpt", [P, SEQ], F32, scope_a)
        kpt = sb("kpt", [P, SEQ], F32, scope_a)
        vt = sb("vt", [P, NT, 2, VH], F32, scope_a)
        qpe = sb("qpe", [P, NT, 2, ROPE], F32, scope_a)
        rt = [sb(f"rt{i}", [P, NT, 2, ROPE // 2], F32, scope_a) for i in range(4)]
        kr_tok = sb("kr_tok", [P, NT, ROPE], F32, scope_a)
        gain_b = sb("gain_b", [P, 2 * NOPE + 2 * ROPE], F32, scope_a)
        maskn = sb("maskn", [P, P], F32, scope_a)
        gth = sb("gth", [P, 2, SEQ], F32, scope_a)
        nrm = sb("nrm", [P, 3, NT, 2], F32, scope_a)
        sm = sb("sm", [P, 4, 8], F32, scope_a)
        scope_a.close()
        scope_z = ExitStack()
        y2_hi = sb("y2_hi", [P, KB, SEQ], F32R, scope_z)
        y2_lo = sb("y2_lo", [P, KB, SEQ], F32R, scope_z)
        xo = sb("xo", [P, NT, TCOL], F32, scope_z)
        oo = sb("oo", [P, NT, TCOL], F32, scope_z)
        scope_z.close()
        scope2.close()

        scope_e = ExitStack()
        x1t = sb("x1t", [P, NT, D], F32, scope_e)
        xh = sb("xh", [P, NT, D], F32, scope_e)
        scope_e.close()
        scope_e2 = ExitStack()
        sb("under_e2", [P, 2 * NT * D + 2 * KB * SEQ], F32, scope_e2)
        adab = sb("adab", [P, D], F32, scope_e2)
        fgb = sb("fgb", [P, D], F32, scope_e2)
        rt_i = sb("rt_i", [P, NT], I32, scope_e2)
        rt_f = sb("rt_f", [P, NT], F32, scope_e2)
        invf = sb("invf", [P, ROPE // 2], F32, scope_e2)
        ra = [ysq[:, i * P:(i + 1) * P].rearrange("p (t n) -> p t n", t=NT) for i in range(3)]
        le = [ysq[:, 3 * P + i * RNN_BLOCKS:3 * P + (i + 1) * RNN_BLOCKS] for i in range(4)]
        scope_e2.close()

        consts_made = sem("consts_made")
        rows_zeroed = sem("rows_zeroed")
        small_landed = sem("small_landed")
        x_landed = [sem(f"x_landed{t}") for t in range(NT)]
        xss_ready = sem("xss_ready")
        x_std_ready = sem("x_std_ready")
        x_normed = sem("x_normed")
        cols_turned = sem("cols_turned")
        cols_ready = sem("cols_ready")
        c_tanh_ready = sem("c_tanh_ready")
        x_turned = sem("x_turned")
        hn_hi_ready = sem("hn_hi_ready")
        hn_lo_ready = sem("hn_lo_ready")
        raw_landed = [sem(f"raw_landed{s}") for s in range(RING)]
        hi_ready = sem("hi_ready")
        lo_ready = sem("lo_ready")
        unit_used = sem("unit_used")
        dve_step = sem("dve_step")
        act_step = sem("act_step")
        pool_step = sem("pool_step")
        dt_abs_ready = sem("dt_abs_ready")
        dt_exp_ready = sem("dt_exp_ready")
        adt_ready = sem("adt_ready")
        cs_summed = sem("cs_summed")
        cs_ready = sem("cs_ready")
        cs_turned = sem("cs_turned")
        cs_t_ready = sem("cs_t_ready")
        cs_stored = sem("cs_stored")
        ecs_ready = sem("ecs_ready")
        pads_zeroed = sem("pads_zeroed")
        x_acc_freed = sem("x_acc_freed")
        z_acc_freed = sem("z_acc_freed")
        z_tanh_ready = sem("z_tanh_ready")
        conv_summed = sem("conv_summed")
        conv_tanh_ready = sem("conv_tanh_ready")
        conv_done = sem("conv_done")
        chunk_in = sem("chunk_in")
        csb_landed = [sem(f"csb_landed{s}") for s in range(2)]
        seg_ready = sem("seg_ready")
        decay_ready = sem("decay_ready")
        wa_ready = sem("wa_ready")
        we_ready = sem("we_ready")
        chunk_mid = sem("chunk_mid")
        chunk_summed = sem("chunk_summed")
        state_read = sem("state_read")
        ytok_ready = sem("ytok_ready")
        ytok_turned = sem("ytok_turned")
        yt_ready = sem("yt_ready")
        yt_free = sem("yt_free")
        y_stored = sem("y_stored")
        gated = sem("gated")
        ada_landed = [sem(f"ada_landed{s}") for s in range(2)]
        ada_used = sem("ada_used")
        ada_stored = sem("ada_stored")

        ysq_summed = sem("ysq_summed")
        ysq_mean_ready = sem("ysq_mean_ready")
        ysq_std_ready = sem("ysq_std_ready")
        yrs_ready = sem("yrs_ready")
        y_in_landed = [sem(f"y_in_landed{i}") for i in range(2)]
        y_hi_ready = sem("y_hi_ready")
        y_lo_ready = sem("y_lo_ready")
        x_in_landed = sem("x_in_landed")
        d_bank_done = sem("d_bank_done")
        d_bank_freed = sem("d_bank_freed")
        x1_free = sem("x1_free")
        x1t_landed = [sem(f"x1t_landed{t}") for t in range(NT)]
        adab_landed = sem("adab_landed")
        fgb_landed = sem("fgb_landed")
        gateb_landed = sem("gateb_landed")
        rope_in_landed = sem("rope_in_landed")
        ada_reduced = sem("ada_reduced")
        ada_cols_ready = sem("ada_cols_ready")
        x1_squared = sem("x1_squared")
        x1_mean_ready = sem("x1_mean_ready")
        x1_std_ready = sem("x1_std_ready")
        x1n_ready = sem("x1n_ready")
        x1n_stored = sem("x1n_stored")
        xh_ready = sem("xh_ready")
        h_turned = sem("h_turned")
        h_mod_ready = sem("h_mod_ready")
        h_hi_ready = sem("h_hi_ready")
        h_lo_ready = sem("h_lo_ready")
        lru_abs_ready = sem("lru_abs_ready")
        lru_exp_ready = sem("lru_exp_ready")
        angles_ready = sem("angles_ready")
        rope_ready = sem("rope_ready")
        f_bank_done = sem("f_bank_done")
        f_bank_freed = sem("f_bank_freed")
        wblk_zeroed = sem("wblk_zeroed")
        wblk_landed = sem("wblk_landed")
        xc_ready = sem("xc_ready")
        gates_summed = sem("gates_summed")
        gates_free = sem("gates_free")
        gates_ready = sem("gates_ready")
        logs_ready = sem("logs_ready")
        decays_ready = sem("decays_ready")
        var_ready = sem("var_ready")
        dev_ready = sem("dev_ready")
        rnn_done = sem("rnn_done")
        gains_landed = sem("gains_landed")
        mask_ready = sem("mask_ready")
        kr_ready = sem("kr_ready")
        kr_squared = sem("kr_squared")
        latent_squared = sem("latent_squared")
        latent_summed = sem("latent_summed")
        latent_var_ready = sem("latent_var_ready")
        latent_std_ready = sem("latent_std_ready")
        c_hi_ready = sem("c_hi_ready")
        c_lo_ready = sem("c_lo_ready")
        kpe_ready = sem("kpe_ready")
        kpe_turned = sem("kpe_turned")
        kpt_ready = sem("kpt_ready")
        q_read = sem("q_read")
        kv_read = sem("kv_read")
        sq_ready = sem("sq_ready")
        q_reduced = sem("q_reduced")
        nrm_ready = sem("nrm_ready")
        nrm_std_ready = sem("nrm_std_ready")
        tok_ready = sem("tok_ready")
        pair_turned = sem("pair_turned")
        qk_ready = sem("qk_ready")
        v_ready = sem("v_ready")
        scored = sem("scored")
        max_ready = sem("max_ready")
        exp_ready = sem("exp_ready")
        prob_ready = sem("prob_ready")
        prob_turned = sem("prob_turned")
        pt_ready = sem("pt_ready")
        head_summed = sem("head_summed")
        head_read = sem("head_read")
        ga_tanh_ready = sem("ga_tanh_ready")
        y2_hi_ready = sem("y2_hi_ready")
        y2_lo_ready = sem("y2_lo_ready")
        xo_landed = sem("xo_landed")
        xo_free = sem("xo_free")
        z_bank_done = sem("z_bank_done")
        z_bank_freed = sem("z_bank_freed")
        o_ready = sem("o_ready")
        out_stored = sem("out_stored")

        x_tok = x[0].rearrange("(t p) n -> p t n", p=P)
        x1_tok = x1_rows.rearrange("(t p) n -> p t n", p=P)
        x1n_tok = x1n_rows.rearrange("(t p) n -> p t n", p=P)
        out_tok = out[0].rearrange("(t p) n -> p t n", p=P)
        w_in_rows = ssm_w_in[0].rearrange("(k p) n -> p k n", p=P)
        w_ada_rows = w_ada_2[0].rearrange("(k p) n -> p k n", p=P)
        SMALL = 19

        def unit_ap(ring, slot, cols_=UCOL):
            return ring[:, slot, 0:UKT * cols_].rearrange("p (k n) -> p k n", k=UKT)

        block = ctx.enter_context(nc.Block())

        def walk(eng, body, steps=None, per=0):
            body(0, False, True)
            with eng.Fori(1, GROUPS) as g:
                if steps:
                    steps.enter(g, per)
                body(g, True, True)
            if steps:
                steps.leave(GROUPS - 1, per)
            body(GROUPS, True, False)

        @block.sync
        def _(sp):
            sp.wait_ge(rows_zeroed, 1)

            def rows(start, ap):
                t, r = divmod(start, P)
                n = ap.shape[0]
                sp.dma_start(vrows[r:r + n, t, :], ap).then_inc(small_landed, 16)

            for k in range(TAPS):
                rows(ROW_CONV_W[k], ssm_conv_w[0, k].rearrange("(b c) -> b c", c=P))
            rows(ROW_LN, ln_g[0].rearrange("(b c) -> b c", c=P))
            for t in range(NT):
                sp.dma_start(xt[:, t, :], x[0, t * P:(t + 1) * P, :]).then_inc(x_landed[t], 16)
            rows(ROW_QA, q_a_norm_2[0].rearrange("(b c) -> b c", c=P))
            rows(ROW_KVA, kv_a_norm_2[0].rearrange("(b c) -> b c", c=P))
            rows(ROW_NORM, ssm_norm_g[0].rearrange("(b c) -> b c", c=P))
            rows(ROW_CONV_B, ssm_conv_b[0].rearrange("(b c) -> b c", c=P))
            rows(ROW_SHIFT_B, b_ada_2[0, 0:2 * D].rearrange("(b c) -> b c", c=P))
            rows(ROW_CONV2_W, conv_w_2[0].rearrange("k (b c) -> (k b) c", c=P))
            rows(ROW_CONV2_B, conv_b_2[0].rearrange("(b c) -> b c", c=P))
            rows(ROW_LRU, lru_lambda_2[0].rearrange("(b c) -> b c", c=P))
            rows(ROW_RG_A, b_rg_a_2[0].rearrange("(b c) -> b c", c=P))
            rows(ROW_RG_X, b_rg_x_2[0].rearrange("(b c) -> b c", c=P))
            rows(ROW_C, c_2[0].rearrange("(b c) -> b c", c=P))
            sp.dma_start(bias_b[:], ssm_dt_bias[0].partition_broadcast(P)).then_inc(small_landed, 16)
            sp.dma_start(alog_b[:], ssm_a_log[0].partition_broadcast(P)).then_inc(small_landed, 16)
            sp.dma_start(d2[:], ssm_d[0].rearrange("(b h) -> h b", h=2),
                         allow_slow_non_contiguous=True).then_inc(small_landed, 16)

            for u in range(DT_UNITS):
                sp.dma_start(unit_ap(w_raw, u, HEADS), w_in_rows[:, u * UKT:(u + 1) * UKT,
                             D_INNER + CONV_DIM:]).then_inc(raw_landed[u], 16)
            sp.wait_ge(unit_used, DT_UNITS)
            sp.wait_ge(cs_stored, 16)

            def body(g, prev, cur):
                if not cur:
                    return
                for u in range(GU):
                    p, kq = divmod(u, UPP)
                    s = u % RING
                    loads = []
                    dst = unit_ap(w_raw, s)
                    src = w_in_rows[:, kq * UKT:(kq + 1) * UKT, :]
                    if p == 0:
                        loads = [(dst[:, :, h * P:(h + 1) * P], src,
                                  g * P + 2 * D_INNER + h * GROUPS * P, P) for h in range(2)]
                    elif p == 3:
                        loads = [(dst[:, k:k + 2, :], src[:, k:k + 2, :], g * GB * P, UCOL) for k in (2, 0)]
                    else:
                        at = (D_INNER if p < 3 else 0) + (p - 1) % 2 * UCOL
                        loads = [(dst, src, g * GB * P + at, UCOL)]
                    wait = sp.snap(g * GU + u + DT_UNITS - RING + 1) if prev else u + DT_UNITS - RING + 1
                    loads = [(to, rows_, sp.snap(at) if prev else at, n) for to, rows_, at, n in loads]
                    sp.wait_ge(lo_ready, wait)
                    for to, rows_, at, n in loads:
                        sp.dma_start(to, rows_[:, :, bass.ds(at, n)]).then_inc(raw_landed[s], 16)
                    if u < KB:
                        ada_at = sp.snap(g * ADA_COLS) if prev else 0
                        used = sp.snap(g * KB + u - 1) if prev else u - 1
                        if u >= 2 or prev:
                            sp.wait_ge(ada_used, used)
                        sp.dma_start(ada_raw[:, u % 2, :],
                                     w_ada_rows[:, u, bass.ds(ada_at, ADA_COLS)]
                                     ).then_inc(ada_landed[u % 2], 16)

            walk(sp, body)

            def load(unit, slot, view, src):
                sp.wait_ge(lo_ready, unit)
                sp.dma_start(view, src).then_inc(raw_landed[slot], 16)

            def tok_view(ring, slot, n=TCOL):
                return ring[:, slot, 0:TKT * n].rearrange("p (k n) -> p k n", k=TKT)

            w_rows = ssm_w_out[0].rearrange("(k p) n -> p k n", p=P)
            sp.wait_ge(yt_free, GROUPS + 1)
            sp.sem_inc(x1_free, 16)
            with sp.Fori(0, OUT_PANELS) as i:
                at = sp.snap(i * TCOL)
                for u in range(OUT1_UPP):
                    n = sp.snap(i * OUT1_UPP + (U_OUT1 + u - RING + 1))
                    load(n, u % RING, tok_view(w_raw, u % RING),
                         w_rows[:, u * TKT:(u + 1) * TKT, bass.ds(at, TCOL)])
                    if u == OUT1_UPP // 2:
                        n = sp.snap(i * 16 + 16)
                        sp.wait_ge(x1_free, n)
                        sp.dma_start(x1p[:], x_tok[:, :, bass.ds(at, TCOL)]).then_inc(x_in_landed, 16)

            w2_rows = w_in_2[0].rearrange("(k p) n -> p k n", p=P)

            def load_panel(i, unit, col):
                at = col if isinstance(col, int) else sp.snap(col)
                for u in range(UPP):
                    n = unit + u - RING + 1
                    load(n if isinstance(n, int) else sp.snap(n), u % RING, unit_ap(w_raw, u % RING),
                         w2_rows[:, u * UKT:(u + 1) * UKT, bass.ds(at, UCOL)])

            load_panel(0, U_RNN, 0)
            sp.wait_ge(unit_used, U_RNN)
            sp.wait_ge(x1_free, 16 * (OUT_PANELS + 1))
            sp.dma_start(gateb[:], b_ada_2[0, 2 * D:].partition_broadcast(P)).then_inc(gateb_landed, 16)
            sp.dma_start(adab[:], ada_part[:, 0:D]).then_inc(adab_landed, 16)
            for t in range(NT):
                sp.dma_start(x1t[:, t, :], x1_rows[t * P:(t + 1) * P, :]).then_inc(x1t_landed[t], 16)
            sp.dma_start(fgb[:], final_g.partition_broadcast(P)).then_inc(fgb_landed, 16)
            sp.dma_start(rt_i[:], positions_2[0].rearrange("(t p) -> p t", p=P),
                         allow_slow_non_contiguous=True).then_inc(rope_in_landed, 16)
            sp.dma_start(invf[:], inv_freq.partition_broadcast(P)).then_inc(rope_in_landed, 16)
            for k in (1, 2):
                sp.wait_ge(ada_reduced, k)
                sp.dma_start(adab[:], ada_part[:, k * D:(k + 1) * D]).then_inc(adab_landed, 16)
            for t in range(NT):
                sp.wait_ge(x1n_ready, t + 1)
                sp.dma_start(x1n_rows[t * P:(t + 1) * P, :], x1t[:, t, :]).then_inc(x1n_stored, 16)
            with sp.Fori(1, RNN_PANELS) as i:
                load_panel(i, i * UPP + U_RNN, i * UCOL)
            with sp.Fori(0, QKV_PANELS) as i:
                load_panel(i, i * UPP + U_QKV, i * UCOL + COL_QKV)
            with sp.Fori(0, GA_PANELS) as i:
                load_panel(i, i * UPP + U_GA, i * UCOL + COL_GA)
            for u in range(DT_UNITS):
                load(U_KR + u - RING + 1, u, unit_ap(w_raw, u, ROPE),
                     w2_rows[:, u * UKT:(u + 1) * UKT, COL_KR:COL_KR + ROPE])

            uq_rows = w_uq_2[0].rearrange("(k p) n -> p k n", p=P)
            ukv_rows = w_ukv_2[0].rearrange("(k p) n -> p k n", p=P)
            with sp.Fori(0, PAIRS) as i:
                for u in range(4):
                    cols_, rows_ = (2 * QH, uq_rows) if u < 2 else (TCOL, ukv_rows)
                    n = sp.snap(i * 4 + (U_PAIR + u - RING + 1))
                    at = sp.snap(i * cols_)
                    load(n, u, tok_view(w_raw, u, cols_),
                         rows_[:, u % 2 * TKT:(u % 2 + 1) * TKT, bass.ds(at, cols_)])

            w_rows = w_out_2[0].rearrange("(k p) n -> p k n", p=P)

            def out2_units(i, us):
                fixed = isinstance(i, int)
                at = i * TCOL if fixed else sp.snap(i * TCOL)
                for u in us:
                    n = i * OUT2_UPP + (U_OUT2 + u - RING + 1)
                    load(n if fixed else sp.snap(n), u % RING, tok_view(w_raw, u % RING),
                         w_rows[:, u * TKT:(u + 1) * TKT, bass.ds(at, TCOL)])

            def out2_rest(i):
                fixed = isinstance(i, int)
                at = i * TCOL if fixed else sp.snap(i * TCOL)
                n = i + 1 if fixed else sp.snap(i + 1)
                sp.wait_ge(xo_free, n)
                sp.dma_start(xo[:], x1n_tok[:, :, bass.ds(at, TCOL)]).then_inc(xo_landed, 16)
                out2_units(i, range(RING, OUT2_UPP))

            out2_units(0, range(RING))
            sp.wait_ge(unit_used, U_OUT2)
            sp.wait_ge(head_read, ATT_HEADS)
            sp.sem_inc(xo_free, 1)
            with sp.Fori(0, OUT_PANELS - 1) as i:
                out2_rest(i)
                out2_units(i + 1, range(RING))
            out2_rest(OUT_PANELS - 1)

        @block.gpsimd
        def _(pool):
            st = Steps(pool, pool_step)
            nc.gpsimd.memset(vrows[:], 0.0).then_inc(rows_zeroed, 1)
            st.done(nc.gpsimd.memset(ident[:], 0.0))
            st.done(nc.gpsimd.memset(ones[:], 1.0))
            st.wait()
            st.done(nc.gpsimd.affine_select(out=ident[:], in_=ident[:], compare_op=ALU.not_equal, fill=1.0,
                                            base=0, pattern=[[-1, P]], channel_multiplier=1))
            st.done(nc.gpsimd.affine_select(out=tri[:], in_=ones[:], compare_op=ALU.is_ge, fill=0.0,
                                            base=0, pattern=[[1, P]], channel_multiplier=-1))
            st.done(nc.gpsimd.affine_select(out=halves[:], in_=ones[0:2, :], compare_op=ALU.is_ge, fill=0.0,
                                            base=0, pattern=[[1, P]], channel_multiplier=-HD))
            st.wait()
            st.done(nc.gpsimd.affine_select(out=halves[:], in_=halves[:], compare_op=ALU.is_ge, fill=0.0,
                                            base=HD - 1, pattern=[[-1, P]], channel_multiplier=HD))
            st.wait()
            st.done(nc.gpsimd.memset(ysq[:], 0.0))
            st.wait()
            pool.sem_inc(consts_made, 1)

            pool.wait_ge(cs_t_ready, 1)
            pool.dma_start(cs_rows, cs_t[:]).then_inc(cs_stored, 16)
            pool.wait_ge(cs_stored, 16)
            nc.gpsimd.memset(xraw[:], 0.0).then_inc(pads_zeroed, 1)

            def load_cs(g, c):
                src = cs_rows[bass.ds(g * HPG, HPG), c * Q:(c + 1) * Q]
                pool.dma_start(csb[:, c % 2, :, :], src.partition_broadcast(P)).then_inc(csb_landed[c % 2], 16)

            load_cs(0, 0)
            load_cs(0, 1)
            pool.sem_inc(yt_free, 1)

            def body(g, prev, cur):
                gp = g - 1
                if prev:
                    for c in (2, 3):
                        pool.wait_ge(seg_ready, gp * NQ + c - 1)
                        load_cs(gp, c)
                    if cur:
                        for c in (0, 1):
                            pool.wait_ge(seg_ready, gp * NQ + c + 3)
                            load_cs(g, c)
                if cur:
                    pool.wait_ge(ada_used, g * KB + KB)
                    pool.dma_start(columns(ada_part, g * ADA_COLS, ADA_COLS), ada_acc[:]).then_inc(ada_stored, 16)
                if prev:
                    pool.wait_ge(yt_ready, gp * NQ + NQ)
                    pool.wait_ge(z_acc_freed, 2 * g)
                    nc.gpsimd.tensor_tensor(yt[:], yt[:], gz[:], ALU.mult).then_inc(gated, 1)
                    pool.wait_ge(gated, g)
                    pool.dma_start(y_rows[bass.ds(gp * GB * P, GB * P), :].rearrange("(b p) n -> p b n", p=P),
                                   yt[:]).then_inc(y_stored, 16)
                    for b in range(GB):
                        st.done(nc.gpsimd.tensor_tensor(ytmp[:], yt[:, b, :], yt[:, b, :], ALU.mult))
                        st.wait()
                        st.done(nc.gpsimd.tensor_tensor(ysq[:], ysq[:], ytmp[:], ALU.add))
                        st.wait()
                    pool.wait_ge(y_stored, g * 16)
                    pool.sem_inc(yt_free, 1)

            walk(pool, body, st, 2 * GB)
            pool.wait_ge(unit_used, U_OUT1)
            pool.wait_ge(ada_stored, 16 * GROUPS)
            for j in range(D_INNER // P // 2):
                if j >= 2:
                    pool.wait_ge(y_lo_ready, 2 * (j - 1))
                pool.dma_start(y_in[:, j % 2, :, :], y_rows[j * 2 * P:(j + 1) * 2 * P, :].rearrange(
                    "(b p) n -> p b n", p=P)).then_inc(y_in_landed[j % 2], 16)

            pool.wait_ge(h_lo_ready, KB)
            nc.gpsimd.memset(wblk[:], 0.0).then_inc(wblk_zeroed, 1)
            pool.wait_ge(wblk_zeroed, 1)
            pool.sem_inc(gates_free, 1)
            with pool.Fori(0, RNN_BLOCKS) as j:
                pool.wait_ge(gates_free, j + 1)
                for kind, w in enumerate((w_rg_a_2, w_rg_x_2)):
                    for h in range(2):
                        pool.dma_start(wblk[h * 64:(h + 1) * 64, kind, h * 64:(h + 1) * 64],
                                       w[0, bass.ds(j * 2 + h, 1), :, :].rearrange("o i j -> (o i) j")
                                       ).then_inc(wblk_landed, 16)

            pool.wait_ge(unit_used, U_PAIR)
            pool.wait_ge(rnn_done, RNN_BLOCKS)
            at = 0
            for gain in (q_norm_nope_2, k_norm_nope_2, q_norm_rope_2, k_norm_rope_2):
                n = gain.shape[1]
                pool.dma_start(gain_b[:, at:at + n], gain[0].partition_broadcast(P)).then_inc(gains_landed, 16)
                at += n
            st.done(nc.gpsimd.memset(maskn[:], 0.0))
            st.wait()
            nc.gpsimd.affine_select(out=maskn[:], in_=maskn[:], compare_op=ALU.is_ge, fill=NEG, base=0,
                                    pattern=[[-1, P]], channel_multiplier=1).then_inc(mask_ready, 1)

        @block.scalar
        def _(act):
            st = Steps(act, act_step)
            for t in range(NT):
                act.wait_ge(x_landed[t], 16)
                if t:
                    act.wait_ge(xss_ready, t)
                nc.scalar.activation(xjunk[:], xt[:, t, :], ACT.Square, accum_out=xss[:, t:t + 1]
                                     ).then_inc(xss_ready, 1)
            act.wait_ge(dve_step, 1)
            nc.scalar.activation(xrs[:], xrs[:], ACT.Sqrt).then_inc(x_std_ready, 1)
            act.wait_ge(cols_ready, 1)
            nc.scalar.activation(th_c[:], cols[:, ROW_C:ROW_C + KB], ACT.Tanh, scale=0.5
                                 ).then_inc(c_tanh_ready, 1)

            def hi(g, u):
                s = u % RING
                before = g * GU + u + DT_UNITS if g is not None else u
                if g is None:
                    act.wait_ge(raw_landed[s], 16)
                    n = UKT * HEADS
                else:
                    act.wait_ge(raw_landed[s], (g * 7 + 1 + 2 + u // RING + u // (3 * UPP)) * 16)
                    act.wait_ge(unit_used, before - RING + 1)
                    n = UNIT
                nc.scalar.activation(w_hi[:, s, 0:n], w_raw[:, s, 0:n], ACT.Copy).then_inc(hi_ready, 1)

            for u in range(DT_UNITS):
                hi(None, u)
            for kb in range(KB):
                act.wait_ge(x_turned, kb + 1)
                nc.scalar.activation(hn_hi[:, kb, :], ps[:, kb % 8, :], ACT.Copy,
                                     scale=cols[:, ROW_LN + kb:ROW_LN + kb + 1]).then_inc(hn_hi_ready, 1)
            act.wait_ge(dt_abs_ready, 1)
            nc.scalar.activation(dtv[1][:], dtv[1][:], ACT.Exp, scale=-1.0)
            nc.scalar.activation(alog_b[:], alog_b[:], ACT.Exp).then_inc(dt_exp_ready, 1)
            act.wait_ge(cs_ready, 1)
            nc.scalar.activation(prep[:, 2 * NT:3 * NT, :], prep[:, NT:2 * NT, :], ACT.Exp
                                 ).then_inc(ecs_ready, 1)
            act.wait_ge(pads_zeroed, 1)

            def take_raw(g, j):
                act.wait_ge(unit_used, g * GU + (j + 1) * UPP + DT_UNITS)
                if not isinstance(g, int) or g:
                    act.wait_ge(conv_summed, g * 3)
                b = 2 * (j % 2)
                nc.scalar.activation(xraw[:, 2 * j:2 * j + 2, 3:], ps[:, b:b + 2, :], ACT.Copy
                                     ).then_inc(x_acc_freed, 1)

            def conv_tanh(g, j):
                act.wait_ge(conv_summed, g * 3 + j + 1)
                if j == 0 and (not isinstance(g, int) or g):
                    act.wait_ge(z_acc_freed, g * 2)
                if j == 2:
                    act.wait_ge(conv_done, g * 3 + 1)
                src = bct[:, :, :] if j == 0 else xst[:, 2 * j - 2:2 * j, :]
                nc.scalar.activation(th[:, j % 2, :, :], src, ACT.Tanh).then_inc(conv_tanh_ready, 1)

            def z_tanh(g, j):
                act.wait_ge(unit_used, g * GU + (4 + j) * UPP + DT_UNITS)
                act.wait_ge(conv_done, g * 3 + 2 + j)
                b = 2 * (1 - j)
                nc.scalar.activation(th[:, 1 - j, :, :], ps[:, b:b + 2, :], ACT.Tanh, scale=0.5
                                     ).then_inc(z_tanh_ready, 1)

            def chunk_exps(gp, c):
                act.wait_ge(wa_ready, gp * NQ + c + 1)
                nc.scalar.activation(we[:], wa[:], ACT.Exp).then_inc(we_ready, 1)
                act.wait_ge(seg_ready, gp * NQ + c + 1)
                nc.scalar.activation(seg[:], seg[:], ACT.Exp).then_inc(decay_ready, 1)

            def body(g, prev, cur):
                gp = g - 1
                for u in range(GU):
                    if cur:
                        hi(g, u)
                    if prev and u == 2:
                        z_tanh(gp, 1)
                    if prev and u in (3, 6, 9, 12):
                        chunk_exps(gp, u // 3 - 1)
                    if cur and u in (5, 10, 14):
                        take_raw(g, {5: 0, 10: 1, 14: 2}[u])
                    if cur and u in (16, 17, 18):
                        conv_tanh(g, u - 16)
                    if cur and u == 19:
                        z_tanh(g, 0)

            walk(act, body)

            def split_hi(unit, slot, landed):
                act.wait_ge(raw_landed[slot], landed * 16)
                act.wait_ge(unit_used, unit - RING + 1)
                nc.scalar.activation(w_hi[:, slot, :], w_raw[:, slot, :], ACT.Copy).then_inc(hi_ready, 1)

            act.wait_ge(yt_free, GROUPS + 1)
            act.wait_ge(unit_used, U_OUT1)
            act.wait_ge(ysq_mean_ready, 1)
            nc.scalar.activation(yrs, yrs, ACT.Sqrt).then_inc(ysq_std_ready, 1)
            for u in range(RING):
                split_hi(U_OUT1 + u, u, landed_before(U_OUT1) + 1)
            for b in range(D_INNER // P):
                j = b // 2
                if b % 2 == 0:
                    act.wait_ge(y_in_landed[j % 2], 16 * (j // 2 + 1))
                nc.scalar.activation(y_hi[:, b, :], y_in[:, j % 2, b % 2, :], ACT.Copy,
                                     scale=cols[:, ROW_NORM + b:ROW_NORM + b + 1]).then_inc(y_hi_ready, 1)
            with act.Fori(0, OUT_PANELS) as i:
                for u in range(OUT1_UPP):
                    split_hi(i * OUT1_UPP + (U_OUT1 + RING + u), u % RING,
                             i * (OUT1_UPP // RING) + (landed_before(U_OUT1) + 2 + u // RING))
                act.wait_ge(d_bank_freed, i * NT + 2 * NT)
                act.dma_start(x1_tok[:, :, bass.ds(i * TCOL, TCOL)], x1p[:]).then_inc(x1_free, 16)

            for t in range(NT):
                act.wait_ge(x1t_landed[t], 16)
                nc.scalar.activation(xh[:, t, :], x1t[:, t, :], ACT.Square, accum_out=x1ss[:, t:t + 1]
                                     ).then_inc(x1_squared, 1)
            act.wait_ge(x1_mean_ready, 1)
            nc.scalar.activation(x1rs, x1rs, ACT.Sqrt).then_inc(x1_std_ready, 1)
            for t in range(NT):
                act.wait_ge(x1n_ready, t + 1)
                if t == 0:
                    act.wait_ge(x1_squared, NT)
                nc.scalar.activation(xh[:, t, :], x1t[:, t, :], ACT.Square, accum_out=x1ss[:, t:t + 1]
                                     ).then_inc(x1_squared, 1)
            act.wait_ge(x1_mean_ready, 2)
            nc.scalar.activation(x1rs, x1rs, ACT.Sqrt).then_inc(x1_std_ready, 1)
            for kb in range(KB):
                act.wait_ge(h_mod_ready, kb + 1)
                nc.scalar.activation(h_hi[:, kb, :], adab[:, kb % 4 * SEQ:(kb % 4 + 1) * SEQ], ACT.Copy
                                     ).then_inc(h_hi_ready, 1)
            act.wait_ge(lru_abs_ready, 1)
            nc.scalar.activation(le[1][:], le[1][:], ACT.Exp, scale=-1.0).then_inc(lru_exp_ready, 1)
            act.wait_ge(angles_ready, 1)
            for k in range(2):
                nc.scalar.activation(rope_t[:, k, :, :], ra[1 - k][:], ACT.Sin).then_inc(rope_ready, 1)

            act.wait_ge(x1n_stored, 16 * NT)
            act.wait_ge(xh_ready, NT)

            def panels(part, unit, count, dst, lru=None):
                fb = part * 8
                with act.Fori(0, count) as i:
                    for u in range(UPP):
                        if u == UPP - 1:
                            act.wait_ge(f_bank_done, i + (part * 4 + 1))
                            nc.scalar.activation(dst[:, bass.ds(i * 2, 1), :], ps[:, 0:1, :], ACT.Copy
                                                 ).then_inc(f_bank_freed, 1)
                            act.wait_ge(unit_used, i * UPP + (unit + UPP))
                            nc.scalar.activation(dst[:, bass.ds(i * 2 + 1, 1), :], ps[:, 1:2, :], ACT.Copy
                                                 ).then_inc(f_bank_freed, 1)
                        split_hi(i * UPP + (unit + RING + u), u, i + (landed_before(unit) + 2))
                        if lru is None:
                            continue
                        j = i + lru
                        if u == 1:
                            act.wait_ge(gates_summed, i + (lru + 1))
                            nc.scalar.activation(lt[1][:], ps[:, 4, :], ACT.Tanh, bias=lc[:, 5:6], scale=0.5)
                            nc.scalar.activation(lt[2][:], ps[:, 5, :], ACT.Tanh, bias=lc[:, 6:7], scale=0.5
                                                 ).then_inc(gates_free, 1)
                            nc.scalar.activation(lt[3][:], gr[:, bass.ds(j, 1), :].rearrange("p o n -> p (o n)"),
                                                 ACT.Tanh, scale=0.5).then_inc(gates_ready, 1)
                        if u == 2:
                            act.wait_ge(logs_ready, i + (lru + 1))
                            nc.scalar.activation(lt[0][:], lt[1][:], ACT.Exp)
                            nc.scalar.activation(lt[4][:], lt[4][:], ACT.Exp).then_inc(decays_ready, 1)
                            act.wait_ge(var_ready, i + (lru + 1))
                            nc.scalar.activation(lt[4][:], lt[4][:], ACT.Sqrt).then_inc(dev_ready, 1)

            panels(0, U_RNN, 4, xr)
            panels(1, U_RNN + 16, 4, gr)
            panels(2, U_QKV, 4, qkvc, 0)
            panels(3, U_GA, 4, ga, 4)

            for u in range(RING):
                split_hi(U_PAIR + u, u, landed_before(U_PAIR) + 1)
            act.wait_ge(rnn_done, RNN_BLOCKS)
            act.wait_ge(unit_used, U_PAIR)
            for part in range(2):
                if part:
                    act.wait_ge(latent_summed, 1)
                nc.scalar.activation(pt[:], qkvc[:, part * 4:part * 4 + 4, :], ACT.Square
                                     ).then_inc(latent_squared, 1)
            for b in range(2 * LORA_KB):
                at = ROW_QA + b
                nc.scalar.activation(c_hi[:, b, :], qkvc[:, b, :], ACT.Copy, scale=cols[:, at:at + 1]
                                     ).then_inc(c_hi_ready, 1)
            act.wait_ge(kr_ready, 1)
            nc.scalar.activation(sqt[:, :, 0, 0:ROPE], kr_tok[:], ACT.Square).then_inc(kr_squared, 1)
            act.wait_ge(latent_var_ready, 1)
            nc.scalar.activation(small[:, 12:24], small[:, 12:24], ACT.Sqrt).then_inc(latent_std_ready, 1)

            def pair(g, prev, cur):
                gp = g - 1
                for k in range(10):
                    if cur and k < 4:
                        split_hi(g * 4 + (U_PAIR + RING + k), k, g + (landed_before(U_PAIR) + 2))
                    if prev and k == 0:
                        nc.scalar.activation(gth[:], ga[:, bass.ds(gp * 2, 2), :], ACT.Tanh, scale=0.5
                                             ).then_inc(ga_tanh_ready, 1)
                    if prev and k < 8:
                        n = (k % 4 + 1) * P
                        act.wait_ge(max_ready, gp * 8 + k + 1)
                        if k >= 2:
                            act.wait_ge(prob_turned, gp * 8 + k - 1)
                        nc.scalar.activation(prob[:, k % 2, 0:n], ps[:, 4 + k % 2, 0:n], ACT.Exp,
                                             bias=sm[:, 1, k:k + 1], scale=SM_SCALE,
                                             accum_out=sm[:, 2, k:k + 1]).then_inc(exp_ready, 1)
                    if cur and k == 3:
                        act.wait_ge(q_read, g + 1)
                        nc.scalar.activation(sqt[:], q_tok[:], ACT.Square).then_inc(sq_ready, 1)
                    if cur and k == 6:
                        act.wait_ge(kv_read, g + 1)
                        act.wait_ge(q_reduced, g + 1)
                        nc.scalar.activation(sqt[:, :, :, 0:NOPE], kv_tok[:, :, :, 0:NOPE], ACT.Square
                                             ).then_inc(sq_ready, 1)
                    if cur and k == 7:
                        act.wait_ge(nrm_ready, g + 1)
                        nc.scalar.activation(nrm[:], nrm[:], ACT.Sqrt).then_inc(nrm_std_ready, 1)
                if cur:
                    act.wait_ge(pair_turned, g + 1)
                    nc.scalar.activation(vt[:], kv_tok[:, :, :, NOPE:], ACT.Copy).then_inc(v_ready, 1)

            pair(0, False, True)
            with act.Fori(1, PAIRS) as g:
                pair(g, True, True)
            pair(PAIRS, True, False)

            act.wait_ge(head_read, ATT_HEADS)
            act.wait_ge(unit_used, U_OUT2)
            for b in range(KB):
                src = xr[:, b, :] if b < 8 else ga[:, b - 8, :]
                nc.scalar.activation(y2_hi[:, b, :], src, ACT.Copy).then_inc(y2_hi_ready, 1)

            def out2_panel(i, last):
                for u in range(OUT2_UPP):
                    if not last or u < OUT2_UPP - RING:
                        split_hi(i * OUT2_UPP + (U_OUT2 + RING + u), u % RING,
                                 i * (OUT2_UPP // RING) + (landed_before(U_OUT2) + 2 + u // RING))
                act.wait_ge(o_ready, i + 1)
                act.dma_start(out_tok[:, :, bass.ds(i * TCOL, TCOL)], oo[:]).then_inc(out_stored, 16)

            with act.Fori(0, OUT_PANELS - 1) as i:
                out2_panel(i, False)
            out2_panel(OUT_PANELS - 1, True)
            act.wait_ge(out_stored, 16 * (OUT_PANELS + 1))

        @block.vector
        def _(dve):
            st = Steps(dve, dve_step)
            dve.wait_ge(xss_ready, NT)
            st.done(nc.vector.tensor_scalar(xrs[:], xss[:], 1.0 / D, EPS, ALU.mult, ALU.add))
            dve.wait_ge(x_std_ready, 1)
            st.done(nc.vector.reciprocal(xrs[:], xrs[:]))
            st.wait()
            for t in range(NT):
                nc.vector.tensor_scalar(xt[:, t, :], xt[:, t, :], xrs[:, t:t + 1], None, ALU.mult
                                        ).then_inc(x_normed, 1)
            dve.wait_ge(cols_turned, 1)
            nc.vector.tensor_copy(cols[:], ps[:, 7, :]).then_inc(cols_ready, 1)
            dve.wait_ge(cols_turned, 2)
            st.done(nc.vector.tensor_copy(dcol[:], ps[:, 6, 0:HEADS // 2]))
            dve.wait_ge(cols_ready, 1)
            for k in range(TAPS + 1):
                at = ROW_CONV_W[k] if k < TAPS else ROW_CONV_B
                st.done(nc.vector.tensor_scalar(convc[:, k, :], cols[:, at:at + CONV_BLOCKS], 0.5, None, ALU.mult))
            dve.wait_ge(c_tanh_ready, 1)
            st.done(nc.vector.scalar_tensor_tensor(silu_c[:], th_c[:], 1.0, cols[:, ROW_C:ROW_C + KB],
                                                   ALU.add, ALU.mult))
            st.wait()
            st.done(nc.vector.tensor_scalar(silu_c[:], silu_c[:], 0.5, None, ALU.mult))
            for kb in range(KB):
                dve.wait_ge(hn_hi_ready, kb + 1)
                nc.vector.scalar_tensor_tensor(hn_lo[:, kb, :], ps[:, kb % 8, :],
                                               cols[:, ROW_LN + kb:ROW_LN + kb + 1],
                                               hn_hi[:, kb, :].bitcast(F32), ALU.mult, ALU.subtract
                                               ).then_inc(hn_lo_ready, 1)

            def lo(g, u):
                s = u % RING
                n = UKT * HEADS if g is None else UNIT
                dve.wait_ge(hi_ready, u + 1 if g is None else g * GU + u + DT_UNITS + 1)
                nc.vector.tensor_tensor(w_lo[:, s, 0:n], w_raw[:, s, 0:n], w_hi[:, s, 0:n].bitcast(F32),
                                        ALU.subtract).then_inc(lo_ready, 1)

            for u in range(DT_UNITS):
                lo(None, u)

            v, e, s1, s2, pl, adt = dtv
            dve.wait_ge(unit_used, DT_UNITS)
            for t in range(NT):
                st.done(nc.vector.tensor_tensor(v[:, t, :], ps[:, t, 0:HEADS], bias_b[:], ALU.add))
            st.wait()
            st.done(nc.vector.tensor_scalar(e[:], v[:], -1.0, None, ALU.mult))
            st.wait()
            nc.vector.tensor_tensor(e[:], e[:], v[:], ALU.max).then_inc(dt_abs_ready, 1)
            dve.wait_ge(dt_exp_ready, 1)
            st.done(nc.vector.tensor_scalar(s1[:], e[:], 2.0, None, ALU.add))
            st.wait()
            st.done(nc.vector.reciprocal(s1[:], s1[:]))
            st.wait()
            st.done(nc.vector.tensor_tensor(s1[:], s1[:], e[:], ALU.mult))
            st.wait()
            st.done(nc.vector.tensor_tensor(s2[:], s1[:], s1[:], ALU.mult))
            st.wait()
            st.done(nc.vector.tensor_scalar(pl[:], s2[:], 1.0 / 15, None, ALU.mult))
            for n in (13, 11, 9, 7, 5, 3):
                st.wait()
                st.done(nc.vector.scalar_tensor_tensor(pl[:], pl[:], 1.0 / n, s2[:], ALU.add, ALU.mult))
            st.wait()
            st.done(nc.vector.scalar_tensor_tensor(pl[:], pl[:], 1.0, s1[:], ALU.add, ALU.mult))
            st.done(nc.vector.tensor_scalar(v[:], v[:], 0.0, None, ALU.max))
            st.wait()
            st.done(nc.vector.scalar_tensor_tensor(prep[:, 0:NT, :], pl[:], 2.0, v[:], ALU.mult, ALU.add))
            st.wait()
            for t in range(NT):
                last = nc.vector.scalar_tensor_tensor(adt[:, t, :], alog_b[:], -1.0, prep[:, t, :],
                                                      ALU.mult, ALU.mult)
                last.then_inc(adt_ready, 1)
            dve.wait_ge(cs_summed, 1)
            nc.vector.tensor_copy(prep[:, NT:2 * NT, :], ps[:, 4, 0:NT * HEADS].rearrange(
                "p (t h) -> p t h", t=NT)).then_inc(cs_ready, 1)
            dve.wait_ge(cs_turned, 1)
            nc.vector.tensor_copy(cs_t[:], ps[0:HEADS, 5, :]).then_inc(cs_t_ready, 1)
            dve.wait_ge(ecs_ready, 1)

            def group_constants(gp):
                st.done(nc.vector.tensor_copy(gprep[:], prep[:, :, bass.ds(gp * HPG, HPG)]))
                st.done(nc.vector.tensor_copy(gd[:], dcol[:, bass.ds(gp * GB, GB)]))

            def conv_constants(g):
                st.done(nc.vector.tensor_copy(gconv[:, :, 0:2], convc[:, :, D_INNER // P:].rearrange(
                    "p k (j g) -> p k j g", g=GROUPS)[:, :, :, bass.ds(g, 1)].rearrange("p k j g -> p k (j g)")))
                st.done(nc.vector.tensor_copy(gconv[:, :, 2:6], convc[:, :, bass.ds(g * GB, GB)]))

            def ada_rows(g, k):
                dve.wait_ge(ada_landed[k % 2], (g * (KB // 2) + k // 2 + 1) * 16)
                if k == 0:
                    if not isinstance(g, int) or g:
                        dve.wait_ge(ada_stored, g * 16)
                    nc.vector.tensor_scalar(ada_acc[:], ada_raw[:, 0, :], silu_c[:, 0:1], None, ALU.mult
                                            ).then_inc(ada_used, 1)
                    return
                dve.wait_ge(ada_used, g * KB + k)
                ins = nc.vector.scalar_tensor_tensor(ada_acc[:], ada_raw[:, k % 2, :], silu_c[:, k:k + 1],
                                                     ada_acc[:], ALU.mult, ALU.add)
                ins.then_inc(ada_used, 1)

            def conv(g, j):
                dve.wait_ge(x_acc_freed, g * 3 + j + 1)
                dst = [bct[:, b, :] if j == 0 else xst[:, 2 * j - 2 + b, :] for b in range(2)]
                for b in range(2):
                    st.done(nc.vector.tensor_scalar(dst[b], xraw[:, 2 * j + b, 3:3 + SEQ],
                                                    gconv[:, 3, 2 * j + b:2 * j + b + 1],
                                                    gconv[:, 4, 2 * j + b:2 * j + b + 1], ALU.mult, ALU.add))
                for k in (2, 1, 0):
                    for b in range(2):
                        st.wait(1)
                        tap = nc.vector.scalar_tensor_tensor(
                            dst[b], xraw[:, 2 * j + b, k:k + SEQ], gconv[:, k, 2 * j + b:2 * j + b + 1],
                            dst[b], ALU.mult, ALU.add)
                        if (k, b) == (0, 1):
                            tap.then_inc(conv_summed, 1)
                        else:
                            st.done(tap)

            def conv_silu(g, j):
                dve.wait_ge(conv_tanh_ready, g * 3 + j + 1)
                dst = bct[:, :, :] if j == 0 else xst[:, 2 * j - 2:2 * j, :]
                nc.vector.scalar_tensor_tensor(dst, th[:, j % 2, :, :], 1.0, dst, ALU.add, ALU.mult
                                               ).then_inc(conv_done, 1)

            def z_silu(g, j):
                dve.wait_ge(z_tanh_ready, g * 2 + j + 1)
                if j == 0 and (not isinstance(g, int) or g):
                    dve.wait_ge(gated, g)
                b = 2 * (1 - j)
                nc.vector.scalar_tensor_tensor(gz[:, 2 * j:2 * j + 2, :], th[:, 1 - j, :, :], 1.0,
                                               ps[:, b:b + 2, :], ALU.add, ALU.mult).then_inc(z_acc_freed, 1)

            def chunk_prepare(gp, c):
                n = gp * NQ + c + 1
                s = c % 2
                cs = gprep[:, NT + c, :]
                dve.wait_ge(csb_landed[s], (gp * 2 + c // 2 + 1) * 16)
                st.done(nc.vector.tensor_tensor(wa[:, 0:HPG], csb[:, s, :, Q - 1], cs, ALU.subtract))
                nc.vector.tensor_copy(wa[:, HPG:], csb[:, s, :, Q - 1]).then_inc(wa_ready, 1)
                for r in range(HPG):
                    ins = nc.vector.tensor_scalar(seg[:, r, :], csb[:, s, r, :], cs[:, r:r + 1], 0.0,
                                                  ALU.subtract, ALU.min)
                ins.then_inc(seg_ready, 1)
                dve.wait_ge(chunk_in, n)
                nc.vector.tensor_copy(btok[:], ps[:, 5, 0:P])
                st.done(nc.vector.tensor_tensor(cbm[:], ps[:, 5, P:2 * P], tri[:], ALU.mult))
                st.done(nc.vector.tensor_tensor(
                    xdt[:], ps[:, 4, :].rearrange("p (r d) -> p r d", r=HPG),
                    gprep[:, c, :].unsqueeze(2).broadcast_to([P, HPG, HD]), ALU.mult))
                st.wait()
                dve.wait_ge(we_ready, n)
                st.done(nc.vector.tensor_tensor(xw[:], xdt[:], we[:, 0:HPG].unsqueeze(2).broadcast_to([P, HPG, HD]),
                                                ALU.mult))
                dve.wait_ge(decay_ready, n)
                nc.vector.tensor_tensor(seg[:], seg[:], cbm[:].unsqueeze(1).broadcast_to([P, HPG, Q]), ALU.mult
                                        ).then_inc(chunk_mid, 1)

            def chunk_collect(gp, c):
                dve.wait_ge(chunk_summed, gp * NQ + c + 1)
                new = ps[:, 4, :].rearrange("p (r d) -> p r d", r=HPG)
                if c == 0:
                    nc.vector.tensor_copy(state[:], new).then_inc(state_read, 1)
                elif c < NQ - 1:
                    st.done(nc.vector.tensor_tensor(
                        state[:], state[:], we[:, HPG:].unsqueeze(2).broadcast_to([P, HPG, HD]), ALU.mult))
                    st.wait()
                    nc.vector.tensor_tensor(state[:], state[:], new, ALU.add).then_inc(state_read, 1)
                y = ytok[:].rearrange("p b (r d) -> p (b r) d", d=HD)
                diag = ps[:, 6, :].rearrange("p (r d) -> p r d", r=HPG)
                if c == 0:
                    nc.vector.tensor_copy(y, diag).then_inc(ytok_ready, 1)
                else:
                    st.done(nc.vector.tensor_tensor(
                        y, ps[:, 7, :].rearrange("p (r d) -> p r d", r=HPG),
                        gprep[:, 2 * NT + c, :].unsqueeze(2).broadcast_to([P, HPG, HD]), ALU.mult))
                    st.wait()
                    nc.vector.tensor_tensor(y, y, diag, ALU.add).then_inc(ytok_ready, 1)

            def chunk_skip(gp, c):
                dve.wait_ge(ytok_turned, gp * NQ + c + 1)
                if c == 0:
                    dve.wait_ge(yt_free, gp + 1)
                for b in range(GB):
                    ins = nc.vector.scalar_tensor_tensor(
                        yt[:, b, c * Q:(c + 1) * Q], xst[:, b, c * Q:(c + 1) * Q], gd[:, b:b + 1],
                        ps[:, 7, b * P:(b + 1) * P], ALU.mult, ALU.add)
                ins.then_inc(yt_ready, 1)

            def body(g, prev, cur):
                gp = g - 1
                if prev:
                    group_constants(gp)
                    st.wait()
                for u in range(GU):
                    if cur:
                        lo(g, u)
                    if prev and u == 2:
                        z_silu(gp, 1)
                    if cur and u < KB:
                        ada_rows(g, u)
                    if prev and u in (6, 9, 12, 15):
                        chunk_skip(gp, u // 3 - 2)
                    if prev and u in (3, 6, 9, 12):
                        chunk_prepare(gp, u // 3 - 1)
                    if prev and u in (5, 8, 11, 14):
                        chunk_collect(gp, (u - 5) // 3)
                    if cur and u == 15:
                        conv_constants(g)
                        st.wait()
                        conv(g, 0)
                    if cur and u == 16:
                        conv(g, 1)
                    if cur and u == 17:
                        conv_silu(g, 0)
                        conv(g, 2)
                    if cur and u == 18:
                        conv_silu(g, 1)
                    if cur and u == 19:
                        conv_silu(g, 2)
                        z_silu(g, 0)

            walk(dve, body, st, 46)

            def split_lo(unit, slot):
                dve.wait_ge(hi_ready, unit + 1)
                nc.vector.tensor_tensor(w_lo[:, slot, :], w_raw[:, slot, :], w_hi[:, slot, :].bitcast(F32),
                                        ALU.subtract).then_inc(lo_ready, 1)

            def mean_eps(out_, in_, n, eps=EPS):
                return nc.vector.tensor_scalar(out_, in_, 1.0 / n, eps, ALU.mult, ALU.add)

            dve.wait_ge(ysq_summed, 1)
            mean_eps(yrs, ps[:, 4, 0:NT], D_INNER, 4 * EPS).then_inc(ysq_mean_ready, 1)
            dve.wait_ge(ysq_std_ready, 1)
            nc.vector.reciprocal(yrs, yrs).then_inc(yrs_ready, 1)
            dve.wait_ge(yrs_ready, 1)
            dve.sem_inc(d_bank_freed, NT)
            for u in range(RING):
                split_lo(U_OUT1 + u, u)
            for b in range(D_INNER // P):
                dve.wait_ge(y_hi_ready, b + 1)
                nc.vector.scalar_tensor_tensor(y_lo[:, b, :], y_in[:, b // 2 % 2, b % 2, :],
                                               cols[:, ROW_NORM + b:ROW_NORM + b + 1],
                                               y_hi[:, b, :].bitcast(F32), ALU.mult, ALU.subtract
                                               ).then_inc(y_lo_ready, 1)
            with dve.Fori(0, OUT_PANELS) as i:
                for u in range(OUT1_UPP):
                    if u == OUT1_UPP - 1:
                        dve.wait_ge(x_in_landed, i * 16 + 16)
                        for t in range(NT):
                            if t < NT - 1:
                                dve.wait_ge(d_bank_done, i * (NT - 1) + t + 1)
                            else:
                                dve.wait_ge(unit_used, i * OUT1_UPP + (U_OUT1 + OUT1_UPP))
                            nc.vector.scalar_tensor_tensor(x1p[:, t, :], ps[:, t, :], yrs[:, t:t + 1], x1p[:, t, :],
                                                           ALU.mult, ALU.add).then_inc(d_bank_freed, 1)
                    split_lo(i * OUT1_UPP + (U_OUT1 + RING + u), u % RING)

            def rstd(n):
                dve.wait_ge(x1_squared, NT * n)
                mean_eps(x1rs, x1ss, D).then_inc(x1_mean_ready, 1)
                dve.wait_ge(x1_std_ready, n)
                st.done(nc.vector.reciprocal(x1rs, x1rs))
                st.wait()

            rstd(1)
            dve.wait_ge(fgb_landed, 16)
            for t in range(NT):
                nc.vector.scalar_tensor_tensor(x1t[:, t, :], x1t[:, t, :], x1rs[:, t:t + 1], fgb[:], ALU.mult, ALU.mult
                                               ).then_inc(x1n_ready, 1)
            dve.wait_ge(ada_reduced, 2)
            st.done(nc.vector.tensor_tensor(shc, ps[:, 4, 0:KB], cols[:, ROW_SHIFT_B:ROW_SHIFT_B + KB], ALU.add))
            st.done(nc.vector.scalar_tensor_tensor(scc, ps[:, 5, 0:KB], 1.0, cols[:, ROW_SCALE_B:ROW_SCALE_B + KB],
                                                   ALU.add, ALU.add))
            dve.wait_ge(ada_reduced, 3)
            dve.wait_ge(gateb_landed, 16)
            for j in range(D // 512):
                at = slice(j * 512, (j + 1) * 512)
                ins = nc.vector.tensor_tensor(gateb[:, at], gateb[:, at], ps[:, j, :], ALU.add)
            ins.then_inc(ada_cols_ready, 1)
            rstd(2)
            for t in range(NT):
                nc.vector.tensor_scalar(xh[:, t, :], x1t[:, t, :], x1rs[:, t:t + 1], None, ALU.mult
                                        ).then_inc(xh_ready, 1)
            for kb in range(KB + 1):
                if kb < KB:
                    dve.wait_ge(h_turned, kb + 1)
                    at = slice(kb % 4 * SEQ, (kb % 4 + 1) * SEQ)
                    nc.vector.tensor_scalar(adab[:, at], ps[:, 4 + kb % 4, :], scc[:, kb:kb + 1], shc[:, kb:kb + 1],
                                            ALU.mult, ALU.add).then_inc(h_mod_ready, 1)
                if kb:
                    dve.wait_ge(h_hi_ready, kb)
                    at = slice((kb - 1) % 4 * SEQ, ((kb - 1) % 4 + 1) * SEQ)
                    nc.vector.tensor_tensor(h_lo[:, kb - 1, :], adab[:, at], h_hi[:, kb - 1, :].bitcast(F32),
                                            ALU.subtract).then_inc(h_lo_ready, 1)
            dve.sem_inc(f_bank_freed, 2)

            for k in range(TAPS):
                st.done(nc.vector.tensor_copy(lconst[:, k, :], cols[:, ROW_CONV2_W + 8 * k:ROW_CONV2_W + 8 * k + 8]))
            st.done(nc.vector.tensor_copy(lconst[:, 4, :], cols[:, ROW_CONV2_B:ROW_CONV2_B + 8]))
            for k, at in ((5, ROW_RG_A), (6, ROW_RG_X)):
                st.done(nc.vector.tensor_scalar(lconst[:, k, :], cols[:, at:at + 8], 0.5, None, ALU.mult))
            lam = cols[:, ROW_LRU:ROW_LRU + 8]
            v, e, s1, s2 = le
            st.done(nc.vector.tensor_scalar(v[:], lam, -1.0, None, ALU.mult))
            st.wait()
            nc.vector.tensor_tensor(e[:], v[:], lam, ALU.max).then_inc(lru_abs_ready, 1)
            dve.wait_ge(lru_exp_ready, 1)
            st.done(nc.vector.tensor_scalar(s1[:], e[:], 2.0, None, ALU.add))
            st.wait()
            st.done(nc.vector.reciprocal(s1[:], s1[:]))
            st.wait()
            st.done(nc.vector.tensor_tensor(s1[:], s1[:], e[:], ALU.mult))
            st.wait()
            st.done(nc.vector.tensor_tensor(s2[:], s1[:], s1[:], ALU.mult))
            st.wait()
            st.done(nc.vector.tensor_scalar(e[:], s2[:], 1.0 / 15, None, ALU.mult))
            for n in (13, 11, 9, 7, 5, 3):
                st.wait()
                st.done(nc.vector.scalar_tensor_tensor(e[:], e[:], 1.0 / n, s2[:], ALU.add, ALU.mult))
            st.wait()
            st.done(nc.vector.scalar_tensor_tensor(e[:], e[:], 1.0, s1[:], ALU.add, ALU.mult))
            st.done(nc.vector.tensor_scalar(v[:], v[:], 0.0, None, ALU.max))
            st.wait()
            st.done(nc.vector.scalar_tensor_tensor(v[:], e[:], 2.0, v[:], ALU.mult, ALU.add))
            st.wait()
            st.done(nc.vector.tensor_scalar(lconst[:, 7, :], v[:], -LRU_C / 2, None, ALU.mult))

            dve.wait_ge(rope_in_landed, 32)
            st.done(nc.vector.tensor_copy(rt_f[:], rt_i[:]))
            st.wait()
            for t in range(NT):
                st.done(nc.vector.tensor_scalar(ra[0][:, t, :], invf[:], rt_f[:, t:t + 1], None, ALU.mult))
            st.wait()
            st.done(nc.vector.tensor_scalar(ra[1][:], ra[0][:], 1.0 / (2 * np.pi), ROUND, ALU.mult, ALU.add))
            st.wait()
            st.done(nc.vector.tensor_scalar(ra[1][:], ra[1][:], -ROUND, None, ALU.add))
            for part in TURN:
                st.wait()
                st.done(nc.vector.scalar_tensor_tensor(ra[0][:], ra[1][:], -part, ra[0][:], ALU.mult, ALU.add))
            st.wait()
            st.done(nc.vector.tensor_scalar(ra[1][:], ra[0][:], float(np.pi / 2), None, ALU.add))
            st.wait()
            st.done(nc.vector.tensor_scalar(ra[2][:], ra[1][:], PI32, -2 * np.pi, ALU.is_gt, ALU.mult))
            st.wait()
            st.done(nc.vector.tensor_tensor(ra[1][:], ra[1][:], ra[2][:], ALU.add))
            st.done(nc.vector.tensor_scalar(ra[0][:], ra[0][:], -PI32, PI32, ALU.max, ALU.min))
            st.wait()
            nc.vector.tensor_scalar(ra[1][:], ra[1][:], -PI32, PI32, ALU.max, ALU.min).then_inc(angles_ready, 1)
            dve.wait_ge(rope_ready, 2)

            def panels(unit, count, lru=None):
                with dve.Fori(0, count) as i:
                    if lru is not None:
                        st.enter(i + 1, LRU_STEPS)
                        j = i + lru
                        n = i + (lru + 1)
                        xb = xr[:, bass.ds(j, 1), :].rearrange("p o n -> p (o n)")
                        gb = gr[:, bass.ds(j, 1), :].rearrange("p o n -> p (o n)")
                    for u in range(UPP):
                        if lru is not None and u == 3:
                            lru_tail(xb, gb, n)
                        split_lo(i * UPP + (unit + RING + u), u)
                        if lru is not None and u == 0:
                            lru_conv(xb, j)
                        if lru is not None and u == 2:
                            lru_logs(gb, n)
                if lru is not None:
                    st.leave(count, LRU_STEPS)

            def lru_conv(xb, j):
                st.done(nc.vector.tensor_copy(lc[:], lconst[:, :, bass.ds(j, 1)].rearrange("p k o -> p (k o)")))
                st.wait()
                st.done(nc.vector.tensor_scalar(lt[0][:], xb, lc[:, 3:4], lc[:, 4:5], ALU.mult, ALU.add))
                for k in (2, 1, 0):
                    off = TAPS - 1 - k
                    st.wait()
                    ins = nc.vector.scalar_tensor_tensor(lt[0][:, off:], xb[:, 0:SEQ - off], lc[:, k:k + 1],
                                                         lt[0][:, off:], ALU.mult, ALU.add)
                    if k:
                        st.done(ins)
                ins.then_inc(xc_ready, 1)

            def lru_logs(gb, n):
                dve.wait_ge(gates_ready, n)
                st.done(nc.vector.tensor_scalar(lt[1][:], lt[1][:], 1.0, lc[:, 7:8], ALU.add, ALU.mult))
                st.done(nc.vector.scalar_tensor_tensor(gb, lt[3][:], 1.0, gb, ALU.add, ALU.mult))
                st.done(nc.vector.scalar_tensor_tensor(lt[2][:], lt[2][:], 1.0, lt[0][:], ALU.add, ALU.mult))
                st.wait()
                st.done(nc.vector.tensor_scalar(lt[3][:], lt[1][:], 2.0, -SERIES_TO, ALU.mult, ALU.max))
                st.wait()
                nc.vector.scalar_tensor_tensor(lt[4][:], lt[1][:], 2.0, lt[3][:], ALU.mult, ALU.subtract
                                               ).then_inc(logs_ready, 1)
                st.done(nc.vector.tensor_scalar(lt[5][:], lt[3][:], 1.0 / 720, None, ALU.mult))
                for c in (1.0 / 120, 1.0 / 24, 1.0 / 6, 0.5, 1.0):
                    st.wait()
                    st.done(nc.vector.scalar_tensor_tensor(lt[5][:], lt[5][:], c, lt[3][:], ALU.add, ALU.mult))
                st.wait()
                dve.wait_ge(decays_ready, n)
                st.done(nc.vector.tensor_scalar(lt[4][:], lt[4][:], -1.0, 1.0, ALU.mult, ALU.add))
                st.wait()
                st.done(nc.vector.scalar_tensor_tensor(lt[4][:], lt[5][:], 1.0, lt[4][:], ALU.add, ALU.mult))
                st.wait()
                nc.vector.tensor_tensor(lt[4][:], lt[4][:], lt[5][:], ALU.subtract).then_inc(var_ready, 1)

            def lru_tail(xb, gb, n):
                dve.wait_ge(dev_ready, n)
                st.done(nc.vector.scalar_tensor_tensor(lt[4][:], lt[4][:], 0.5, lt[2][:], ALU.mult, ALU.mult))
                st.wait()
                st.done(nc.vector.tensor_tensor_scan(lt[1][:], lt[0][:], lt[4][:], 0.0, ALU.mult, ALU.add))
                st.wait()
                nc.vector.scalar_tensor_tensor(xb, lt[1][:], 0.5, gb, ALU.mult, ALU.mult).then_inc(rnn_done, 1)

            panels(U_RNN, 4)
            panels(U_RNN + 16, 4)
            panels(U_QKV, 4, 0)
            panels(U_GA, 4, 4)

            for u in range(RING):
                split_lo(U_PAIR + u, u)
            for b in range(2 * LORA_KB):
                dve.wait_ge(c_hi_ready, b + 1)
                at = ROW_QA + b
                nc.vector.scalar_tensor_tensor(c_lo[:, b, :], qkvc[:, b, :], cols[:, at:at + 1],
                                               c_hi[:, b, :].bitcast(F32), ALU.mult, ALU.subtract
                                               ).then_inc(c_lo_ready, 1)
            dve.wait_ge(unit_used, U_PAIR)
            nc.vector.tensor_copy(kr_tok[:], ps[:, 0:NT, 0:ROPE]).then_inc(kr_ready, 1)
            dve.wait_ge(kr_squared, 1)
            st.done(nc.vector.tensor_reduce(krs, sqt[:, :, 0, 0:ROPE], AX_X, ALU.add))
            st.wait()
            st.done(mean_eps(krs, krs, ROPE))
            dve.wait_ge(latent_summed, 2)
            st.done(mean_eps(small[:, 12:20], ps[:, 4, 0:8], 4 * P))
            st.wait()
            dve.sem_inc(latent_var_ready, 1)
            dve.wait_ge(latent_std_ready, 1)
            st.done(nc.vector.reciprocal(small[:, 12:24], small[:, 12:24]))
            st.wait()

            def rotate(dst, src, shape):
                cos, sin = (rope_t[:, k, :, :] for k in range(2))
                temps = [a[:] for a in rt]
                if len(shape) == 3:
                    temps = [a[:, :, 0, :] for a in rt]
                else:
                    cos, sin = (a.unsqueeze(2).broadcast_to(shape) for a in (cos, sin))
                lo_, hi_ = src[..., 0:ROPE // 2], src[..., ROPE // 2:ROPE]
                for a, (h_, c_) in zip(temps, ((lo_, cos), (hi_, sin), (lo_, sin), (hi_, cos))):
                    st.done(nc.vector.tensor_tensor(a, h_, c_, ALU.mult))
                st.wait()
                for d in dst:
                    st.done(nc.vector.tensor_tensor(d[..., 0:ROPE // 2], temps[0], temps[1], ALU.subtract))
                    last = nc.vector.tensor_tensor(d[..., ROPE // 2:ROPE], temps[2], temps[3], ALU.add)
                    if d is not dst[-1]:
                        st.done(last)
                return last

            dve.wait_ge(gains_landed, 64)
            st.done(nc.vector.tensor_tensor(kr_tok[:], kr_tok[:], krs.unsqueeze(2).broadcast_to([P, NT, ROPE]),
                                            ALU.mult))
            st.wait()
            st.done(nc.vector.tensor_tensor(kr_tok[:], kr_tok[:],
                                            gain_b[:, 320:384].unsqueeze(1).broadcast_to([P, NT, ROPE]), ALU.mult))
            st.wait()
            rotate([qpe[:, :, 0, :], qpe[:, :, 1, :]], kr_tok[:], [P, NT, ROPE // 2]).then_inc(kpe_ready, 1)
            dve.wait_ge(kpe_turned, 1)
            nc.vector.tensor_copy(kpt[:], ps[:, 5, :]).then_inc(kpt_ready, 1)

            def pair(g, prev, cur):
                gp = g - 1
                for k in range(11):
                    if cur and k == 2:
                        dve.wait_ge(unit_used, g * 4 + (U_PAIR + 2))
                        for t in range(NT):
                            ins = nc.vector.tensor_scalar(q_tok[:, t, :, :].rearrange("p h n -> p (h n)"),
                                                          ps[:, t, 0:2 * QH], rsq[:, t:t + 1], None, ALU.mult)
                        ins.then_inc(q_read, 1)
                    if cur and k < 4:
                        split_lo(g * 4 + (U_PAIR + RING + k), k)
                    if prev and k == 1:
                        dve.wait_ge(ga_tanh_ready, g)
                        st.done(nc.vector.scalar_tensor_tensor(gth[:], gth[:], 1.0, ga[:, bass.ds(gp * 2, 2), :],
                                                               ALU.add, ALU.mult))
                    if prev and k < 8:
                        n = (k % 4 + 1) * P
                        dve.wait_ge(scored, gp * 8 + k + 1)
                        st.done(nc.vector.tensor_reduce(sm[:, 0, k:k + 1], ps[:, 4 + k % 2, 0:n], AX_X, ALU.max))
                        st.wait()
                        nc.vector.tensor_scalar(sm[:, 1, k:k + 1], sm[:, 0, k:k + 1], -SM_SCALE, None, ALU.mult
                                                ).then_inc(max_ready, 1)
                    if prev and 1 <= k < 9:
                        j = k - 1
                        n = (j % 4 + 1) * P
                        dve.wait_ge(exp_ready, gp * 8 + j + 1)
                        st.done(nc.vector.reciprocal(sm[:, 3, j:j + 1], sm[:, 2, j:j + 1]))
                        st.wait()
                        nc.vector.tensor_scalar(prob[:, j % 2, 0:n], prob[:, j % 2, 0:n], sm[:, 3, j:j + 1], None,
                                                ALU.mult).then_inc(prob_ready, 1)
                    if prev and k == 8:
                        head_out(gp, 0)
                    if prev and k >= 3:
                        j = k - 3
                        qb = j % 4
                        if j == NT:
                            dve.wait_ge(head_summed, gp * 2 + 1)
                        dve.wait_ge(prob_turned, gp * 8 + j + 1)
                        nc.vector.tensor_copy(pt[:, 0:qb + 1, qb * P:(qb + 1) * P],
                                              ps[:, 6, 0:(qb + 1) * P].rearrange("p (k q) -> p k q", q=P)
                                              ).then_inc(pt_ready, 1)
                    if cur and k == 4:
                        dve.wait_ge(sq_ready, g * 2 + 1)
                        st.done(nc.vector.tensor_reduce(nrm[:, 0, :, :], sqt[:, :, :, 0:NOPE], AX_X, ALU.add))
                        nc.vector.tensor_reduce(nrm[:, 1, :, :], sqt[:, :, :, NOPE:], AX_X, ALU.add
                                                ).then_inc(q_reduced, 1)
                    if cur and k == 5:
                        dve.wait_ge(unit_used, g * 4 + (U_PAIR + 4))
                        for t in range(NT):
                            ins = nc.vector.tensor_scalar(kv_tok[:, t, :, :].rearrange("p h n -> p (h n)"),
                                                          ps[:, t, :], rskv[:, t:t + 1], None, ALU.mult)
                        ins.then_inc(kv_read, 1)
                    if cur and k == 7:
                        dve.wait_ge(sq_ready, g * 2 + 2)
                        dve.wait_ge(q_reduced, g + 1)
                        st.done(nc.vector.tensor_reduce(nrm[:, 2, :, :], sqt[:, :, :, 0:NOPE], AX_X, ALU.add))
                        st.wait()
                        st.done(mean_eps(nrm[:, 0, :, :], nrm[:, 0, :, :], NOPE))
                        st.done(mean_eps(nrm[:, 1, :, :], nrm[:, 1, :, :], ROPE))
                        mean_eps(nrm[:, 2, :, :], nrm[:, 2, :, :], NOPE).then_inc(nrm_ready, 1)
                    if cur and k == 8:
                        norm_pair(g)
                if prev:
                    head_out(gp, 1)
                if cur:
                    dve.wait_ge(pair_turned, g + 1)
                    st.done(nc.vector.tensor_copy(qt[:], ps[:, 4:6, :]))
                    st.done(nc.vector.tensor_copy(kt[:], ps[:, 6:8, :]))
                    nc.vector.tensor_copy(qpt[:], ps[:, 0, :]).then_inc(qk_ready, 1)

            def head_out(gp, h):
                dve.wait_ge(head_summed, gp * 2 + h + 1)
                nc.vector.scalar_tensor_tensor(ga[:, bass.ds(gp * 2 + h, 1), :].rearrange("p o n -> p (o n)"),
                                               ps[:, 7, :], 0.5, gth[:, h, :], ALU.mult, ALU.mult
                                               ).then_inc(head_read, 1)

            def norm_pair(g):
                dve.wait_ge(nrm_std_ready, g + 1)
                st.done(nc.vector.reciprocal(nrm[:], nrm[:]))
                st.wait()
                parts = ((q_tok, 0, NOPE, 0, 0), (q_tok, NOPE, ROPE, 1, 2 * NOPE), (kv_tok, 0, NOPE, 2, NOPE))
                views = [a[:, :, :, at:at + n].rearrange("p t h n -> p (t h) n") for a, at, n, _, _ in parts]
                for v_, (_, _, n, k, _) in zip(views, parts):
                    st.done(nc.vector.tensor_tensor(
                        v_, v_, nrm[:, k, :, :].rearrange("p t h -> p (t h)").unsqueeze(2).broadcast_to([P, 2 * NT, n]),
                        ALU.mult))
                for at, (v_, (_, _, n, _, gain)) in enumerate(zip(views, parts)):
                    st.wait(2)
                    st.done(nc.vector.tensor_tensor(
                        v_, v_, gain_b[:, gain:gain + n].unsqueeze(1).broadcast_to([P, 2 * NT, n]), ALU.mult))
                st.wait()
                rotate([qpe[:]], q_tok[:, :, :, NOPE:], [P, NT, 2, ROPE // 2]).then_inc(tok_ready, 1)

            pair(0, False, True)
            with dve.Fori(1, PAIRS) as g:
                st.enter(g, PAIR_STEPS)
                pair(g, True, True)
            st.leave(PAIRS - 1, PAIR_STEPS)
            pair(PAIRS, True, False)

            for b in range(KB):
                src = xr[:, b, :] if b < 8 else ga[:, b - 8, :]
                dve.wait_ge(y2_hi_ready, b + 1)
                nc.vector.tensor_tensor(y2_lo[:, b, :], src, y2_hi[:, b, :].bitcast(F32), ALU.subtract
                                        ).then_inc(y2_lo_ready, 1)
            dve.sem_inc(z_bank_freed, NT)
            dve.wait_ge(y2_lo_ready, KB)
            dve.sem_inc(out_stored, 16)

            def out2_panel(i, last):
                for u in range(OUT2_UPP):
                    if u == OUT2_UPP - 1:
                        dve.wait_ge(xo_landed, i * 16 + 16)
                        dve.wait_ge(out_stored, i * 16 + 16)
                        for t in range(NT):
                            if t < NT - 1:
                                dve.wait_ge(z_bank_done, i * (NT - 1) + t + 1)
                            else:
                                dve.wait_ge(unit_used, i * OUT2_UPP + (U_OUT2 + OUT2_UPP))
                            nc.vector.tensor_tensor(oo[:, t, :], ps[:, t, :], gateb[:, bass.ds(i * TCOL, TCOL)],
                                                    ALU.mult).then_inc(z_bank_freed, 1)
                        dve.wait_ge(z_bank_freed, i * NT + 2 * NT)
                        nc.vector.tensor_tensor(oo[:], oo[:], xo[:], ALU.add).then_inc(o_ready, 1)
                        dve.wait_ge(o_ready, i + 1)
                        dve.sem_inc(xo_free, 1)
                    if not last or u < OUT2_UPP - RING:
                        split_lo(i * OUT2_UPP + (U_OUT2 + RING + u), u % RING)

            with dve.Fori(0, OUT_PANELS - 1) as i:
                out2_panel(i, False)
            out2_panel(OUT_PANELS - 1, True)

        @block.tensor
        def _(pe):
            pe.wait_ge(consts_made, 1)
            for kb in range(KB):
                if kb < 1:
                    pe.wait_ge(x_normed, NT)
                if kb >= 8:
                    pe.wait_ge(hn_lo_ready, kb - 7)
                if kb == 6:
                    pe.wait_ge(small_landed, SMALL * 16)
                    for t in range(4):
                        mm = nc.tensor.transpose(ps[:, 7, t * P:(t + 1) * P], vrows[:, t, :], ident[:])
                    mm.then_inc(cols_turned, 1)
                    nc.tensor.matmul(ps[:, 6, 0:HEADS // 2], halves[:], d2[:], start=True, stop=True
                                     ).then_inc(cols_turned, 1)
                    pe.wait_ge(dve_step, 3)
                    pe.wait_ge(cols_ready, 1)
                for t in range(NT):
                    mm = nc.tensor.transpose(ps[:, kb % 8, t * P:(t + 1) * P], xt[:, t, kb * P:(kb + 1) * P], ident[:])
                mm.then_inc(x_turned, 1)

            def three(out_, a_hi, a_lo, b_hi, b_lo, start, stop):
                nc.tensor.matmul(out_, a_hi, b_hi, start=start, stop=False)
                nc.tensor.matmul(out_, a_hi, b_lo, start=False, stop=False)
                return nc.tensor.matmul(out_, a_lo, b_hi, start=False, stop=stop)

            for u in range(DT_UNITS):
                pe.wait_ge(lo_ready, u + 1)
                if u == 0:
                    pe.wait_ge(hn_lo_ready, KB)
                for k in range(UKT):
                    kb = u * UKT + k
                    for t in range(NT):
                        w = [unit_ap(r, u, HEADS)[:, k, :] for r in (w_hi, w_lo)]
                        mm = three(ps[:, t, 0:HEADS], hn_hi[:, kb, t * P:(t + 1) * P],
                                   hn_lo[:, kb, t * P:(t + 1) * P], *w, kb == 0, kb == KB - 1)
                mm.then_inc(unit_used, 1)
            for t in range(NT):
                pe.wait_ge(adt_ready, t + 1)
                mm = nc.tensor.matmul(ps[:, 4, t * HEADS:(t + 1) * HEADS], tri[:], dtv[5][:, t, :],
                                      start=True, stop=True)
            mm.then_inc(cs_summed, 1)
            pe.wait_ge(cs_ready, 1)
            for t in range(NT):
                mm = nc.tensor.transpose(ps[0:HEADS, 5, t * P:(t + 1) * P], prep[:, NT + t, :], ident[:])
            mm.then_inc(cs_turned, 1)

            def project(g, u):
                p, kq = divmod(u, UPP)
                s = u % RING
                if kq == 0:
                    if p == 0:
                        if not isinstance(g, int) or g:
                            pe.wait_ge(z_acc_freed, g * 2)
                    elif p >= 2:
                        pe.wait_ge(x_acc_freed, g * 3 + p - 1)
                pe.wait_ge(lo_ready, g * GU + u + DT_UNITS + 1)
                for k in range(UKT):
                    kb = kq * UKT + k
                    for n in range(2):
                        w = [unit_ap(r, s)[:, k, n * P:(n + 1) * P] for r in (w_hi, w_lo)]
                        mm = three(ps[:, 2 * (p % 2) + n, :], *w, hn_hi[:, kb, :], hn_lo[:, kb, :],
                                   kb == 0, kb == KB - 1)
                mm.then_inc(unit_used, 1)

            def chunk_turn(gp, c):
                at = slice(c * Q, (c + 1) * Q)
                if c == 0:
                    pe.wait_ge(conv_done, gp * 3 + 3)
                else:
                    pe.wait_ge(state_read, gp * 3 + c)
                for b in range(GB):
                    nc.tensor.transpose(ps[:, 4, b * P:(b + 1) * P], xst[:, b, at], ident[:])
                nc.tensor.transpose(ps[:, 5, 0:P], bct[:, 0, at], ident[:])
                nc.tensor.matmul(ps[:, 5, P:2 * P], bct[:, 0, at], bct[:, 1, at], start=True, stop=True
                                 ).then_inc(chunk_in, 1)

            def chunk_sum(gp, c):
                at = slice(c * Q, (c + 1) * Q)
                pe.wait_ge(chunk_mid, gp * NQ + c + 1)
                if c:
                    pe.wait_ge(yt_ready, gp * NQ + c)
                    nc.tensor.matmul(ps[:, 7, :], bct[:, 1, at], state[:].rearrange("p r d -> p (r d)"),
                                     start=True, stop=True)
                for r in range(HPG):
                    mm = nc.tensor.matmul(ps[:, 6, r * HD:(r + 1) * HD], seg[:, r, :], xdt[:, r, :],
                                          start=True, stop=True)
                if c < NQ - 1:
                    mm = nc.tensor.matmul(ps[:, 4, :], btok[:], xw[:].rearrange("p r d -> p (r d)"),
                                          start=True, stop=True)
                mm.then_inc(chunk_summed, 1)

            def chunk_turn_back(gp, c):
                pe.wait_ge(ytok_ready, gp * NQ + c + 1)
                for b in range(GB):
                    mm = nc.tensor.transpose(ps[:, 7, b * P:(b + 1) * P], ytok[:, b, :], ident[:])
                mm.then_inc(ytok_turned, 1)

            def body(g, prev, cur):
                gp = g - 1
                for u in range(GU):
                    if cur:
                        project(g, u)
                    if prev and u in (1, 4, 7, 10):
                        chunk_turn(gp, u // 3)
                    if prev and u in (3, 6, 9, 12):
                        chunk_sum(gp, u // 3 - 1)
                    if prev and u in (5, 8, 11, 14):
                        chunk_turn_back(gp, (u - 5) // 3)

            walk(pe, body)

            def tok_unit(unit_wait, slot, n, lhs, kb0, first, last, freed=None, done=None):
                a_hi, a_lo = lhs
                pe.wait_ge(lo_ready, unit_wait)
                for t in range(NT):
                    if first and freed is not None:
                        freed(t)
                    at = slice(t * P, (t + 1) * P)
                    for k in range(TKT):
                        w = [r[:, slot, k * n:(k + 1) * n] for r in (w_hi, w_lo)]
                        mm = three(ps[:, t, 0:n], a_hi[:, kb0 + k, at], a_lo[:, kb0 + k, at], *w,
                                   first and k == 0, last and k == TKT - 1)
                    if last and done is not None and t < NT - 1:
                        mm.then_inc(done, 1)
                mm.then_inc(unit_used, 1)

            pe.wait_ge(yt_free, GROUPS + 1)
            for t in range(NT):
                mm = nc.tensor.matmul(ps[:, 4, t:t + 1], ysq[:, t * P:(t + 1) * P], ones[:, 0:1],
                                      start=True, stop=True)
            mm.then_inc(ysq_summed, 1)
            with pe.Fori(0, OUT_PANELS) as i:
                for u in range(OUT1_UPP):
                    pe.wait_ge(y_lo_ready, (u + 1) * TKT)
                    tok_unit(i * OUT1_UPP + (U_OUT1 + u + 1), u % RING, TCOL, (y_hi, y_lo), u * TKT,
                             u == 0, u == OUT1_UPP - 1,
                             lambda t: pe.wait_ge(d_bank_freed, i * NT + t + 1), d_bank_done)

            for k in range(3):
                pe.wait_ge(adab_landed, 16 * (k + 1))
                if k < 2:
                    for b in range(KB):
                        mm = nc.tensor.matmul(ps[:, 4 + k, b:b + 1], adab[:, b * P:(b + 1) * P], ones[:, 0:1],
                                              start=True, stop=True)
                else:
                    pe.wait_ge(d_bank_freed, NT * (OUT_PANELS + 1))
                    for j in range(D // 512):
                        mm = nc.tensor.matmul(ps[:, j, :], ones[:], adab[:, j * 512:(j + 1) * 512],
                                              start=True, stop=True)
                mm.then_inc(ada_reduced, 1)
            pe.wait_ge(xh_ready, NT)
            pe.wait_ge(ada_cols_ready, 1)
            for kb in range(KB):
                if kb >= 4:
                    pe.wait_ge(h_mod_ready, kb - 3)
                for t in range(NT):
                    mm = nc.tensor.transpose(ps[:, 4 + kb % 4, t * P:(t + 1) * P], xh[:, t, kb * P:(kb + 1) * P],
                                             ident[:])
                mm.then_inc(h_turned, 1)
            pe.wait_ge(h_lo_ready, KB)

            def panels(part, unit, count, lru=None):
                with pe.Fori(0, count) as i:
                    for u in range(UPP):
                        pe.wait_ge(lo_ready, i * UPP + (unit + u + 1))
                        for n in range(2):
                            if u == 0:
                                pe.wait_ge(f_bank_freed, i * 2 + (part * 8 + n + 1))
                            for k in range(UKT):
                                kb = u * UKT + k
                                w = [unit_ap(r, u)[:, k, n * P:(n + 1) * P] for r in (w_hi, w_lo)]
                                mm = three(ps[:, n, :], *w, h_hi[:, kb, :], h_lo[:, kb, :],
                                           kb == 0, kb == KB - 1)
                            if n == 0 and u == UPP - 1:
                                mm.then_inc(f_bank_done, 1)
                        mm.then_inc(unit_used, 1)
                        if lru is not None and u == 1:
                            j = i + (lru + 1)
                            pe.wait_ge(xc_ready, j)
                            pe.wait_ge(wblk_landed, i * 64 + (lru + 1) * 64)
                            for kind in range(2):
                                mm = nc.tensor.matmul(ps[:, 4 + kind, :], wblk[:, kind, :], lt[0][:],
                                                      start=True, stop=True)
                            mm.then_inc(gates_summed, 1)

            panels(0, U_RNN, 4)
            panels(1, U_RNN + 16, 4)
            panels(2, U_QKV, 4, 0)
            panels(3, U_GA, 4, 4)

            pe.wait_ge(f_bank_freed, 34)
            for u in range(DT_UNITS):
                pe.wait_ge(lo_ready, U_KR + u + 1)
                for k in range(UKT):
                    kb = u * UKT + k
                    for t in range(NT):
                        w = [unit_ap(r, u, ROPE)[:, k, :] for r in (w_hi, w_lo)]
                        mm = three(ps[:, t, 0:ROPE], h_hi[:, kb, t * P:(t + 1) * P],
                                   h_lo[:, kb, t * P:(t + 1) * P], *w, kb == 0, kb == KB - 1)
                mm.then_inc(unit_used, 1)

            for part in range(2):
                pe.wait_ge(latent_squared, part + 1)
                for t in range(NT):
                    for b in range(LORA_KB):
                        mm = nc.tensor.matmul(ps[:, 4, part * NT + t:part * NT + t + 1], pt[:, b, t * P:(t + 1) * P],
                                              ones[:, 0:1], start=b == 0, stop=b == LORA_KB - 1)
                mm.then_inc(latent_summed, 1)
            pe.wait_ge(kpe_ready, 1)
            for t in range(NT):
                mm = nc.tensor.transpose(ps[:, 5, t * P:(t + 1) * P], qpe[:, t, :, :].rearrange("p h n -> p (h n)"),
                                         ident[:])
            mm.then_inc(kpe_turned, 1)
            pe.wait_ge(kpt_ready, 1)
            pe.wait_ge(c_lo_ready, 2 * LORA_KB)
            pe.wait_ge(mask_ready, 1)

            def score(gp, k):
                h, qb = divmod(k, NT)
                n = (qb + 1) * P
                at = slice(qb * P, n)
                out_ = ps[:, 4 + k % 2, 0:n]
                if k >= 2:
                    pe.wait_ge(exp_ready, gp * 8 + k - 1)
                nc.tensor.matmul(out_, qt[:, h, at], kt[:, h, 0:n], start=True, stop=False)
                rows = slice(h * ROPE, (h + 1) * ROPE)
                nc.tensor.matmul(out_, qpt[rows, at], kpt[rows, 0:n], start=False, stop=False)
                nc.tensor.matmul(ps[:, 4 + k % 2, qb * P:n], ident[:], maskn[:], start=False, stop=True
                                 ).then_inc(scored, 1)

            def turn_prob(gp, j):
                qb = j % 4
                pe.wait_ge(prob_ready, gp * 8 + j + 1)
                if j:
                    pe.wait_ge(pt_ready, gp * 8 + j)
                for kb in range(qb + 1):
                    mm = nc.tensor.transpose(ps[:, 6, kb * P:(kb + 1) * P], prob[:, j % 2, kb * P:(kb + 1) * P],
                                             ident[:])
                mm.then_inc(prob_turned, 1)

            def head_sum(gp, h):
                pe.wait_ge(pt_ready, gp * 8 + 4 * h + 4)
                if h:
                    pe.wait_ge(head_read, gp * 2 + 1)
                for kb in range(NT):
                    mm = nc.tensor.matmul(ps[:, 7, kb * P:], vt[:, kb, h, :], pt[:, kb, kb * P:],
                                          start=kb == 0, stop=kb == NT - 1)
                mm.then_inc(head_summed, 1)

            def pair(g, prev, cur):
                gp = g - 1
                if prev:
                    pe.wait_ge(qk_ready, g)
                    pe.wait_ge(v_ready, g)
                for k in range(10):
                    if cur and k < 4:
                        half = k % 2
                        if k == 2:
                            pe.wait_ge(q_read, g + 1)
                        if k < 2:
                            tok_unit(g * 4 + (U_PAIR + k + 1), k, 2 * QH, (c_hi, c_lo), half * TKT, half == 0, half == 1)
                        else:
                            tok_unit(g * 4 + (U_PAIR + k + 1), k, TCOL, (c_hi, c_lo), LORA_KB + half * TKT,
                                     half == 0, half == 1)
                    if prev and k < 8:
                        score(gp, k)
                    if prev and k == 7:
                        head_sum(gp, 0)
                    if prev and k >= 2:
                        turn_prob(gp, k - 2)
                if prev:
                    head_sum(gp, 1)
                if cur:
                    pe.wait_ge(tok_ready, g + 1)
                    pe.wait_ge(kv_read, g + 1)
                    if prev:
                        pe.wait_ge(head_read, g * 2)
                    for h in range(2):
                        for t in range(NT):
                            at = slice(t * P, (t + 1) * P)
                            nc.tensor.transpose(ps[:, 4 + h, at], q_tok[:, t, h, 0:NOPE], ident[:])
                            nc.tensor.transpose(ps[:, 6 + h, at], kv_tok[:, t, h, 0:NOPE], ident[:])
                    for t in range(NT):
                        mm = nc.tensor.transpose(ps[:, 0, t * P:(t + 1) * P],
                                                 qpe[:, t, :, :].rearrange("p h n -> p (h n)"), ident[:])
                    mm.then_inc(pair_turned, 1)

            pair(0, False, True)
            with pe.Fori(1, PAIRS) as g:
                pair(g, True, True)
            pair(PAIRS, True, False)

            with pe.Fori(0, OUT_PANELS) as i:
                for u in range(OUT2_UPP):
                    pe.wait_ge(y2_lo_ready, (u + 1) * TKT)
                    tok_unit(i * OUT2_UPP + (U_OUT2 + u + 1), u % RING, TCOL, (y2_hi, y2_lo), u * TKT,
                             u == 0, u == OUT2_UPP - 1,
                             lambda t: pe.wait_ge(z_bank_freed, i * NT + t + 1), z_bank_done)


_INS = ["x", "ln_g", "final_g", "ssm_w_in", "ssm_conv_w", "ssm_conv_b", "ssm_dt_bias", "ssm_a_log", "ssm_d",
        "ssm_norm_g", "ssm_w_out", "c_2", "positions_2", "w_ada_2", "b_ada_2", "w_in_2", "conv_w_2", "conv_b_2",
        "w_rg_a_2", "b_rg_a_2", "w_rg_x_2", "b_rg_x_2", "lru_lambda_2", "q_a_norm_2", "w_uq_2", "kv_a_norm_2",
        "w_ukv_2", "q_norm_nope_2", "q_norm_rope_2", "k_norm_nope_2", "k_norm_rope_2", "w_out_2"]


def kernel(**inputs):
    import concourse.bacc as _bacc
    from concourse.bass_utils import run_bass_kernel_spmd as _run

    nc = _bacc.Bacc("TRN2", target_bir_lowering=False, num_devices=1)
    arrays = {f"in_{name}_dram": np.ascontiguousarray(inputs[name]) for name in _INS}
    steps = np.arange(0, ROPE, 2, dtype=np.float32) / np.float32(ROPE)
    arrays["in_inv_freq_dram"] = (np.float32(1.0) / np.power(np.float32(10000.0), steps)).astype(np.float32)
    args = [nc.dram_tensor(name, a.shape, mybir.dt.from_np(a.dtype), kind="ExternalInput").ap()
            for name, a in arrays.items()]
    out = nc.dram_tensor("out_0_dram", (1, SEQ, D), F32, kind="ExternalOutput").ap()
    build_program(nc, *args, out)
    r = _run(nc, [arrays], core_ids=[0])
    return r.results[0]["out_0_dram"]
```

```python
from contextlib import ExitStack

import numpy as np
import concourse.bass as bass
from concourse import mybir

F32 = mybir.dt.float32
F32R = mybir.dt.float32r
I32 = mybir.dt.int32
ALU = mybir.AluOpType
ACT = mybir.ActivationFunctionType
AX_X = mybir.AxisListType.X

P = 128
SEQ = 512
NT = SEQ // P
D = 2048
KB = D // P
EPS = 1e-6

D_INNER = 4096
GROUPS = 8
HPG = 8
HD = 64
HEADS = GROUPS * HPG
STATE = 128
TAPS = 4
CONV_DIM = D_INNER + 2 * GROUPS * STATE
CONV_BLOCKS = CONV_DIM // P
GB = D_INNER // GROUPS // P
Q = P
NQ = SEQ // Q

RING = 4
UKT = 4
UCOL = 256
UNIT = UKT * UCOL
UPP = KB // UKT
PANELS = 5
GU = PANELS * UPP
DT_UNITS = KB // UKT
ADA = 3 * D
ADA_COLS = ADA // GROUPS

ROW_CONV_W = (0, 48, 128, 176)
ROW_LN, ROW_QA, ROW_KVA = 96, 112, 116
ROW_NORM = 224
ROW_CONV_B = 256
ROW_SHIFT_B, ROW_SCALE_B = 304, 320
ROW_CONV2_W, ROW_CONV2_B, ROW_LRU = 336, 368, 376
ROW_RG_A, ROW_RG_X, ROW_C = 384, 392, 400


RNN_BLOCKS = 8
ATT_HEADS = 8
NOPE, ROPE, VH = 128, 64, 128
QH = NOPE + ROPE
PAIRS = ATT_HEADS // 2
LORA_KB = 4
COL_QKV, COL_KR, COL_GA = 2048, 3072, 3136
LRU_C = 8.0
SM_SCALE = float(QH) ** -0.5
SERIES_TO = 0.25
NEG = -1.0e30

TKT, TCOL = 2, 512
OUT1_UPP = D_INNER // P // TKT
Y_HALF = D_INNER // P // 2
Y_LAST = (D_INNER // P - GB) // 2
OUT2_UPP = KB // TKT
OUT_PANELS = D // TCOL
U_OUT1 = DT_UNITS + GROUPS * GU
L_OUT1 = 1 + GROUPS * (GU // RING + 2)
AHEAD = 2
U_RNN = U_OUT1 + OUT_PANELS * OUT1_UPP
RNN_PANELS, QKV_PANELS, GA_PANELS = 8, 4, 4
U_QKV = U_RNN + RNN_PANELS * UPP
U_GA = U_QKV + QKV_PANELS * UPP
U_KR = U_GA + GA_PANELS * UPP
U_PAIR = U_KR + DT_UNITS
U_OUT2 = U_PAIR + PAIRS * 4
U_END = U_OUT2 + OUT_PANELS * OUT2_UPP


def landed_before(unit):
    return L_OUT1 + (unit - U_OUT1) // RING + (unit > U_OUT1)


LRU_STEPS = 18
PAIR_STEPS = 21
ROUND = 1.5 * 2 ** 23
PI32 = 3.1415925
TURN = (6.28125, 2.0 ** -9 - 2.0 ** -16, 2 * np.pi - 6.28125 - 2.0 ** -9 + 2.0 ** -16)


LAST_SCAN = (1, 2, 4, 5, 7, 8, 10, 11)


class Steps:

    def __init__(self, eng, sem):
        self.eng, self.sem, self.n, self.base = eng, sem, 0, 0

    def done(self, instruction):
        instruction.then_inc(self.sem, 1)
        self.n += 1

    def wait(self, behind=0):
        self.eng.wait_ge(self.sem, self.base + (self.n - behind))

    def enter(self, g, per):
        self.base = (g - 1) * per
        self.first = self.n

    def leave(self, times, per):
        assert self.n - self.first == per, (self.n - self.first, per)
        self.n = self.first + times * per
        self.base = 0


def columns(ap, start, size):
    return ap[:, bass.ds(start, size)]


def build_program(nc, x, ln_g, final_g, ssm_w_in, ssm_conv_w, ssm_conv_b, ssm_dt_bias, ssm_a_log, ssm_d,
                  ssm_norm_g, ssm_w_out, c_2, positions_2, w_ada_2, b_ada_2, w_in_2, conv_w_2, conv_b_2,
                  w_rg_a_2, b_rg_a_2, w_rg_x_2, b_rg_x_2, lru_lambda_2, q_a_norm_2, w_uq_2, kv_a_norm_2,
                  w_ukv_2, q_norm_nope_2, q_norm_rope_2, k_norm_nope_2, k_norm_rope_2, w_out_2, inv_freq, out):
    ctx = ExitStack()
    with ctx:
        sem_names = {}

        def sem(name):
            assert name not in sem_names
            sem_names[name] = ctx.enter_context(nc.semaphore(name))
            return sem_names[name]

        def sb(name, shape, dt=F32, scope=ctx):
            return scope.enter_context(nc.sbuf_tensor(name, shape, dt))

        cs_rows = nc.dram_tensor("cs_rows", (HEADS, SEQ), F32).ap()
        y_rows = nc.dram_tensor("y_rows", (D_INNER, SEQ), F32).ap()
        x1_rows = nc.dram_tensor("x1_rows", (SEQ, D), F32).ap()
        ada_part = nc.dram_tensor("ada_part", (P, ADA), F32).ap()

        ps = ctx.enter_context(nc.psum_tensor("ps", [P, 8, 512], F32))

        w_raw = sb("w_raw", [P, RING, UNIT])
        w_hi = sb("w_hi", [P, RING, UNIT], F32R)
        w_lo = sb("w_lo", [P, RING, UNIT], F32R)
        ident = sb("ident", [P, P])
        ones = sb("ones", [P, P])
        cols = sb("cols", [P, 4 * P])
        ysq = sb("ysq", [P, SEQ])

        small = sb("small", [P, 64])
        yrs, x1ss, x1rs = small[:, 0:4], small[:, 4:8], small[:, 8:12]
        rsq, rskv, krs = small[:, 12:16], small[:, 16:20], small[:, 20:24]
        shc, scc = small[:, 24:40], small[:, 40:56]
        x1gs, x1rr = small[:, 56:60], small[:, 60:64]
        x1_part = sb("x1_part", [P, 2, NT])

        scope1 = ExitStack()
        ada_raw = sb("ada_raw", [P, 2, ADA_COLS], F32, scope1)
        ada_acc = sb("ada_acc", [P, ADA_COLS], F32, scope1)
        sb("kept_later", [P, 64], F32, scope1)
        hn_hi = sb("hn_hi", [P, KB, SEQ], F32R, scope1)
        hn_lo = sb("hn_lo", [P, KB, SEQ], F32R, scope1)
        xraw = sb("xraw", [P, 6, 3 + SEQ], F32, scope1)
        tri = sb("tri", [P, P], F32, scope1)
        halves = sb("halves", [2, P], F32, scope1)
        d2 = sb("d_pairs", [2, HEADS // 2], F32, scope1)
        dcol = sb("dcol", [P, HEADS // 2], F32, scope1)
        convc = sb("convc", [P, TAPS + 1, CONV_BLOCKS], F32, scope1)
        prep = sb("prep", [P, 3 * NT, HEADS], F32, scope1)
        silu_c = sb("silu_c", [P, KB], F32, scope1)
        th_c = sb("th_c", [P, KB], F32, scope1)

        scope_x = ExitStack()
        xt = sb("xt", [P, NT, D], F32, scope_x)
        xjunk = sb("xjunk", [P, D], F32, scope_x)
        vrows = sb("vrows", [P, 4, P], F32, scope_x)
        xss = sb("xss", [P, NT], F32, scope_x)
        xrs = sb("xrs", [P, NT], F32, scope_x)
        bias_b = sb("bias_b", [P, HEADS], F32, scope_x)
        alog_b = sb("alog_b", [P, HEADS], F32, scope_x)
        dtv = [sb(f"dtv{i}", [P, NT, HEADS], F32, scope_x) for i in range(6)]
        cs_t = sb("cs_t", [HEADS, SEQ], F32, scope_x)
        scope_x.close()

        scope_g = ExitStack()
        bct = sb("bct", [P, 2, SEQ], F32, scope_g)
        xst = sb("xst", [P, GB, SEQ], F32, scope_g)
        th = sb("th", [P, 2, 2, SEQ], F32, scope_g)
        csb = sb("csb", [P, 2, HPG, Q], F32, scope_g)
        seg = sb("seg", [P, HPG, Q], F32, scope_g)
        xdt = sb("xdt", [P, HPG, HD], F32, scope_g)
        xw = sb("xw", [P, HPG, HD], F32, scope_g)
        ytok = sb("ytok", [P, GB, P], F32, scope_g)
        state = sb("state", [P, HPG, HD], F32, scope_g)
        btok = sb("btok", [P, P], F32, scope_g)
        cbm = sb("cbm", [P, P], F32, scope_g)
        ytmp = sb("ytmp", [P, SEQ], F32, scope_g)
        gprep = sb("gprep", [P, 3 * NT, HPG], F32, scope_g)
        gconv = sb("gconv", [P, TAPS + 1, 6], F32, scope_g)
        gd = sb("gd", [P, GB], F32, scope_g)
        wa = sb("wa", [P, 2 * HPG], F32, scope_g)
        we = sb("we", [P, 2 * HPG], F32, scope_g)
        gz = sb("gz", [P, GB, SEQ], F32, scope_g)
        yt = sb("yt", [P, GB, SEQ], F32, scope_g)
        scope_g.close()
        scope1.close()

        gateb = sb("gateb", [P, D])
        rope_t = sb("rope_t", [P, 2, NT, ROPE // 2])
        lconst = sb("lconst", [P, 8, RNN_BLOCKS])

        scope_o = ExitStack()
        y_parts = [[sb(f"y_{what}0", [P, Y_HALF, SEQ], F32R, scope_o) for what in ("hi", "lo")]]
        y_in = sb("y_in", [P, 2, 2, SEQ], F32, scope_o)
        y_parts += [[sb(f"y_{what}1", [P, Y_HALF, SEQ], F32R, scope_o) for what in ("hi", "lo")]]
        x1p = sb("x1p", [P, NT, TCOL], F32, scope_o)
        scope_o.close()

        def y_block(b, low):
            return y_parts[b // Y_HALF][low][:, b % Y_HALF, :]

        scope2 = ExitStack()
        xr = sb("xr", [P, RNN_BLOCKS, SEQ], F32, scope2)
        ga = sb("ga", [P, RNN_BLOCKS, SEQ], F32, scope2)
        qkvc = sb("qkvc", [P, 2 * LORA_KB, SEQ], F32, scope2)
        scope_f = ExitStack()
        gr = sb("gr", [P, RNN_BLOCKS, SEQ], F32, scope_f)
        h_hi = sb("h_hi", [P, KB, SEQ], F32R, scope_f)
        h_lo = sb("h_lo", [P, KB, SEQ], F32R, scope_f)
        lt = [sb(f"lt{i}", [P, SEQ], F32, scope_f) for i in range(6)]
        wblk = sb("wblk", [P, 2, P], F32, scope_f)
        lc = sb("lc", [P, 8], F32, scope_f)
        scope_f.close()
        scope_a = ExitStack()
        c_hi = sb("c_hi", [P, 2 * LORA_KB, SEQ], F32R, scope_a)
        c_lo = sb("c_lo", [P, 2 * LORA_KB, SEQ], F32R, scope_a)
        q_tok = sb("q_tok", [P, NT, 2, QH], F32, scope_a)
        kv_tok = sb("kv_tok", [P, NT, 2, NOPE + VH], F32, scope_a)
        sqt = sb("sqt", [P, NT, 2, QH], F32, scope_a)
        prob = sb("prob", [P, 2, SEQ], F32, scope_a)
        pt = sb("pt", [P, NT, SEQ], F32, scope_a)
        qt = sb("qt", [P, 2, SEQ], F32, scope_a)
        kt = sb("kt", [P, 2, SEQ], F32, scope_a)
        qpt = sb("qpt", [P, SEQ], F32, scope_a)
        kpt = sb("kpt", [P, SEQ], F32, scope_a)
        vt = sb("vt", [P, NT, 2, VH], F32, scope_a)
        qpe = sb("qpe", [P, NT, 2, ROPE], F32, scope_a)
        rt = [sb(f"rt{i}", [P, NT, 2, ROPE // 2], F32, scope_a) for i in range(4)]
        kr_tok = sb("kr_tok", [P, NT, ROPE], F32, scope_a)
        gain_b = sb("gain_b", [P, 2 * ROPE], F32, scope_a)
        gain_c = sb("gain_c", [P, 2], F32, scope_a)
        maskn = sb("maskn", [P, P], F32, scope_a)
        gth = sb("gth", [P, 2, SEQ], F32, scope_a)
        latent_sq = (pt[:], kv_tok[:].rearrange("p t h n -> p t (h n)"))
        nrm = sb("nrm", [P, 3, NT, 2], F32, scope_a)
        sm = sb("sm", [P, 4, 8], F32, scope_a)
        scope_a.close()
        scope_z = ExitStack()
        y2_hi = sb("y2_hi", [P, KB, SEQ], F32R, scope_z)
        y2_lo = sb("y2_lo", [P, KB, SEQ], F32R, scope_z)
        xo = sb("xo", [P, NT, TCOL], F32, scope_z)
        oo = sb("oo", [P, NT, TCOL], F32, scope_z)
        scope_z.close()
        scope2.close()

        scope_e = ExitStack()
        x1t = sb("x1t", [P, NT, D], F32, scope_e)
        xh = sb("xh", [P, NT, D], F32, scope_e)
        scope_e.close()
        scope_e2 = ExitStack()
        sb("under_ada", [P, 2 * NT * D + 2 * KB * SEQ - ADA], F32, scope_e2)
        ada_in = sb("ada_in", [P, ADA], F32, scope_e2)
        h_mod = sb("h_mod", [P, 4, SEQ], F32, scope_e2)
        sb("under_x1p", [P, NT * TCOL], F32, scope_e2)
        rt_i = sb("rt_i", [P, NT], I32, scope_e2)
        rt_f = sb("rt_f", [P, NT], F32, scope_e2)
        invf = sb("invf", [P, ROPE // 2], F32, scope_e2)
        ra = [ysq[:, i * P:(i + 1) * P].rearrange("p (t n) -> p t n", t=NT) for i in range(3)]
        le = [ysq[:, 3 * P + i * RNN_BLOCKS:3 * P + (i + 1) * RNN_BLOCKS] for i in range(4)]
        scope_e2.close()

        consts_made = sem("consts_made")
        rows_zeroed = sem("rows_zeroed")
        small_landed = sem("small_landed")
        x_landed = [sem(f"x_landed{t}") for t in range(NT)]
        xss_ready = sem("xss_ready")
        x_std_ready = sem("x_std_ready")
        x_normed = sem("x_normed")
        cols_turned = sem("cols_turned")
        cols_ready = sem("cols_ready")
        c_tanh_ready = sem("c_tanh_ready")
        x_turned = sem("x_turned")
        hn_hi_ready = sem("hn_hi_ready")
        hn_lo_ready = sem("hn_lo_ready")
        raw_landed = [sem(f"raw_landed{s}") for s in range(RING)]
        hi_ready = sem("hi_ready")
        lo_ready = sem("lo_ready")
        unit_used = sem("unit_used")
        dve_step = sem("dve_step")
        pool_step = sem("pool_step")
        dt_taken = sem("dt_taken")
        dt_turned = sem("dt_turned")
        dt_abs_ready = sem("dt_abs_ready")
        dt_exp_ready = sem("dt_exp_ready")
        adt_ready = sem("adt_ready")
        cs_summed = sem("cs_summed")
        cs_ready = sem("cs_ready")
        cs_turned = sem("cs_turned")
        cs_t_ready = sem("cs_t_ready")
        cs_stored = sem("cs_stored")
        ecs_ready = sem("ecs_ready")
        pads_zeroed = sem("pads_zeroed")
        x_acc_freed = sem("x_acc_freed")
        z_half_done = sem("z_half_done")
        z_acc_freed = sem("z_acc_freed")
        z_tanh_ready = sem("z_tanh_ready")
        conv_summed = sem("conv_summed")
        conv_tanh_ready = sem("conv_tanh_ready")
        conv_done = sem("conv_done")
        chunk_in = sem("chunk_in")
        csb_landed = [sem(f"csb_landed{s}") for s in range(2)]
        seg_ready = sem("seg_ready")
        decay_ready = sem("decay_ready")
        wa_ready = sem("wa_ready")
        we_ready = sem("we_ready")
        chunk_mid = sem("chunk_mid")
        chunk_summed = sem("chunk_summed")
        state_read = sem("state_read")
        ytok_ready = sem("ytok_ready")
        ytok_turned = sem("ytok_turned")
        yt_ready = sem("yt_ready")
        yt_free = sem("yt_free")
        y_stored = sem("y_stored")
        gated = sem("gated")
        ada_landed = [sem(f"ada_landed{s}") for s in range(2)]
        ada_used = sem("ada_used")
        ada_stored = sem("ada_stored")

        y_squared = sem("y_squared")
        ysq_summed = sem("ysq_summed")
        ysq_mean_ready = sem("ysq_mean_ready")
        ysq_std_ready = sem("ysq_std_ready")
        y_in_landed = [sem(f"y_in_landed{i}") for i in range(2)]
        y_hi_ready = sem("y_hi_ready")
        y_lo_ready = sem("y_lo_ready")
        x_in_landed = sem("x_in_landed")
        d_bank_done = sem("d_bank_done")
        d_bank_freed = sem("d_bank_freed")
        x1_free = sem("x1_free")
        x1_added = sem("x1_added")
        x1_squared = sem("x1_squared")
        x1g_ready = sem("x1g_ready")
        x1g_squared = sem("x1g_squared")
        x1_summed = sem("x1_summed")
        x1_mean_ready = sem("x1_mean_ready")
        x1_std_ready = sem("x1_std_ready")
        x1t_landed = sem("x1t_landed")
        ada_in_landed = sem("ada_in_landed")
        gateb_landed = sem("gateb_landed")
        rope_in_landed = sem("rope_in_landed")
        ada_reduced = sem("ada_reduced")
        ada_cols_ready = sem("ada_cols_ready")
        xh_ready = sem("xh_ready")
        h_turned = sem("h_turned")
        h_mod_ready = sem("h_mod_ready")
        h_hi_ready = sem("h_hi_ready")
        h_lo_ready = sem("h_lo_ready")
        lru_abs_ready = sem("lru_abs_ready")
        lru_exp_ready = sem("lru_exp_ready")
        angles_ready = sem("angles_ready")
        rope_ready = sem("rope_ready")
        f_bank_done = sem("f_bank_done")
        f_bank_freed = sem("f_bank_freed")
        wblk_landed = sem("wblk_landed")
        xc_ready = sem("xc_ready")
        gates_summed = sem("gates_summed")
        gates_free = sem("gates_free")
        gates_ready = sem("gates_ready")
        logs_ready = sem("logs_ready")
        decays_ready = sem("decays_ready")
        var_ready = sem("var_ready")
        dev_ready = sem("dev_ready")
        rnn_done = sem("rnn_done")
        gains_landed = sem("gains_landed")
        mask_ready = sem("mask_ready")
        kr_taken = sem("kr_taken")
        kr_turned = sem("kr_turned")
        kr_ready = sem("kr_ready")
        kr_squared = sem("kr_squared")
        latent_squared = sem("latent_squared")
        latent_added = sem("latent_added")
        latent_summed = sem("latent_summed")
        latent_var_ready = sem("latent_var_ready")
        latent_std_ready = sem("latent_std_ready")
        latent_rms_ready = sem("latent_rms_ready")
        c_hi_ready = sem("c_hi_ready")
        c_lo_ready = sem("c_lo_ready")
        kpe_ready = sem("kpe_ready")
        kpe_turned = sem("kpe_turned")
        kpt_ready = sem("kpt_ready")
        q_read = sem("q_read")
        kv_read = sem("kv_read")
        sq_ready = sem("sq_ready")
        q_reduced = sem("q_reduced")
        nrm_ready = sem("nrm_ready")
        nrm_std_ready = sem("nrm_std_ready")
        nope_normed = sem("nope_normed")
        rope_turned = sem("rope_turned")
        pair_turned = sem("pair_turned")
        pe_turned = sem("pe_turned")
        qk_ready = sem("qk_ready")
        v_ready = sem("v_ready")
        scored = sem("scored")
        max_ready = sem("max_ready")
        exp_ready = sem("exp_ready")
        prob_ready = sem("prob_ready")
        prob_turned = sem("prob_turned")
        pt_ready = sem("pt_ready")
        head_summed = sem("head_summed")
        head_read = sem("head_read")
        ga_tanh_ready = sem("ga_tanh_ready")
        y2_hi_ready = sem("y2_hi_ready")
        y2_lo_ready = sem("y2_lo_ready")
        xo_landed = sem("xo_landed")
        xo_free = sem("xo_free")
        z_bank_done = sem("z_bank_done")
        z_bank_freed = sem("z_bank_freed")
        o_ready = sem("o_ready")
        out_stored = sem("out_stored")

        x_tok = x[0].rearrange("(t p) n -> p t n", p=P)
        x1_tok = x1_rows.rearrange("(t p) n -> p t n", p=P)
        out_tok = out[0].rearrange("(t p) n -> p t n", p=P)
        w_in_rows = ssm_w_in[0].rearrange("(k p) n -> p k n", p=P)
        w_ada_rows = w_ada_2[0].rearrange("(k p) n -> p k n", p=P)
        SMALL = 19

        def unit_ap(ring, slot, cols_=UCOL):
            return ring[:, slot, 0:UKT * cols_].rearrange("p (k n) -> p k n", k=UKT)

        block = ctx.enter_context(nc.Block())

        def walk(eng, body, steps=None, per=0):
            body(0, False, True)
            with eng.Fori(1, GROUPS) as g:
                if steps:
                    steps.enter(g, per)
                body(g, True, True)
            if steps:
                steps.leave(GROUPS - 1, per)
            body(GROUPS, True, False)

        @block.sync
        def _(sp):
            sp.wait_ge(rows_zeroed, 1)

            def rows(start, ap):
                t, r = divmod(start, P)
                n = ap.shape[0]
                sp.dma_start(vrows[r:r + n, t, :], ap).then_inc(small_landed, 16)

            for k in range(TAPS):
                rows(ROW_CONV_W[k], ssm_conv_w[0, k].rearrange("(b c) -> b c", c=P))
            rows(ROW_LN, ln_g[0].rearrange("(b c) -> b c", c=P))
            for t in range(NT):
                sp.dma_start(xt[:, t, :], x[0, t * P:(t + 1) * P, :]).then_inc(x_landed[t], 16)
            rows(ROW_QA, q_a_norm_2[0].rearrange("(b c) -> b c", c=P))
            rows(ROW_KVA, kv_a_norm_2[0].rearrange("(b c) -> b c", c=P))
            rows(ROW_NORM, ssm_norm_g[0].rearrange("(b c) -> b c", c=P))
            rows(ROW_CONV_B, ssm_conv_b[0].rearrange("(b c) -> b c", c=P))
            rows(ROW_SHIFT_B, b_ada_2[0, 0:2 * D].rearrange("(b c) -> b c", c=P))
            rows(ROW_CONV2_W, conv_w_2[0].rearrange("k (b c) -> (k b) c", c=P))
            rows(ROW_CONV2_B, conv_b_2[0].rearrange("(b c) -> b c", c=P))
            rows(ROW_LRU, lru_lambda_2[0].rearrange("(b c) -> b c", c=P))
            rows(ROW_RG_A, b_rg_a_2[0].rearrange("(b c) -> b c", c=P))
            rows(ROW_RG_X, b_rg_x_2[0].rearrange("(b c) -> b c", c=P))
            rows(ROW_C, c_2[0].rearrange("(b c) -> b c", c=P))
            sp.dma_start(bias_b[:], ssm_dt_bias[0].partition_broadcast(P)).then_inc(small_landed, 16)
            sp.dma_start(alog_b[:], ssm_a_log[0].partition_broadcast(P)).then_inc(small_landed, 16)
            sp.dma_start(d2[:], ssm_d[0].rearrange("(b h) -> h b", h=2),
                         allow_slow_non_contiguous=True).then_inc(small_landed, 16)

            for u in range(DT_UNITS):
                sp.dma_start(unit_ap(w_raw, u, HEADS), w_in_rows[:, u * UKT:(u + 1) * UKT,
                             D_INNER + CONV_DIM:]).then_inc(raw_landed[u], 16)

            def body(g, prev, cur):
                if not cur:
                    return
                for u in range(GU):
                    p, kq = divmod(u, UPP)
                    s = u % RING
                    loads = []
                    dst = unit_ap(w_raw, s)
                    src = w_in_rows[:, kq * UKT:(kq + 1) * UKT, :]
                    if p == 0:
                        loads = [(dst[:, :, h * P:(h + 1) * P], src,
                                  g * P + 2 * D_INNER + h * GROUPS * P, P) for h in range(2)]
                    elif p == 3:
                        loads = [(dst[:, k:k + 2, :], src[:, k:k + 2, :], g * GB * P, UCOL) for k in (2, 0)]
                    else:
                        at = (D_INNER if p < 3 else 0) + (p - 1) % 2 * UCOL
                        loads = [(dst, src, g * GB * P + at, UCOL)]
                    wait = sp.snap(g * GU + u + DT_UNITS - RING + 1) if prev else u + DT_UNITS - RING + 1
                    loads = [(to, rows_, sp.snap(at) if prev else at, n) for to, rows_, at, n in loads]
                    sp.wait_ge(lo_ready, wait)
                    for to, rows_, at, n in loads:
                        sp.dma_start(to, rows_[:, :, bass.ds(at, n)]).then_inc(raw_landed[s], 16)
                    k = u - AHEAD
                    if 0 <= k < KB:
                        ada_at = sp.snap(g * ADA_COLS) if prev else 0
                        used = sp.snap(g * KB + k - 1) if prev else k - 1
                        if k >= 2 or prev:
                            sp.wait_ge(ada_used, used)
                        sp.dma_start(ada_raw[:, k % 2, :],
                                     w_ada_rows[:, k, bass.ds(ada_at, ADA_COLS)]
                                     ).then_inc(ada_landed[k % 2], 16)

            walk(sp, body)

            def load(unit, slot, view, src):
                sp.wait_ge(lo_ready, unit)
                sp.dma_start(view, src).then_inc(raw_landed[slot], 16)

            def tok_view(ring, slot, n=TCOL):
                return ring[:, slot, 0:TKT * n].rearrange("p (k n) -> p k n", k=TKT)

            w_rows = ssm_w_out[0].rearrange("(k p) n -> p k n", p=P)

            def out1_units(i, us):
                fixed = isinstance(i, int)
                at = i * TCOL if fixed else sp.snap(i * TCOL)
                for u in us:
                    if fixed and u < RING:
                        sp.wait_ge(lo_ready, U_OUT1 + u - RING + 1)
                        for k in range(TKT):
                            sp.dma_start(tok_view(w_raw, u)[:, k, :], w_rows[:, u * TKT + k, 0:TCOL]
                                         ).then_inc(raw_landed[u], 16)
                        continue
                    n = i * OUT1_UPP + (U_OUT1 + u - RING + 1)
                    load(n if fixed else sp.snap(n), u % RING, tok_view(w_raw, u % RING),
                         w_rows[:, u * TKT:(u + 1) * TKT, bass.ds(at, TCOL)])

            def load_y(j):
                if j >= 2:
                    sp.wait_ge(y_lo_ready, 2 * (j - 1))
                sp.dma_start(y_in[:, j % 2, :, :], y_rows[j * 2 * P:(j + 1) * 2 * P, :].rearrange(
                    "(b p) n -> p b n", p=P)).then_inc(y_in_landed[j % 2], 16)

            def load_x1(i):
                fixed = isinstance(i, int)
                at = i * TCOL if fixed else sp.snap(i * TCOL)
                n = i * 16 + 16
                sp.wait_ge(x1_free, n if fixed else sp.snap(n))
                if not fixed:
                    sp.wait_ge(x1_summed, i)
                sp.dma_start(x1p[:], x_tok[:, :, bass.ds(at, TCOL)]).then_inc(x_in_landed, 16)

            out1_units(0, range(RING))
            sp.wait_ge(conv_summed, 3 * GROUPS)
            sp.wait_ge(yt_free, GROUPS)
            for j in range(Y_HALF // 2):
                load_y(j)
                out1_units(0, (j + RING,))
            for j in range(Y_HALF // 2, Y_HALF):
                if j == Y_LAST:
                    sp.wait_ge(y_stored, GROUPS * 16)
                load_y(j)
                if j + RING < OUT1_UPP:
                    out1_units(0, (j + RING,))
            sp.wait_ge(yt_free, GROUPS + 1)
            sp.sem_inc(x1_free, 16)
            sp.dma_start(gateb[:], final_g.partition_broadcast(P)).then_inc(gateb_landed, 16)
            load_x1(0)
            with sp.Fori(1, OUT_PANELS) as i:
                out1_units(i, range(OUT1_UPP // 2))
                load_x1(i)
                out1_units(i, range(OUT1_UPP // 2, OUT1_UPP))

            w2_rows = w_in_2[0].rearrange("(k p) n -> p k n", p=P)

            def load_panel(i, unit, col):
                at = col if isinstance(col, int) else sp.snap(col)
                for u in range(UPP):
                    n = unit + u - RING + 1
                    load(n if isinstance(n, int) else sp.snap(n), u % RING, unit_ap(w_raw, u % RING),
                         w2_rows[:, u * UKT:(u + 1) * UKT, bass.ds(at, UCOL)])

            load_panel(0, U_RNN, 0)
            sp.wait_ge(unit_used, U_RNN - OUT1_UPP // 2)
            sp.wait_ge(x1_free, 16 * OUT_PANELS)
            for t in range(NT):
                sp.dma_start(x1t[:, t, 0:D - TCOL], x1_rows[t * P:(t + 1) * P, 0:D - TCOL]
                             ).then_inc(x1t_landed, 16)
            sp.wait_ge(unit_used, U_RNN - 2)
            sp.wait_ge(ada_stored, 16 * GROUPS)
            for k in range(3):
                sp.dma_start(ada_in[:, k * D:(k + 1) * D], ada_part[:, k * D:(k + 1) * D]
                             ).then_inc(ada_in_landed, 16)
            sp.dma_start(rt_i[:], positions_2[0].rearrange("(t p) -> p t", p=P),
                         allow_slow_non_contiguous=True).then_inc(rope_in_landed, 16)
            sp.dma_start(invf[:], inv_freq.partition_broadcast(P)).then_inc(rope_in_landed, 16)
            sp.wait_ge(x1g_ready, NT * OUT_PANELS)
            sp.dma_start(gateb[:], b_ada_2[0, 2 * D:].partition_broadcast(P)).then_inc(gateb_landed, 16)
            with sp.Fori(1, RNN_PANELS) as i:
                load_panel(i, i * UPP + U_RNN, i * UCOL)
            with sp.Fori(0, QKV_PANELS) as i:
                load_panel(i, i * UPP + U_QKV, i * UCOL + COL_QKV)
            with sp.Fori(0, GA_PANELS) as i:
                load_panel(i, i * UPP + U_GA, i * UCOL + COL_GA)
            for u in range(DT_UNITS):
                load(U_KR + u - RING + 1, u, unit_ap(w_raw, u, ROPE),
                     w2_rows[:, u * UKT:(u + 1) * UKT, COL_KR:COL_KR + ROPE])

            uq_rows = w_uq_2[0].rearrange("(k p) n -> p k n", p=P)
            ukv_rows = w_ukv_2[0].rearrange("(k p) n -> p k n", p=P)
            with sp.Fori(0, PAIRS) as i:
                for u in range(4):
                    cols_, rows_ = (2 * QH, uq_rows) if u < 2 else (TCOL, ukv_rows)
                    n = sp.snap(i * 4 + (U_PAIR + u - RING + 1))
                    at = sp.snap(i * cols_)
                    load(n, u, tok_view(w_raw, u, cols_),
                         rows_[:, u % 2 * TKT:(u % 2 + 1) * TKT, bass.ds(at, cols_)])

            w_rows = w_out_2[0].rearrange("(k p) n -> p k n", p=P)

            def out2_units(i, us):
                fixed = isinstance(i, int)
                at = i * TCOL if fixed else sp.snap(i * TCOL)
                for u in us:
                    n = i * OUT2_UPP + (U_OUT2 + u - RING + 1)
                    load(n if fixed else sp.snap(n), u % RING, tok_view(w_raw, u % RING),
                         w_rows[:, u * TKT:(u + 1) * TKT, bass.ds(at, TCOL)])

            def out2_rest(i):
                fixed = isinstance(i, int)
                at = i * TCOL if fixed else sp.snap(i * TCOL)
                n = i + 1 if fixed else sp.snap(i + 1)
                sp.wait_ge(xo_free, n)
                sp.dma_start(xo[:], x1_tok[:, :, bass.ds(at, TCOL)]).then_inc(xo_landed, 16)
                out2_units(i, range(RING, OUT2_UPP))

            out2_units(0, range(RING))
            sp.wait_ge(unit_used, U_OUT2)
            sp.wait_ge(head_read, ATT_HEADS)
            sp.sem_inc(xo_free, 1)
            with sp.Fori(0, OUT_PANELS - 1) as i:
                out2_rest(i)
                out2_units(i + 1, range(RING))
            out2_rest(OUT_PANELS - 1)

        @block.gpsimd
        def _(pool):
            st = Steps(pool, pool_step)
            nc.gpsimd.memset(vrows[:], 0.0).then_inc(rows_zeroed, 1)
            st.done(nc.gpsimd.memset(ident[:], 0.0))
            st.done(nc.gpsimd.memset(ones[:], 1.0))
            st.wait()
            st.done(nc.gpsimd.affine_select(out=ident[:], in_=ident[:], compare_op=ALU.not_equal, fill=1.0,
                                            base=0, pattern=[[-1, P]], channel_multiplier=1))
            st.done(nc.gpsimd.affine_select(out=tri[:], in_=ones[:], compare_op=ALU.is_ge, fill=0.0,
                                            base=0, pattern=[[1, P]], channel_multiplier=-1))
            st.done(nc.gpsimd.affine_select(out=halves[:], in_=ones[0:2, :], compare_op=ALU.is_ge, fill=0.0,
                                            base=0, pattern=[[1, P]], channel_multiplier=-HD))
            st.wait()
            st.done(nc.gpsimd.affine_select(out=halves[:], in_=halves[:], compare_op=ALU.is_ge, fill=0.0,
                                            base=HD - 1, pattern=[[-1, P]], channel_multiplier=HD))
            st.wait()
            st.done(nc.gpsimd.memset(ysq[:], 0.0))
            st.wait()
            pool.sem_inc(consts_made, 1)
            nc.gpsimd.memset(xraw[:], 0.0).then_inc(pads_zeroed, 1)

            pool.wait_ge(cs_t_ready, 1)
            pool.dma_start(cs_rows, cs_t[:]).then_inc(cs_stored, 16)
            pool.wait_ge(cs_stored, 16)

            def load_cs(g, c):
                src = cs_rows[bass.ds(g * HPG, HPG), c * Q:(c + 1) * Q]
                pool.dma_start(csb[:, c % 2, :, :], src.partition_broadcast(P)).then_inc(csb_landed[c % 2], 16)

            load_cs(0, 0)
            load_cs(0, 1)
            pool.sem_inc(yt_free, 1)

            def body(g, prev, cur):
                gp = g - 1
                if prev:
                    for c in (2, 3):
                        pool.wait_ge(seg_ready, gp * NQ + c - 1)
                        load_cs(gp, c)
                    if cur:
                        for c in (0, 1):
                            pool.wait_ge(seg_ready, gp * NQ + c + 3)
                            load_cs(g, c)
                if cur:
                    pool.wait_ge(ada_used, g * KB + KB)
                    pool.dma_start(columns(ada_part, g * ADA_COLS, ADA_COLS), ada_acc[:]).then_inc(ada_stored, 16)
                if prev:
                    if cur:
                        pool.wait_ge(yt_ready, gp * NQ + NQ)
                        pool.wait_ge(z_acc_freed, 3 * g)
                        nc.gpsimd.tensor_tensor(yt[:], yt[:], gz[:], ALU.mult).then_inc(gated, 1)
                    pool.wait_ge(gated, g)
                    pool.dma_start(y_rows[bass.ds(gp * GB * P, GB * P), :].rearrange("(b p) n -> p b n", p=P),
                                   yt[:]).then_inc(y_stored, 16)
                    if not cur:
                        pool.wait_ge(ysq_summed, 1)
                    for b in range(GB if cur else 0):
                        st.done(nc.gpsimd.tensor_tensor(ytmp[:], yt[:, b, :], yt[:, b, :], ALU.mult))
                        st.wait()
                        st.done(nc.gpsimd.tensor_tensor(ysq[:], ysq[:], ytmp[:], ALU.add))
                        st.wait()
                    pool.wait_ge(y_stored, g * 16)
                    pool.sem_inc(yt_free, 1)

            walk(pool, body, st, 2 * GB)
            pool.wait_ge(h_lo_ready, KB)
            pool.wait_ge(x1_free, 16 * (OUT_PANELS + 1))
            st.done(nc.gpsimd.memset(wblk[:], 0.0))
            st.wait()
            pool.sem_inc(gates_free, 1)
            with pool.Fori(0, RNN_BLOCKS) as j:
                pool.wait_ge(gates_free, j + 1)
                for kind, w in enumerate((w_rg_a_2, w_rg_x_2)):
                    for h in range(2):
                        pool.dma_start(wblk[h * 64:(h + 1) * 64, kind, h * 64:(h + 1) * 64],
                                       w[0, bass.ds(j * 2 + h, 1), :, :].rearrange("o i j -> (o i) j")
                                       ).then_inc(wblk_landed, 16)

            pool.wait_ge(unit_used, U_PAIR)
            pool.wait_ge(rnn_done, RNN_BLOCKS)
            for k, gain in enumerate((q_norm_nope_2, k_norm_nope_2)):
                pool.dma_start(gain_c[:, k:k + 1], gain[0].rearrange("(c o) -> c o", o=1)).then_inc(gains_landed, 16)
            for k, gain in enumerate((q_norm_rope_2, k_norm_rope_2)):
                pool.dma_start(gain_b[:, k * ROPE:(k + 1) * ROPE], gain[0].partition_broadcast(P)
                               ).then_inc(gains_landed, 16)
            st.done(nc.gpsimd.memset(maskn[:], 0.0))
            st.wait()
            nc.gpsimd.affine_select(out=maskn[:], in_=maskn[:], compare_op=ALU.is_ge, fill=NEG, base=0,
                                    pattern=[[-1, P]], channel_multiplier=1).then_inc(mask_ready, 1)

            pool.wait_ge(gains_landed, 64)
            pool.wait_ge(kpe_turned, 1)
            with pool.Fori(0, PAIRS) as g:
                st.enter(g + 1, 6)
                pool.wait_ge(nrm_std_ready, g + 1)
                pool.wait_ge(nope_normed, g * 2 + 1)
                qr = q_tok[:, :, :, NOPE:].rearrange("p t h n -> p (t h) n")
                st.done(nc.gpsimd.tensor_tensor(
                    qr, qr, nrm[:, 1, :, :].rearrange("p t h -> p (t h)").unsqueeze(2).broadcast_to(
                        [P, 2 * NT, ROPE]), ALU.mult))
                st.wait()
                st.done(nc.gpsimd.tensor_tensor(
                    qr, qr, gain_b[:, 0:ROPE].unsqueeze(1).broadcast_to([P, 2 * NT, ROPE]), ALU.mult))
                st.wait()
                cos, sin = (rope_t[:, k, :, :].unsqueeze(2).broadcast_to([P, NT, 2, ROPE // 2]) for k in range(2))
                lo_, hi_ = (q_tok[:, :, :, NOPE + k * ROPE // 2:NOPE + (k + 1) * ROPE // 2] for k in range(2))
                for a, (h_, c_) in zip(rt, ((lo_, cos), (hi_, sin), (lo_, sin), (hi_, cos))):
                    st.done(nc.gpsimd.tensor_tensor(a[:], h_, c_, ALU.mult))
                st.wait()
                pool.wait_ge(pe_turned, g + 1)
                nc.gpsimd.tensor_tensor(qpe[:, :, :, 0:ROPE // 2], rt[0][:], rt[1][:], ALU.subtract)
                nc.gpsimd.tensor_tensor(qpe[:, :, :, ROPE // 2:], rt[2][:], rt[3][:], ALU.add
                                        ).then_inc(rope_turned, 1)
            st.leave(PAIRS, 6)

        @block.scalar
        def _(act):
            for t in range(NT):
                act.wait_ge(x_landed[t], 16)
                if t:
                    act.wait_ge(xss_ready, t)
                nc.scalar.activation(xjunk[:], xt[:, t, :], ACT.Square, accum_out=xss[:, t:t + 1]
                                     ).then_inc(xss_ready, 1)
            act.wait_ge(dve_step, 1)
            nc.scalar.activation(xrs[:], xrs[:], ACT.Sqrt).then_inc(x_std_ready, 1)
            act.wait_ge(cols_ready, 1)
            nc.scalar.activation(th_c[:], cols[:, ROW_C:ROW_C + KB], ACT.Tanh, scale=0.5
                                 ).then_inc(c_tanh_ready, 1)

            def hi(g, u):
                s = u % RING
                before = g * GU + u + DT_UNITS if g is not None else u
                if g is None:
                    act.wait_ge(raw_landed[s], 16)
                    n = UKT * HEADS
                else:
                    ahead = u // GU
                    n = u % GU
                    act.wait_ge(raw_landed[s], (g * 7 + 7 * ahead + 1 + 2 + n // RING + n // (3 * UPP)) * 16)
                    act.wait_ge(unit_used, before - RING + 1)
                    n = UNIT
                nc.scalar.activation(w_hi[:, s, 0:n], w_raw[:, s, 0:n], ACT.Copy).then_inc(hi_ready, 1)

            for u in range(DT_UNITS):
                hi(None, u)
            for kb in range(KB):
                act.wait_ge(x_turned, kb + 1)
                nc.scalar.activation(hn_hi[:, kb, :], ps[:, kb % 8, :], ACT.Copy,
                                     scale=cols[:, ROW_LN + kb:ROW_LN + kb + 1]).then_inc(hn_hi_ready, 1)
            act.wait_ge(pads_zeroed, 1)

            def dt_exp():
                act.wait_ge(dt_abs_ready, 1)
                nc.scalar.activation(dtv[1][:], dtv[1][:], ACT.Exp, scale=-1.0)
                nc.scalar.activation(alog_b[:], alog_b[:], ACT.Exp).then_inc(dt_exp_ready, 1)

            def cs_exp():
                act.wait_ge(cs_ready, 1)
                nc.scalar.activation(prep[:, 2 * NT:3 * NT, :], prep[:, NT:2 * NT, :], ACT.Exp
                                     ).then_inc(ecs_ready, 1)

            def take_raw(g, j):
                act.wait_ge(unit_used, g * GU + (j + 1) * UPP + DT_UNITS)
                if not isinstance(g, int) or g:
                    act.wait_ge(conv_summed, g * 3)
                b = 2 * (j % 2)
                nc.scalar.activation(xraw[:, 2 * j:2 * j + 2, 3:], ps[:, b:b + 2, :], ACT.Copy
                                     ).then_inc(x_acc_freed, 1)

            def conv_tanh(g, j):
                act.wait_ge(conv_summed, g * 3 + j + 1)
                if j == 0 and (not isinstance(g, int) or g):
                    act.wait_ge(z_acc_freed, g * 3)
                if j == 2:
                    act.wait_ge(conv_done, g * 3 + 1)
                src = bct[:, :, :] if j == 0 else xst[:, 2 * j - 2:2 * j, :]
                nc.scalar.activation(th[:, j % 2, :, :], src, ACT.Tanh).then_inc(conv_tanh_ready, 1)

            def z_tanh(g, j):
                act.wait_ge(conv_done, g * 3 + 2 + j)
                if j == 0:
                    act.wait_ge(unit_used, g * GU + (4 + j) * UPP + DT_UNITS)
                    nc.scalar.activation(th[:, 1, :, :], ps[:, 2:4, :], ACT.Tanh, scale=0.5).then_inc(z_tanh_ready, 1)
                    return
                for b in range(2):
                    if b:
                        act.wait_ge(unit_used, g * GU + (4 + j) * UPP + DT_UNITS)
                    else:
                        act.wait_ge(z_half_done, g + 1)
                    nc.scalar.activation(th[:, 0, b, :], ps[:, b, :], ACT.Tanh, scale=0.5).then_inc(z_tanh_ready, 1)

            def chunk_exps(gp, c):
                act.wait_ge(wa_ready, gp * NQ + c + 1)
                nc.scalar.activation(we[:], wa[:], ACT.Exp).then_inc(we_ready, 1)
                act.wait_ge(seg_ready, gp * NQ + c + 1)
                nc.scalar.activation(seg[:], seg[:], ACT.Exp).then_inc(decay_ready, 1)

            def body(g, prev, cur):
                gp = g - 1
                for u in range(GU):
                    if cur:
                        hi(g, u + AHEAD)
                    if not prev and u == 0:
                        dt_exp()
                    if not prev and u == 3:
                        cs_exp()
                    if prev and u == 0:
                        z_tanh(gp, 1)
                    if prev and u in (3, 6, 9, 12):
                        chunk_exps(gp, u // 3 - 1)
                    if not cur and u in LAST_SCAN:
                        j = LAST_SCAN.index(u)
                        y_hi(j)
                        out1_hi(0, j + AHEAD)
                    if cur and u in (5, 10, 14):
                        take_raw(g, {5: 0, 10: 1, 14: 2}[u])
                    if cur and u in (16, 17, 18):
                        conv_tanh(g, u - 16)
                    if cur and u == 19:
                        z_tanh(g, 0)

            def split_hi(unit, slot, landed):
                act.wait_ge(raw_landed[slot], landed * 16)
                act.wait_ge(unit_used, unit - RING + 1)
                nc.scalar.activation(w_hi[:, slot, :], w_raw[:, slot, :], ACT.Copy).then_inc(hi_ready, 1)

            def out1_hi(i, u):
                split_hi(i * OUT1_UPP + (U_OUT1 + u), u % RING,
                         i * (OUT1_UPP // RING) + (L_OUT1 + 2 + u // RING))

            def y_hi(j):
                if j == 0:
                    act.wait_ge(unit_used, U_OUT1)
                act.wait_ge(y_in_landed[j % 2], 16 * (j // 2 + 1))
                for b in (2 * j, 2 * j + 1):
                    nc.scalar.activation(y_block(b, 0), y_in[:, j % 2, b % 2, :], ACT.Copy,
                                         scale=cols[:, ROW_NORM + b:ROW_NORM + b + 1]).then_inc(y_hi_ready, 1)

            for u in range(AHEAD):
                hi(0, u)
            walk(act, body)

            act.wait_ge(yt_ready, GROUPS * NQ)
            for j in range(Y_HALF // 2, Y_HALF):
                if j == Y_HALF // 2 + 1:
                    act.wait_ge(gated, GROUPS)
                    nc.scalar.activation(gz[:], yt[:], ACT.Square).then_inc(y_squared, 1)
                if j == Y_LAST - 1:
                    act.wait_ge(yt_free, GROUPS + 1)
                y_hi(j)
                out1_hi(*divmod(j + AHEAD, OUT1_UPP))
            act.wait_ge(ysq_mean_ready, 1)
            nc.scalar.activation(yrs, yrs, ACT.Sqrt).then_inc(ysq_std_ready, 1)
            def x1_squares(i):
                for t in range(NT):
                    act.wait_ge(x1_added, i * NT + (t + 1))
                    if t == 0 and not isinstance(i, int):
                        act.wait_ge(x1_summed, i)
                    if t:
                        act.wait_ge(x1_squared, i * NT + t)
                    nc.scalar.activation(ysq[:], x1p[:, t, :], ACT.Square, accum_out=x1_part[:, 0, t:t + 1]
                                         ).then_inc(x1_squared, 1)
                act.wait_ge(x1g_ready, i * NT + NT)
                act.dma_start(x1_tok[:, :, bass.ds(i * TCOL, TCOL)], x1p[:]).then_inc(x1_free, 16)
                for t in range(NT):
                    if t:
                        act.wait_ge(x1g_squared, i * NT + t)
                    nc.scalar.activation(ysq[:], x1p[:, t, :], ACT.Square, accum_out=x1_part[:, 1, t:t + 1]
                                         ).then_inc(x1g_squared, 1)

            for u in range(AHEAD, RING):
                out1_hi(1, u)
            x1_squares(0)
            with act.Fori(1, OUT_PANELS) as i:
                for u in range(RING, OUT1_UPP + RING):
                    out1_hi(i, u)
                x1_squares(i)

            for n, r in ((1, x1rs), (2, x1rr)):
                act.wait_ge(x1_mean_ready, n)
                nc.scalar.activation(r, r, ACT.Sqrt).then_inc(x1_std_ready, 1)
            act.wait_ge(ada_cols_ready, 1)
            for kb in range(KB + 1):
                if kb < KB:
                    act.wait_ge(h_turned, kb + 1)
                    if kb >= 4:
                        act.wait_ge(h_lo_ready, kb - 3)
                    nc.scalar.activation(h_mod[:, kb % 4, :], ps[:, 4 + kb % 4, :], ACT.Identity,
                                         bias=shc[:, kb:kb + 1], scale=scc[:, kb:kb + 1]).then_inc(h_mod_ready, 1)
                if kb:
                    act.wait_ge(h_mod_ready, kb)
                    nc.scalar.activation(h_hi[:, kb - 1, :], h_mod[:, (kb - 1) % 4, :], ACT.Copy
                                         ).then_inc(h_hi_ready, 1)
            act.wait_ge(lru_abs_ready, 1)
            nc.scalar.activation(le[1][:], le[1][:], ACT.Exp, scale=-1.0).then_inc(lru_exp_ready, 1)
            act.wait_ge(angles_ready, 1)
            for k in range(2):
                nc.scalar.activation(rope_t[:, k, :, :], ra[1 - k][:], ACT.Sin).then_inc(rope_ready, 1)

            act.wait_ge(h_turned, KB)

            def panels(part, unit, count, dst, lru=None):
                fb = part * 8
                with act.Fori(0, count) as i:
                    for u in range(UPP):
                        if u == UPP - 1:
                            act.wait_ge(f_bank_done, i + (part * 4 + 1))
                            nc.scalar.activation(dst[:, bass.ds(i * 2, 1), :], ps[:, 0:1, :], ACT.Copy
                                                 ).then_inc(f_bank_freed, 1)
                            act.wait_ge(unit_used, i * UPP + (unit + UPP))
                            nc.scalar.activation(dst[:, bass.ds(i * 2 + 1, 1), :], ps[:, 1:2, :], ACT.Copy
                                                 ).then_inc(f_bank_freed, 1)
                            if lru is not None:
                                act.wait_ge(var_ready, i + (lru + 1))
                                nc.scalar.activation(lt[4][:], lt[4][:], ACT.Sqrt).then_inc(dev_ready, 1)
                        split_hi(i * UPP + (unit + RING + u), u, i + (landed_before(unit) + 2))
                        if lru is None:
                            continue
                        j = i + lru
                        if u == 1:
                            act.wait_ge(gates_summed, i + (lru + 1))
                            nc.scalar.activation(lt[1][:], ps[:, 4, :], ACT.Tanh, bias=lc[:, 5:6], scale=0.5)
                            nc.scalar.activation(lt[2][:], ps[:, 5, :], ACT.Tanh, bias=lc[:, 6:7], scale=0.5
                                                 ).then_inc(gates_free, 1)
                            nc.scalar.activation(lt[3][:], gr[:, bass.ds(j, 1), :].rearrange("p o n -> p (o n)"),
                                                 ACT.Tanh, scale=0.5).then_inc(gates_ready, 1)
                        if u == 2:
                            act.wait_ge(logs_ready, i + (lru + 1))
                            nc.scalar.activation(lt[0][:], lt[1][:], ACT.Exp)
                            nc.scalar.activation(lt[4][:], lt[4][:], ACT.Exp).then_inc(decays_ready, 1)

            panels(0, U_RNN, 4, xr)
            panels(1, U_RNN + 16, 4, gr)
            panels(2, U_QKV, 4, qkvc, 0)
            panels(3, U_GA, 4, ga, 4)

            for u in range(RING):
                split_hi(U_PAIR + u, u, landed_before(U_PAIR) + 1)
            act.wait_ge(rnn_done, RNN_BLOCKS)
            act.wait_ge(unit_used, U_PAIR)
            for b in range(2 * LORA_KB):
                at = ROW_QA + b
                nc.scalar.activation(c_hi[:, b, :], qkvc[:, b, :], ACT.Copy, scale=cols[:, at:at + 1]
                                     ).then_inc(c_hi_ready, 1)
            for part, to in enumerate(latent_sq):
                nc.scalar.activation(to, qkvc[:, part * 4:part * 4 + 4, :], ACT.Square).then_inc(latent_squared, 1)
            act.wait_ge(kr_ready, 1)
            nc.scalar.activation(sqt[:, :, 0, 0:ROPE], kr_tok[:], ACT.Square).then_inc(kr_squared, 1)
            act.wait_ge(latent_var_ready, 1)
            nc.scalar.activation(small[:, 12:24], small[:, 12:24], ACT.Sqrt).then_inc(latent_std_ready, 1)

            act.wait_ge(gains_landed, 64)
            act.wait_ge(latent_rms_ready, 1)

            def pair(g, prev, cur):
                gp = g - 1
                for k in range(8):
                    if cur and k in (1, 3):
                        to, n, r = (q_tok, 2 * QH, rsq) if k == 1 else (kv_tok, TCOL, rskv)
                        act.wait_ge(unit_used, g * 4 + (U_PAIR + k + 1))
                        for t in range(NT):
                            ins = nc.scalar.activation(to[:, t, :, :].rearrange("p h n -> p (h n)"), ps[:, t, 0:n],
                                                       ACT.Copy, scale=r[:, t:t + 1])
                        ins.then_inc(q_read if k == 1 else kv_read, 1)
                    if cur and k < 4:
                        split_hi(g * 4 + (U_PAIR + RING + k), k, g + (landed_before(U_PAIR) + 2))
                    if prev and k == 0:
                        act.wait_ge(v_ready, g)
                        nc.scalar.activation(gth[:], ga[:, bass.ds(gp * 2, 2), :], ACT.Tanh, scale=0.5
                                             ).then_inc(ga_tanh_ready, 1)
                    if prev:
                        n = (k % 4 + 1) * P
                        act.wait_ge(max_ready, gp * 8 + k + 1)
                        if k >= 2:
                            act.wait_ge(prob_turned, gp * 8 + k - 1)
                        nc.scalar.activation(prob[:, k % 2, 0:n], ps[:, 4 + k % 2, 0:n], ACT.Exp,
                                             bias=sm[:, 1, k:k + 1], scale=SM_SCALE,
                                             accum_out=sm[:, 2, k:k + 1]).then_inc(exp_ready, 1)
                    if cur and k == 2:
                        act.wait_ge(q_read, g + 1)
                        nc.scalar.activation(sqt[:], q_tok[:], ACT.Square).then_inc(sq_ready, 1)
                    if cur and k == 4:
                        act.wait_ge(kv_read, g + 1)
                        act.wait_ge(q_reduced, g + 1)
                        nc.scalar.activation(sqt[:, :, :, 0:NOPE], kv_tok[:, :, :, 0:NOPE], ACT.Square
                                             ).then_inc(sq_ready, 1)
                    if cur and k == 5:
                        act.wait_ge(nrm_ready, g + 1)
                        nc.scalar.activation(nrm[:], nrm[:], ACT.Sqrt).then_inc(nrm_std_ready, 1)
                if cur:
                    act.wait_ge(pair_turned, g + 1)
                    nc.scalar.activation(qt[:], ps[:, 0:2, :], ACT.Copy, scale=gain_c[:, 0:1])
                    nc.scalar.activation(kt[:], ps[:, 2:4, :], ACT.Copy, scale=gain_c[:, 1:2]).then_inc(qk_ready, 1)
                    act.wait_ge(pe_turned, g + 2)
                    nc.scalar.activation(qpt[:], ps[:, 4, :], ACT.Copy).then_inc(qk_ready, 1)

            pair(0, False, True)
            with act.Fori(1, PAIRS) as g:
                pair(g, True, True)
            pair(PAIRS, True, False)

            act.wait_ge(head_read, ATT_HEADS)
            act.wait_ge(unit_used, U_OUT2)
            for b in range(KB):
                src = xr[:, b, :] if b < 8 else ga[:, b - 8, :]
                nc.scalar.activation(y2_hi[:, b, :], src, ACT.Copy).then_inc(y2_hi_ready, 1)

            def out2_panel(i, last):
                for u in range(OUT2_UPP):
                    if not last or u < OUT2_UPP - RING:
                        split_hi(i * OUT2_UPP + (U_OUT2 + RING + u), u % RING,
                                 i * (OUT2_UPP // RING) + (landed_before(U_OUT2) + 2 + u // RING))
                if last:
                    for t in range(NT):
                        act.wait_ge(o_ready, i + t + 1)
                        act.dma_start(out_tok[:, t, i * TCOL:(i + 1) * TCOL], oo[:, t, :]).then_inc(out_stored, 16)
                    return
                act.wait_ge(o_ready, i + 1)
                act.dma_start(out_tok[:, :, bass.ds(i * TCOL, TCOL)], oo[:]).then_inc(out_stored, 16)

            with act.Fori(0, OUT_PANELS - 1) as i:
                out2_panel(i, False)
            out2_panel(OUT_PANELS - 1, True)
            act.wait_ge(out_stored, 16 * (OUT_PANELS + NT))

        @block.vector
        def _(dve):
            st = Steps(dve, dve_step)
            dve.wait_ge(xss_ready, NT)
            st.done(nc.vector.tensor_scalar(xrs[:], xss[:], 1.0 / D, EPS, ALU.mult, ALU.add))
            dve.wait_ge(x_std_ready, 1)
            st.done(nc.vector.reciprocal(xrs[:], xrs[:]))
            st.wait()
            for t in range(NT):
                nc.vector.tensor_scalar(xt[:, t, :], xt[:, t, :], xrs[:, t:t + 1], None, ALU.mult
                                        ).then_inc(x_normed, 1)
            dve.wait_ge(cols_turned, 1)
            nc.vector.tensor_copy(cols[:], ps[:, 7, :]).then_inc(cols_ready, 1)
            dve.wait_ge(cols_turned, 2)
            st.done(nc.vector.tensor_copy(dcol[:], ps[:, 6, 0:HEADS // 2]))
            dve.wait_ge(cols_ready, 1)
            for k in range(TAPS + 1):
                at = ROW_CONV_W[k] if k < TAPS else ROW_CONV_B
                st.done(nc.vector.tensor_scalar(convc[:, k, :], cols[:, at:at + CONV_BLOCKS], 0.5, None, ALU.mult))
            dve.wait_ge(c_tanh_ready, 1)
            st.done(nc.vector.scalar_tensor_tensor(silu_c[:], th_c[:], 1.0, cols[:, ROW_C:ROW_C + KB],
                                                   ALU.add, ALU.mult))
            st.wait()
            st.done(nc.vector.tensor_scalar(silu_c[:], silu_c[:], 0.5, None, ALU.mult))
            def lo(g, u):
                s = u % RING
                n = UKT * HEADS if g is None else UNIT
                dve.wait_ge(hi_ready, u + 1 if g is None else g * GU + u + DT_UNITS + 1)
                nc.vector.tensor_tensor(w_lo[:, s, 0:n], w_raw[:, s, 0:n], w_hi[:, s, 0:n].bitcast(F32),
                                        ALU.subtract).then_inc(lo_ready, 1)

            for u in range(DT_UNITS):
                lo(None, u)

            for kb in range(KB):
                dve.wait_ge(hn_hi_ready, kb + 1)
                nc.vector.scalar_tensor_tensor(hn_lo[:, kb, :], ps[:, kb % 8, :],
                                               cols[:, ROW_LN + kb:ROW_LN + kb + 1],
                                               hn_hi[:, kb, :].bitcast(F32), ALU.mult, ALU.subtract
                                               ).then_inc(hn_lo_ready, 1)

            v, e, s1, s2, pl, adt = dtv
            dve.wait_ge(unit_used, DT_UNITS)
            nc.vector.tensor_copy(cs_t[:], ps[0:HEADS, 0, :]).then_inc(dt_taken, 1)
            dve.wait_ge(dt_turned, 1)
            for t in range(NT):
                st.done(nc.vector.tensor_tensor(v[:, t, :], ps[:, 4, t * HEADS:(t + 1) * HEADS], bias_b[:], ALU.add))
            st.wait()
            st.done(nc.vector.tensor_scalar(e[:], v[:], -1.0, None, ALU.mult))
            st.wait()
            nc.vector.tensor_tensor(e[:], e[:], v[:], ALU.max).then_inc(dt_abs_ready, 1)

            def softplus():
                dve.wait_ge(dt_exp_ready, 1)
                st.done(nc.vector.tensor_scalar(s1[:], e[:], 2.0, None, ALU.add))
                st.wait()
                st.done(nc.vector.reciprocal(s1[:], s1[:]))
                st.wait()
                st.done(nc.vector.tensor_tensor(s1[:], s1[:], e[:], ALU.mult))
                st.wait()
                st.done(nc.vector.tensor_tensor(s2[:], s1[:], s1[:], ALU.mult))
                st.wait()
                st.done(nc.vector.tensor_scalar(pl[:], s2[:], 1.0 / 15, None, ALU.mult))
                for n in (13, 11, 9, 7, 5, 3):
                    st.wait()
                    st.done(nc.vector.scalar_tensor_tensor(pl[:], pl[:], 1.0 / n, s2[:], ALU.add, ALU.mult))
                st.wait()
                st.done(nc.vector.scalar_tensor_tensor(pl[:], pl[:], 1.0, s1[:], ALU.add, ALU.mult))
                st.done(nc.vector.tensor_scalar(v[:], v[:], 0.0, None, ALU.max))
                st.wait()
                st.done(nc.vector.scalar_tensor_tensor(prep[:, 0:NT, :], pl[:], 2.0, v[:], ALU.mult, ALU.add))
                st.wait()
                for t in range(NT):
                    last = nc.vector.scalar_tensor_tensor(adt[:, t, :], alog_b[:], -1.0, prep[:, t, :],
                                                          ALU.mult, ALU.mult)
                    last.then_inc(adt_ready, 1)

            def take_cs():
                dve.wait_ge(cs_summed, 1)
                nc.vector.tensor_copy(prep[:, NT:2 * NT, :], ps[:, 4, 0:NT * HEADS].rearrange(
                    "p (t h) -> p t h", t=NT)).then_inc(cs_ready, 1)

            def take_cs_rows():
                dve.wait_ge(cs_turned, 1)
                nc.vector.tensor_copy(cs_t[:], ps[0:HEADS, 5, :]).then_inc(cs_t_ready, 1)
                dve.wait_ge(ecs_ready, 1)

            def group_constants(gp):
                st.done(nc.vector.tensor_copy(gprep[:], prep[:, :, bass.ds(gp * HPG, HPG)]))
                st.done(nc.vector.tensor_copy(gd[:], dcol[:, bass.ds(gp * GB, GB)]))

            def conv_constants(g):
                st.done(nc.vector.tensor_copy(gconv[:, :, 0:2], convc[:, :, D_INNER // P:].rearrange(
                    "p k (j g) -> p k j g", g=GROUPS)[:, :, :, bass.ds(g, 1)].rearrange("p k j g -> p k (j g)")))
                st.done(nc.vector.tensor_copy(gconv[:, :, 2:6], convc[:, :, bass.ds(g * GB, GB)]))

            def ada_rows(g, k):
                dve.wait_ge(ada_landed[k % 2], (g * (KB // 2) + k // 2 + 1) * 16)
                if k == 0:
                    if not isinstance(g, int) or g:
                        dve.wait_ge(ada_stored, g * 16)
                    nc.vector.tensor_scalar(ada_acc[:], ada_raw[:, 0, :], silu_c[:, 0:1], None, ALU.mult
                                            ).then_inc(ada_used, 1)
                    return
                dve.wait_ge(ada_used, g * KB + k)
                ins = nc.vector.scalar_tensor_tensor(ada_acc[:], ada_raw[:, k % 2, :], silu_c[:, k:k + 1],
                                                     ada_acc[:], ALU.mult, ALU.add)
                ins.then_inc(ada_used, 1)

            def conv(g, j):
                dve.wait_ge(x_acc_freed, g * 3 + j + 1)
                dst = [bct[:, b, :] if j == 0 else xst[:, 2 * j - 2 + b, :] for b in range(2)]
                for b in range(2):
                    st.done(nc.vector.tensor_scalar(dst[b], xraw[:, 2 * j + b, 3:3 + SEQ],
                                                    gconv[:, 3, 2 * j + b:2 * j + b + 1],
                                                    gconv[:, 4, 2 * j + b:2 * j + b + 1], ALU.mult, ALU.add))
                for k in (2, 1, 0):
                    for b in range(2):
                        st.wait(1)
                        tap = nc.vector.scalar_tensor_tensor(
                            dst[b], xraw[:, 2 * j + b, k:k + SEQ], gconv[:, k, 2 * j + b:2 * j + b + 1],
                            dst[b], ALU.mult, ALU.add)
                        if (k, b) == (0, 1):
                            tap.then_inc(conv_summed, 1)
                        else:
                            st.done(tap)

            def conv_silu(g, j):
                dve.wait_ge(conv_tanh_ready, g * 3 + j + 1)
                dst = bct[:, :, :] if j == 0 else xst[:, 2 * j - 2:2 * j, :]
                nc.vector.scalar_tensor_tensor(dst, th[:, j % 2, :, :], 1.0, dst, ALU.add, ALU.mult
                                               ).then_inc(conv_done, 1)

            def z_silu(g, j):
                if j == 1:
                    for b in range(2):
                        dve.wait_ge(z_tanh_ready, g * 3 + 2 + b)
                        nc.vector.scalar_tensor_tensor(gz[:, 2 + b, :], th[:, 0, b, :], 1.0, ps[:, b, :], ALU.add,
                                                       ALU.mult).then_inc(z_acc_freed, 1)
                    return
                dve.wait_ge(z_tanh_ready, g * 3 + 1)
                if j == 0 and (not isinstance(g, int) or g):
                    dve.wait_ge(gated, g)
                b = 2 * (1 - j)
                nc.vector.scalar_tensor_tensor(gz[:, 2 * j:2 * j + 2, :], th[:, 1 - j, :, :], 1.0,
                                               ps[:, b:b + 2, :], ALU.add, ALU.mult).then_inc(z_acc_freed, 1)

            def chunk_prepare(gp, c):
                n = gp * NQ + c + 1
                s = c % 2
                cs = gprep[:, NT + c, :]
                dve.wait_ge(csb_landed[s], (gp * 2 + c // 2 + 1) * 16)
                st.done(nc.vector.tensor_tensor(wa[:, 0:HPG], csb[:, s, :, Q - 1], cs, ALU.subtract))
                nc.vector.tensor_copy(wa[:, HPG:], csb[:, s, :, Q - 1]).then_inc(wa_ready, 1)
                for r in range(HPG):
                    ins = nc.vector.tensor_scalar(seg[:, r, :], csb[:, s, r, :], cs[:, r:r + 1], 0.0,
                                                  ALU.subtract, ALU.min)
                ins.then_inc(seg_ready, 1)
                dve.wait_ge(chunk_in, n)
                nc.vector.tensor_copy(btok[:], ps[:, 5, 0:P])
                st.done(nc.vector.tensor_tensor(cbm[:], ps[:, 5, P:2 * P], tri[:], ALU.mult))
                st.done(nc.vector.tensor_tensor(
                    xdt[:], ps[:, 4, :].rearrange("p (r d) -> p r d", r=HPG),
                    gprep[:, c, :].unsqueeze(2).broadcast_to([P, HPG, HD]), ALU.mult))
                st.wait()
                dve.wait_ge(we_ready, n)
                st.done(nc.vector.tensor_tensor(xw[:], xdt[:], we[:, 0:HPG].unsqueeze(2).broadcast_to([P, HPG, HD]),
                                                ALU.mult))
                dve.wait_ge(decay_ready, n)
                nc.vector.tensor_tensor(seg[:], seg[:], cbm[:].unsqueeze(1).broadcast_to([P, HPG, Q]), ALU.mult
                                        ).then_inc(chunk_mid, 1)

            def chunk_collect(gp, c):
                dve.wait_ge(chunk_summed, gp * NQ + c + 1)
                new = ps[:, 4, :].rearrange("p (r d) -> p r d", r=HPG)
                if c == 0:
                    nc.vector.tensor_copy(state[:], new).then_inc(state_read, 1)
                elif c < NQ - 1:
                    st.done(nc.vector.tensor_tensor(
                        state[:], state[:], we[:, HPG:].unsqueeze(2).broadcast_to([P, HPG, HD]), ALU.mult))
                    st.wait()
                    nc.vector.tensor_tensor(state[:], state[:], new, ALU.add).then_inc(state_read, 1)
                y = ytok[:].rearrange("p b (r d) -> p (b r) d", d=HD)
                diag = ps[:, 6, :].rearrange("p (r d) -> p r d", r=HPG)
                if c == 0:
                    nc.vector.tensor_copy(y, diag).then_inc(ytok_ready, 1)
                else:
                    st.done(nc.vector.tensor_tensor(
                        y, ps[:, 7, :].rearrange("p (r d) -> p r d", r=HPG),
                        gprep[:, 2 * NT + c, :].unsqueeze(2).broadcast_to([P, HPG, HD]), ALU.mult))
                    st.wait()
                    nc.vector.tensor_tensor(y, y, diag, ALU.add).then_inc(ytok_ready, 1)

            def chunk_skip(gp, c):
                dve.wait_ge(ytok_turned, gp * NQ + c + 1)
                if c == 0:
                    dve.wait_ge(yt_free, gp + 1)
                for b in range(GB):
                    ins = nc.vector.scalar_tensor_tensor(
                        yt[:, b, c * Q:(c + 1) * Q], xst[:, b, c * Q:(c + 1) * Q], gd[:, b:b + 1],
                        ps[:, 7, b * P:(b + 1) * P], ALU.mult, ALU.add)
                ins.then_inc(yt_ready, 1)

            def body(g, prev, cur):
                gp = g - 1
                if prev:
                    group_constants(gp)
                    st.wait()
                for u in range(GU):
                    if cur:
                        lo(g, u + AHEAD)
                    if not prev and u == 0:
                        softplus()
                    if not prev and u == 2:
                        take_cs()
                    if not prev and u == 4:
                        take_cs_rows()
                    if not prev and u == 15:
                        dve.wait_ge(cs_stored, 16)
                    if prev and u == 0:
                        z_silu(gp, 1)
                        if not cur:
                            dve.wait_ge(z_acc_freed, 3 * GROUPS)
                            dve.sem_inc(d_bank_freed, NT)
                    if cur and u < KB:
                        ada_rows(g, u)
                    if prev and u in (3, 6, 9, 12):
                        chunk_prepare(gp, u // 3 - 1)
                    if prev and u in (6, 9, 12, 15):
                        chunk_skip(gp, u // 3 - 2)
                    if prev and u in (5, 8, 11, 14):
                        chunk_collect(gp, (u - 5) // 3)
                    if not cur and u in LAST_SCAN:
                        y_lo(LAST_SCAN.index(u))
                        out1_lo(0, LAST_SCAN.index(u) + AHEAD)
                    if cur and u == 15:
                        conv_constants(g)
                        st.wait()
                        conv(g, 0)
                    if cur and u == 16:
                        conv(g, 1)
                    if cur and u == 17:
                        conv_silu(g, 0)
                        conv(g, 2)
                    if cur and u == 18:
                        conv_silu(g, 1)
                    if cur and u == 19:
                        conv_silu(g, 2)
                        z_silu(g, 0)

            def split_lo(unit, slot):
                dve.wait_ge(hi_ready, unit + 1)
                nc.vector.tensor_tensor(w_lo[:, slot, :], w_raw[:, slot, :], w_hi[:, slot, :].bitcast(F32),
                                        ALU.subtract).then_inc(lo_ready, 1)

            def out1_lo(i, u):
                split_lo(i * OUT1_UPP + (U_OUT1 + u), u % RING)

            def y_lo(j):
                for b in (2 * j, 2 * j + 1):
                    dve.wait_ge(y_hi_ready, b + 1)
                    nc.vector.scalar_tensor_tensor(y_block(b, 1), y_in[:, j % 2, b % 2, :],
                                                   cols[:, ROW_NORM + b:ROW_NORM + b + 1],
                                                   y_block(b, 0).bitcast(F32), ALU.mult, ALU.subtract
                                                   ).then_inc(y_lo_ready, 1)

            def mean_eps(out_, in_, n, eps=EPS):
                return nc.vector.tensor_scalar(out_, in_, 1.0 / n, eps, ALU.mult, ALU.add)

            for u in range(AHEAD):
                lo(0, u)
            walk(dve, body, st, 46)

            for j in range(Y_HALF // 2, Y_HALF):
                if j == Y_HALF // 2 + 1:
                    dve.wait_ge(yt_ready, GROUPS * NQ)
                    nc.vector.tensor_tensor(yt[:], yt[:], gz[:], ALU.mult).then_inc(gated, 1)
                if j == Y_HALF // 2 + 2:
                    dve.wait_ge(yt_free, GROUPS)
                    dve.wait_ge(y_squared, 1)
                    st.done(nc.vector.tensor_tensor(gz[:, 0:2, :], gz[:, 0:2, :], gz[:, 2:4, :], ALU.add))
                    st.wait()
                    st.done(nc.vector.tensor_tensor(ysq[:], ysq[:], gz[:, 0, :], ALU.add))
                    st.wait()
                    nc.vector.tensor_tensor(ysq[:], ysq[:], gz[:, 1, :], ALU.add).then_inc(y_squared, 1)
                y_lo(j)
                out1_lo(*divmod(j + AHEAD, OUT1_UPP))
            dve.wait_ge(ysq_summed, 1)
            mean_eps(yrs, ps[:, 4, 0:NT], D_INNER, 4 * EPS).then_inc(ysq_mean_ready, 1)
            dve.wait_ge(ysq_std_ready, 1)
            st.done(nc.vector.reciprocal(yrs, yrs))
            st.wait()

            def x1_panel(i):
                dve.wait_ge(x_in_landed, i * 16 + 16)
                for t in range(NT):
                    if t < NT - 1:
                        dve.wait_ge(d_bank_done, i * (NT - 1) + t + 1)
                    else:
                        dve.wait_ge(unit_used, i * OUT1_UPP + (U_OUT1 + OUT1_UPP))
                    nc.vector.scalar_tensor_tensor(x1p[:, t, :], ps[:, t, :], yrs[:, t:t + 1], x1p[:, t, :],
                                                   ALU.mult, ALU.add).then_inc(x1_added, 1)
                    dve.wait_ge(x1_added, i * NT + (t + 1))
                    dve.sem_inc(d_bank_freed, 1)

            def x1_gain(i):
                if isinstance(i, int):
                    dve.wait_ge(gateb_landed, 16)
                for t in range(NT):
                    dve.wait_ge(x1_squared, i * NT + (t + 1))
                    nc.vector.tensor_tensor(x1p[:, t, :], x1p[:, t, :], gateb[:, bass.ds(i * TCOL, TCOL)], ALU.mult
                                            ).then_inc(x1g_ready, 1)

            def x1_sum(i):
                dve.wait_ge(x1g_squared, i * NT + NT)
                for k, s_ in enumerate((x1ss, x1gs)):
                    part = x1_part[:, k, :]
                    if isinstance(i, int):
                        ins = nc.vector.tensor_copy(s_, part)
                    else:
                        ins = nc.vector.tensor_tensor(s_, s_, part, ALU.add)
                ins.then_inc(x1_summed, 1)

            for u in range(AHEAD, RING - 1):
                out1_lo(1, u)
            x1_panel(0)
            out1_lo(1, RING - 1)
            x1_gain(0)
            x1_sum(0)
            with dve.Fori(1, OUT_PANELS) as i:
                dve.wait_ge(x1_summed, i)
                for u in range(RING, OUT1_UPP + RING):
                    if u == OUT1_UPP + RING - 1:
                        x1_panel(i)
                    out1_lo(i, u)
                x1_gain(i)
                x1_sum(i)

            dve.wait_ge(x1_summed, OUT_PANELS)
            mean_eps(x1rs, x1ss, D).then_inc(x1_mean_ready, 1)
            dve.wait_ge(x1_std_ready, 1)
            st.done(nc.vector.reciprocal(x1rs, x1rs))
            st.wait()
            st.done(nc.vector.tensor_tensor(x1rr, x1rs, x1rs, ALU.mult))
            st.wait()
            st.done(nc.vector.tensor_tensor(x1rr, x1rr, x1gs, ALU.mult))
            st.wait()
            mean_eps(x1rr, x1rr, D).then_inc(x1_mean_ready, 1)
            dve.wait_ge(x1_std_ready, 2)
            st.done(nc.vector.reciprocal(x1rr, x1rr))
            st.wait()
            st.done(nc.vector.tensor_tensor(x1rr, x1rr, x1rs, ALU.mult))
            st.wait()
            for c in range(OUT_PANELS):
                at = slice(c * TCOL, (c + 1) * TCOL)
                for t in range(NT):
                    if c == t == 0:
                        dve.wait_ge(x1t_landed, 16 * NT)
                    src = x1t[:, t, at] if c < OUT_PANELS - 1 else x1p[:, t, :]
                    nc.vector.tensor_scalar(xh[:, t, at], src, x1rr[:, t:t + 1], None, ALU.mult).then_inc(xh_ready, 1)
                if c == 0:
                    dve.wait_ge(ada_reduced, 2)
                    for k, col in enumerate((shc, scc)):
                        st.done(nc.vector.tensor_reduce(
                            col, ps[:, 4 - 4 * k:8 - 4 * k, :].rearrange("p b (c n) -> p (b c) n", n=P), AX_X, ALU.add))
                    st.wait()
                    nc.vector.tensor_tensor(shc, shc, cols[:, ROW_SHIFT_B:ROW_SHIFT_B + KB], ALU.add)
                    nc.vector.scalar_tensor_tensor(scc, scc, 1.0, cols[:, ROW_SCALE_B:ROW_SCALE_B + KB],
                                                   ALU.add, ALU.add).then_inc(ada_cols_ready, 1)
            dve.wait_ge(x1_free, 16 * (OUT_PANELS + 1))
            for kb in range(KB):
                dve.wait_ge(h_hi_ready, kb + 1)
                if kb == 4:
                    dve.wait_ge(ada_reduced, 3)
                    dve.wait_ge(gateb_landed, 32)
                    for j in range(D // 512):
                        at = slice(j * 512, (j + 1) * 512)
                        ins = nc.vector.tensor_tensor(gateb[:, at], gateb[:, at], ps[:, j, :], ALU.add)
                    st.done(ins)
                    st.wait()
                    dve.sem_inc(f_bank_freed, 2)
                nc.vector.tensor_tensor(h_lo[:, kb, :], h_mod[:, kb % 4, :], h_hi[:, kb, :].bitcast(F32),
                                        ALU.subtract).then_inc(h_lo_ready, 1)

            for k in range(TAPS):
                st.done(nc.vector.tensor_copy(lconst[:, k, :], cols[:, ROW_CONV2_W + 8 * k:ROW_CONV2_W + 8 * k + 8]))
            st.done(nc.vector.tensor_copy(lconst[:, 4, :], cols[:, ROW_CONV2_B:ROW_CONV2_B + 8]))
            for k, at in ((5, ROW_RG_A), (6, ROW_RG_X)):
                st.done(nc.vector.tensor_scalar(lconst[:, k, :], cols[:, at:at + 8], 0.5, None, ALU.mult))
            lam = cols[:, ROW_LRU:ROW_LRU + 8]
            v, e, s1, s2 = le
            st.done(nc.vector.tensor_scalar(v[:], lam, -1.0, None, ALU.mult))
            st.wait()
            nc.vector.tensor_tensor(e[:], v[:], lam, ALU.max).then_inc(lru_abs_ready, 1)
            dve.wait_ge(lru_exp_ready, 1)
            st.done(nc.vector.tensor_scalar(s1[:], e[:], 2.0, None, ALU.add))
            st.wait()
            st.done(nc.vector.reciprocal(s1[:], s1[:]))
            st.wait()
            st.done(nc.vector.tensor_tensor(s1[:], s1[:], e[:], ALU.mult))
            st.wait()
            st.done(nc.vector.tensor_tensor(s2[:], s1[:], s1[:], ALU.mult))
            st.wait()
            st.done(nc.vector.tensor_scalar(e[:], s2[:], 1.0 / 15, None, ALU.mult))
            for n in (13, 11, 9, 7, 5, 3):
                st.wait()
                st.done(nc.vector.scalar_tensor_tensor(e[:], e[:], 1.0 / n, s2[:], ALU.add, ALU.mult))
            st.wait()
            st.done(nc.vector.scalar_tensor_tensor(e[:], e[:], 1.0, s1[:], ALU.add, ALU.mult))
            st.done(nc.vector.tensor_scalar(v[:], v[:], 0.0, None, ALU.max))
            st.wait()
            st.done(nc.vector.scalar_tensor_tensor(v[:], e[:], 2.0, v[:], ALU.mult, ALU.add))
            st.wait()
            st.done(nc.vector.tensor_scalar(lconst[:, 7, :], v[:], -LRU_C / 2, None, ALU.mult))

            dve.wait_ge(rope_in_landed, 32)
            st.done(nc.vector.tensor_copy(rt_f[:], rt_i[:]))
            st.wait()
            for t in range(NT):
                st.done(nc.vector.tensor_scalar(ra[0][:, t, :], invf[:], rt_f[:, t:t + 1], None, ALU.mult))
            st.wait()
            st.done(nc.vector.tensor_scalar(ra[1][:], ra[0][:], 1.0 / (2 * np.pi), ROUND, ALU.mult, ALU.add))
            st.wait()
            st.done(nc.vector.tensor_scalar(ra[1][:], ra[1][:], -ROUND, None, ALU.add))
            for part in TURN:
                st.wait()
                st.done(nc.vector.scalar_tensor_tensor(ra[0][:], ra[1][:], -part, ra[0][:], ALU.mult, ALU.add))
            st.wait()
            st.done(nc.vector.tensor_scalar(ra[1][:], ra[0][:], float(np.pi / 2), None, ALU.add))
            st.wait()
            st.done(nc.vector.tensor_scalar(ra[2][:], ra[1][:], PI32, -2 * np.pi, ALU.is_gt, ALU.mult))
            st.wait()
            st.done(nc.vector.tensor_tensor(ra[1][:], ra[1][:], ra[2][:], ALU.add))
            st.done(nc.vector.tensor_scalar(ra[0][:], ra[0][:], -PI32, PI32, ALU.max, ALU.min))
            st.wait()
            nc.vector.tensor_scalar(ra[1][:], ra[1][:], -PI32, PI32, ALU.max, ALU.min).then_inc(angles_ready, 1)
            dve.wait_ge(rope_ready, 2)

            def panels(unit, count, lru=None):
                with dve.Fori(0, count) as i:
                    if lru is not None:
                        st.enter(i + 1, LRU_STEPS)
                        j = i + lru
                        n = i + (lru + 1)
                        xb = xr[:, bass.ds(j, 1), :].rearrange("p o n -> p (o n)")
                        gb = gr[:, bass.ds(j, 1), :].rearrange("p o n -> p (o n)")
                    for u in range(UPP):
                        if lru is not None and u == 3:
                            lru_tail(xb, gb, n)
                        if lru is not None and u == 0:
                            lru_conv(xb, j)
                        split_lo(i * UPP + (unit + RING + u), u)
                        if lru is not None and u == 1:
                            lru_logs(gb, n)
                if lru is not None:
                    st.leave(count, LRU_STEPS)

            def lru_conv(xb, j):
                st.done(nc.vector.tensor_copy(lc[:], lconst[:, :, bass.ds(j, 1)].rearrange("p k o -> p (k o)")))
                st.wait()
                st.done(nc.vector.tensor_scalar(lt[0][:], xb, lc[:, 3:4], lc[:, 4:5], ALU.mult, ALU.add))
                for k in (2, 1, 0):
                    off = TAPS - 1 - k
                    st.wait()
                    ins = nc.vector.scalar_tensor_tensor(lt[0][:, off:], xb[:, 0:SEQ - off], lc[:, k:k + 1],
                                                         lt[0][:, off:], ALU.mult, ALU.add)
                    if k:
                        st.done(ins)
                ins.then_inc(xc_ready, 1)

            def lru_logs(gb, n):
                dve.wait_ge(gates_ready, n)
                st.done(nc.vector.tensor_scalar(lt[1][:], lt[1][:], 1.0, lc[:, 7:8], ALU.add, ALU.mult))
                st.done(nc.vector.scalar_tensor_tensor(gb, lt[3][:], 1.0, gb, ALU.add, ALU.mult))
                st.done(nc.vector.scalar_tensor_tensor(lt[2][:], lt[2][:], 1.0, lt[0][:], ALU.add, ALU.mult))
                st.wait()
                st.done(nc.vector.tensor_scalar(lt[3][:], lt[1][:], 2.0, -SERIES_TO, ALU.mult, ALU.max))
                st.wait()
                nc.vector.scalar_tensor_tensor(lt[4][:], lt[1][:], 2.0, lt[3][:], ALU.mult, ALU.subtract
                                               ).then_inc(logs_ready, 1)
                st.done(nc.vector.tensor_scalar(lt[5][:], lt[3][:], 1.0 / 720, None, ALU.mult))
                for c in (1.0 / 120, 1.0 / 24, 1.0 / 6, 0.5, 1.0):
                    st.wait()
                    st.done(nc.vector.scalar_tensor_tensor(lt[5][:], lt[5][:], c, lt[3][:], ALU.add, ALU.mult))
                st.wait()
                dve.wait_ge(decays_ready, n)
                st.done(nc.vector.tensor_scalar(lt[4][:], lt[4][:], -1.0, 1.0, ALU.mult, ALU.add))
                st.wait()
                st.done(nc.vector.scalar_tensor_tensor(lt[4][:], lt[5][:], 1.0, lt[4][:], ALU.add, ALU.mult))
                st.wait()
                nc.vector.tensor_tensor(lt[4][:], lt[4][:], lt[5][:], ALU.subtract).then_inc(var_ready, 1)

            def lru_tail(xb, gb, n):
                dve.wait_ge(dev_ready, n)
                st.done(nc.vector.scalar_tensor_tensor(lt[4][:], lt[4][:], 0.5, lt[2][:], ALU.mult, ALU.mult))
                st.wait()
                st.done(nc.vector.tensor_tensor_scan(lt[1][:], lt[0][:], lt[4][:], 0.0, ALU.mult, ALU.add))
                st.wait()
                nc.vector.scalar_tensor_tensor(xb, lt[1][:], 0.5, gb, ALU.mult, ALU.mult).then_inc(rnn_done, 1)

            panels(U_RNN, 4)
            panels(U_RNN + 16, 4)
            panels(U_QKV, 4, 0)
            panels(U_GA, 4, 4)

            for u in range(RING):
                split_lo(U_PAIR + u, u)
            dve.wait_ge(unit_used, U_PAIR)
            nc.vector.tensor_copy(kpt[0:ROPE, :], ps[0:ROPE, 0, :]).then_inc(kr_taken, 1)
            for b in range(2 * LORA_KB):
                dve.wait_ge(c_hi_ready, b + 1)
                at = ROW_QA + b
                nc.vector.scalar_tensor_tensor(c_lo[:, b, :], qkvc[:, b, :], cols[:, at:at + 1],
                                               c_hi[:, b, :].bitcast(F32), ALU.mult, ALU.subtract
                                               ).then_inc(c_lo_ready, 1)
            for part, sq in enumerate(latent_sq):
                dve.wait_ge(latent_squared, part + 1)
                st.done(nc.vector.tensor_tensor(sq[:, 0:2, :], sq[:, 0:2, :], sq[:, 2:4, :], ALU.add))
                st.wait()
                nc.vector.tensor_tensor(sq[:, 0, :], sq[:, 0, :], sq[:, 1, :], ALU.add).then_inc(latent_added, 1)
            dve.wait_ge(kr_turned, 1)
            nc.vector.tensor_copy(kr_tok[:], ps[:, 6, 0:NT * ROPE].rearrange("p (t n) -> p t n", t=NT)
                                  ).then_inc(kr_ready, 1)
            dve.wait_ge(kr_squared, 1)
            st.done(nc.vector.tensor_reduce(krs, sqt[:, :, 0, 0:ROPE], AX_X, ALU.add))
            st.wait()
            st.done(mean_eps(krs, krs, ROPE))
            dve.wait_ge(latent_summed, 2)
            st.done(mean_eps(small[:, 12:20], ps[:, 4, 0:8], 4 * P))
            st.wait()
            dve.sem_inc(latent_var_ready, 1)
            dve.wait_ge(latent_std_ready, 1)
            nc.vector.reciprocal(small[:, 12:24], small[:, 12:24]).then_inc(latent_rms_ready, 1)
            dve.wait_ge(latent_rms_ready, 1)

            def rotate(dst, src, shape):
                cos, sin = (rope_t[:, k, :, :] for k in range(2))
                temps = [a[:] for a in rt]
                if len(shape) == 3:
                    temps = [a[:, :, 0, :] for a in rt]
                else:
                    cos, sin = (a.unsqueeze(2).broadcast_to(shape) for a in (cos, sin))
                lo_, hi_ = src[..., 0:ROPE // 2], src[..., ROPE // 2:ROPE]
                for a, (h_, c_) in zip(temps, ((lo_, cos), (hi_, sin), (lo_, sin), (hi_, cos))):
                    st.done(nc.vector.tensor_tensor(a, h_, c_, ALU.mult))
                st.wait()
                for d in dst:
                    st.done(nc.vector.tensor_tensor(d[..., 0:ROPE // 2], temps[0], temps[1], ALU.subtract))
                    last = nc.vector.tensor_tensor(d[..., ROPE // 2:ROPE], temps[2], temps[3], ALU.add)
                    if d is not dst[-1]:
                        st.done(last)
                return last

            dve.wait_ge(gains_landed, 64)
            st.done(nc.vector.tensor_tensor(kr_tok[:], kr_tok[:], krs.unsqueeze(2).broadcast_to([P, NT, ROPE]),
                                            ALU.mult))
            st.wait()
            st.done(nc.vector.tensor_tensor(kr_tok[:], kr_tok[:],
                                            gain_b[:, ROPE:].unsqueeze(1).broadcast_to([P, NT, ROPE]), ALU.mult))
            st.wait()
            rotate([qpe[:, :, 0, :], qpe[:, :, 1, :]], kr_tok[:], [P, NT, ROPE // 2]).then_inc(kpe_ready, 1)

            def pair(g, prev, cur):
                gp = g - 1
                for k in range(11):
                    if cur and k < 4:
                        split_lo(g * 4 + (U_PAIR + RING + k), k)
                    if prev and k == 4:
                        dve.wait_ge(ga_tanh_ready, g)
                        st.done(nc.vector.scalar_tensor_tensor(gth[:], gth[:], 1.0, ga[:, bass.ds(gp * 2, 2), :],
                                                               ALU.add, ALU.mult))
                    if prev and k >= 3:
                        j = k - 3
                        qb = j % 4
                        if j == NT:
                            dve.wait_ge(head_summed, gp * 2 + 1)
                        dve.wait_ge(prob_turned, gp * 8 + j + 1)
                        nc.vector.tensor_copy(pt[:, 0:qb + 1, qb * P:(qb + 1) * P],
                                              ps[:, 6, 0:(qb + 1) * P].rearrange("p (k q) -> p k q", q=P)
                                              ).then_inc(pt_ready, 1)
                    if prev and k < 8:
                        n = (k % 4 + 1) * P
                        dve.wait_ge(scored, gp * 8 + k + 1)
                        st.done(nc.vector.tensor_reduce(sm[:, 0, k:k + 1], ps[:, 4 + k % 2, 0:n], AX_X, ALU.max))
                        st.wait()
                        nc.vector.tensor_scalar(sm[:, 1, k:k + 1], sm[:, 0, k:k + 1], -SM_SCALE, None, ALU.mult
                                                ).then_inc(max_ready, 1)
                    if prev and 1 <= k < 9:
                        j = k - 1
                        n = (j % 4 + 1) * P
                        dve.wait_ge(exp_ready, gp * 8 + j + 1)
                        st.done(nc.vector.reciprocal(sm[:, 3, j:j + 1], sm[:, 2, j:j + 1]))
                        st.wait()
                        nc.vector.tensor_scalar(prob[:, j % 2, 0:n], prob[:, j % 2, 0:n], sm[:, 3, j:j + 1], None,
                                                ALU.mult).then_inc(prob_ready, 1)
                    if prev and k == 8:
                        head_out(gp, 0)
                    if cur and k == 4:
                        dve.wait_ge(sq_ready, g * 2 + 1)
                        st.done(nc.vector.tensor_reduce(nrm[:, 0, :, :], sqt[:, :, :, 0:NOPE], AX_X, ALU.add))
                        nc.vector.tensor_reduce(nrm[:, 1, :, :], sqt[:, :, :, NOPE:], AX_X, ALU.add
                                                ).then_inc(q_reduced, 1)
                    if cur and k == 5:
                        dve.wait_ge(sq_ready, g * 2 + 2)
                        dve.wait_ge(q_reduced, g + 1)
                        st.done(nc.vector.tensor_reduce(nrm[:, 2, :, :], sqt[:, :, :, 0:NOPE], AX_X, ALU.add))
                        st.wait()
                        st.done(mean_eps(nrm[:, 0, :, :], nrm[:, 0, :, :], NOPE))
                        st.done(mean_eps(nrm[:, 1, :, :], nrm[:, 1, :, :], ROPE))
                        mean_eps(nrm[:, 2, :, :], nrm[:, 2, :, :], NOPE).then_inc(nrm_ready, 1)
                    if cur and k == 6:
                        dve.wait_ge(nrm_std_ready, g + 1)
                        nc.vector.reciprocal(nrm[:], nrm[:]).then_inc(nope_normed, 1)
                        dve.wait_ge(nope_normed, g * 2 + 1)
                        for k_, a in ((0, q_tok), (2, kv_tok)):
                            v_ = a[:, :, :, 0:NOPE].rearrange("p t h n -> p (t h) n")
                            ins = nc.vector.tensor_tensor(
                                v_, v_, nrm[:, k_, :, :].rearrange("p t h -> p (t h)").unsqueeze(2).broadcast_to(
                                    [P, 2 * NT, NOPE]), ALU.mult)
                        ins.then_inc(nope_normed, 1)
                if prev:
                    head_out(gp, 1)
                if cur:
                    dve.wait_ge(kv_read, g + 1)
                    nc.vector.tensor_copy(vt[:], kv_tok[:, :, :, NOPE:]).then_inc(v_ready, 1)

            def head_out(gp, h):
                dve.wait_ge(head_summed, gp * 2 + h + 1)
                nc.vector.scalar_tensor_tensor(ga[:, bass.ds(gp * 2 + h, 1), :].rearrange("p o n -> p (o n)"),
                                               ps[:, 7, :], 0.5, gth[:, h, :], ALU.mult, ALU.mult
                                               ).then_inc(head_read, 1)

            pair(0, False, True)
            dve.wait_ge(kpe_turned, 1)
            nc.vector.tensor_copy(kpt[:], ps[:, 5, :]).then_inc(kpt_ready, 1)
            with dve.Fori(1, PAIRS) as g:
                st.enter(g, PAIR_STEPS)
                pair(g, True, True)
            st.leave(PAIRS - 1, PAIR_STEPS)
            pair(PAIRS, True, False)

            dve.sem_inc(z_bank_freed, NT)
            for b in range(KB):
                src = xr[:, b, :] if b < 8 else ga[:, b - 8, :]
                dve.wait_ge(y2_hi_ready, b + 1)
                nc.vector.tensor_tensor(y2_lo[:, b, :], src, y2_hi[:, b, :].bitcast(F32), ALU.subtract
                                        ).then_inc(y2_lo_ready, 1)
            dve.wait_ge(y2_lo_ready, KB)
            dve.sem_inc(out_stored, 16)

            def out2_panel(i, last):
                for u in range(OUT2_UPP):
                    if u == OUT2_UPP - 1:
                        dve.wait_ge(xo_landed, i * 16 + 16)
                        dve.wait_ge(out_stored, i * 16 + 16)
                        for t in range(NT):
                            if t < NT - 1:
                                dve.wait_ge(z_bank_done, i * (NT - 1) + t + 1)
                            else:
                                dve.wait_ge(unit_used, i * OUT2_UPP + (U_OUT2 + OUT2_UPP))
                            nc.vector.tensor_tensor(oo[:, t, :], ps[:, t, :], gateb[:, bass.ds(i * TCOL, TCOL)],
                                                    ALU.mult).then_inc(z_bank_freed, 1)
                            dve.wait_ge(z_bank_freed, i * NT + (NT + t + 1))
                            ins = nc.vector.scalar_tensor_tensor(oo[:, t, :], xo[:, t, :], x1rs[:, t:t + 1],
                                                                 oo[:, t, :], ALU.mult, ALU.add)
                            if last or t == NT - 1:
                                ins.then_inc(o_ready, 1)
                        if not last:
                            dve.wait_ge(o_ready, i + 1)
                            dve.sem_inc(xo_free, 1)
                    if not last or u < OUT2_UPP - RING:
                        split_lo(i * OUT2_UPP + (U_OUT2 + RING + u), u % RING)

            with dve.Fori(0, OUT_PANELS - 1) as i:
                out2_panel(i, False)
            out2_panel(OUT_PANELS - 1, True)

        @block.tensor
        def _(pe):
            pe.wait_ge(consts_made, 1)
            for kb in range(KB):
                if kb < 1:
                    pe.wait_ge(x_normed, NT)
                if kb >= 8:
                    pe.wait_ge(hn_lo_ready, kb - 7)
                if kb == 6:
                    pe.wait_ge(small_landed, SMALL * 16)
                    for t in range(4):
                        mm = nc.tensor.transpose(ps[:, 7, t * P:(t + 1) * P], vrows[:, t, :], ident[:])
                    mm.then_inc(cols_turned, 1)
                    nc.tensor.matmul(ps[:, 6, 0:HEADS // 2], halves[:], d2[:], start=True, stop=True
                                     ).then_inc(cols_turned, 1)
                    pe.wait_ge(dve_step, 3)
                    pe.wait_ge(cols_ready, 1)
                for t in range(NT):
                    mm = nc.tensor.transpose(ps[:, kb % 8, t * P:(t + 1) * P], xt[:, t, kb * P:(kb + 1) * P], ident[:])
                mm.then_inc(x_turned, 1)

            def three(out_, a_hi, a_lo, b_hi, b_lo, start, stop):
                nc.tensor.matmul(out_, a_hi, b_hi, start=start, stop=False)
                nc.tensor.matmul(out_, a_hi, b_lo, start=False, stop=False)
                return nc.tensor.matmul(out_, a_lo, b_hi, start=False, stop=stop)

            for u in range(DT_UNITS):
                pe.wait_ge(lo_ready, u + 1)
                pe.wait_ge(hn_lo_ready, max((u + 1) * UKT, 9))
                for k in range(UKT):
                    kb = u * UKT + k
                    w = [unit_ap(r, u, HEADS)[:, k, :] for r in (w_hi, w_lo)]
                    mm = three(ps[0:HEADS, 0, :], *w, hn_hi[:, kb, :], hn_lo[:, kb, :], kb == 0, kb == KB - 1)
                mm.then_inc(unit_used, 1)
            pe.wait_ge(dt_taken, 1)
            for t in range(NT):
                mm = nc.tensor.transpose(ps[:, 4, t * HEADS:(t + 1) * HEADS], cs_t[:, t * P:(t + 1) * P],
                                         ident[0:HEADS, 0:HEADS])
            mm.then_inc(dt_turned, 1)
            def sum_cs():
                for t in range(NT):
                    pe.wait_ge(adt_ready, t + 1)
                    mm = nc.tensor.matmul(ps[:, 4, t * HEADS:(t + 1) * HEADS], tri[:], dtv[5][:, t, :],
                                          start=True, stop=True)
                mm.then_inc(cs_summed, 1)

            def turn_cs():
                pe.wait_ge(cs_ready, 1)
                for t in range(NT):
                    mm = nc.tensor.transpose(ps[0:HEADS, 5, t * P:(t + 1) * P], prep[:, NT + t, :], ident[:])
                mm.then_inc(cs_turned, 1)

            def project(g, u):
                p, kq = divmod(u, UPP)
                s = u % RING
                if kq == 0:
                    if p == 0:
                        if not isinstance(g, int) or g:
                            pe.wait_ge(z_acc_freed, g * 3 - 1)
                    elif p >= 2:
                        pe.wait_ge(x_acc_freed, g * 3 + p - 1)
                pe.wait_ge(lo_ready, g * GU + u + DT_UNITS + 1)
                for n in range(2):
                    if u == 0 and n == 1 and (not isinstance(g, int) or g):
                        pe.wait_ge(z_acc_freed, g * 3)
                    for k in range(UKT):
                        kb = kq * UKT + k
                        w = [unit_ap(r, s)[:, k, n * P:(n + 1) * P] for r in (w_hi, w_lo)]
                        mm = three(ps[:, 2 * (p % 2) + n, :], *w, hn_hi[:, kb, :], hn_lo[:, kb, :],
                                   kb == 0, kb == KB - 1)
                    if u == GU - 1 and n == 0:
                        mm.then_inc(z_half_done, 1)
                mm.then_inc(unit_used, 1)

            def chunk_turn(gp, c):
                at = slice(c * Q, (c + 1) * Q)
                if c == 0:
                    pe.wait_ge(conv_done, gp * 3 + 3)
                else:
                    pe.wait_ge(state_read, gp * 3 + c)
                for b in range(GB):
                    nc.tensor.transpose(ps[:, 4, b * P:(b + 1) * P], xst[:, b, at], ident[:])
                nc.tensor.transpose(ps[:, 5, 0:P], bct[:, 0, at], ident[:])
                nc.tensor.matmul(ps[:, 5, P:2 * P], bct[:, 0, at], bct[:, 1, at], start=True, stop=True
                                 ).then_inc(chunk_in, 1)

            def chunk_sum(gp, c):
                at = slice(c * Q, (c + 1) * Q)
                pe.wait_ge(chunk_mid, gp * NQ + c + 1)
                for r in range(HPG):
                    mm = nc.tensor.matmul(ps[:, 6, r * HD:(r + 1) * HD], seg[:, r, :], xdt[:, r, :],
                                          start=True, stop=True)
                if c:
                    pe.wait_ge(yt_ready, gp * NQ + c)
                    mm = nc.tensor.matmul(ps[:, 7, :], bct[:, 1, at], state[:].rearrange("p r d -> p (r d)"),
                                          start=True, stop=True)
                if c < NQ - 1:
                    mm = nc.tensor.matmul(ps[:, 4, :], btok[:], xw[:].rearrange("p r d -> p (r d)"),
                                          start=True, stop=True)
                mm.then_inc(chunk_summed, 1)

            def chunk_turn_back(gp, c):
                pe.wait_ge(ytok_ready, gp * NQ + c + 1)
                for b in range(GB):
                    mm = nc.tensor.transpose(ps[:, 7, b * P:(b + 1) * P], ytok[:, b, :], ident[:])
                mm.then_inc(ytok_turned, 1)

            def body(g, prev, cur):
                gp = g - 1
                for u in range(GU):
                    if cur:
                        project(g, u)
                    if not prev and u == 1:
                        sum_cs()
                    if not prev and u == 3:
                        turn_cs()
                    if prev and u in (1, 4, 7, 10):
                        chunk_turn(gp, u // 3)
                    if prev and u in (3, 6, 9, 12):
                        chunk_sum(gp, u // 3 - 1)
                    if prev and u in (5, 8, 11, 14):
                        chunk_turn_back(gp, (u - 5) // 3)
                    if not cur and u in LAST_SCAN:
                        out1_unit(0, LAST_SCAN.index(u))

            def tok_unit(unit_wait, slot, n, lhs, kb0, first, last, freed=None, done=None):
                pe.wait_ge(lo_ready, unit_wait)
                for t in range(NT):
                    if first and freed is not None:
                        freed(t)
                    at = slice(t * P, (t + 1) * P)
                    for k in range(TKT):
                        w = [r[:, slot, k * n:(k + 1) * n] for r in (w_hi, w_lo)]
                        mm = three(ps[:, t, 0:n], *(a(kb0 + k)[:, at] for a in lhs), *w,
                                   first and k == 0, last and k == TKT - 1)
                    if last and done is not None and t < NT - 1:
                        mm.then_inc(done, 1)
                mm.then_inc(unit_used, 1)

            def blocks(tensors):
                return [lambda b, a=a: a[:, b, :] for a in tensors]

            def out1_unit(i, u):
                pe.wait_ge(y_lo_ready, (u + 1) * TKT)
                tok_unit(i * OUT1_UPP + (U_OUT1 + u + 1), u % RING, TCOL,
                         [lambda b: y_block(b, 0), lambda b: y_block(b, 1)], u * TKT,
                         u == 0, u == OUT1_UPP - 1,
                         lambda t: pe.wait_ge(d_bank_freed, i * NT + t + 1), d_bank_done)

            walk(pe, body)

            for u in range(Y_HALF // TKT, OUT1_UPP):
                if u == Y_HALF // TKT + 3:
                    pe.wait_ge(y_squared, 2)
                    for t in range(NT):
                        mm = nc.tensor.matmul(ps[:, 4, t:t + 1], ysq[:, t * P:(t + 1) * P], ones[:, 0:1],
                                              start=True, stop=True)
                    mm.then_inc(ysq_summed, 1)
                out1_unit(0, u)
            with pe.Fori(1, OUT_PANELS) as i:
                for u in range(OUT1_UPP):
                    out1_unit(i, u)

            pe.wait_ge(ada_in_landed, 16 * 3)
            for k in range(2):
                if k:
                    pe.wait_ge(d_bank_freed, NT * (OUT_PANELS + 1))
                for b in range(KB):
                    mm = nc.tensor.transpose(ps[:, 4 - 4 * k + b // 4, b % 4 * P:(b % 4 + 1) * P],
                                             ada_in[:, k * D + b * P:k * D + (b + 1) * P], ident[:])
                mm.then_inc(ada_reduced, 1)
            pe.wait_ge(ada_cols_ready, 1)
            for kb in range(KB):
                if kb == 4:
                    for j in range(D // 512):
                        mm = nc.tensor.matmul(ps[:, j, :], ones[:], ada_in[:, 2 * D + j * 512:2 * D + (j + 1) * 512],
                                              start=True, stop=True)
                    mm.then_inc(ada_reduced, 1)
                pe.wait_ge(xh_ready, (kb // 4 + 1) * NT)
                if kb >= 4:
                    pe.wait_ge(h_mod_ready, kb - 3)
                for t in range(NT):
                    mm = nc.tensor.transpose(ps[:, 4 + kb % 4, t * P:(t + 1) * P], xh[:, t, kb * P:(kb + 1) * P],
                                             ident[:])
                mm.then_inc(h_turned, 1)

            def panels(part, unit, count, lru=None):
                with pe.Fori(0, count) as i:
                    for u in range(UPP):
                        pe.wait_ge(lo_ready, i * UPP + (unit + u + 1))
                        if part == 0:
                            pe.wait_ge(h_lo_ready, (u + 1) * UKT)
                        for n in range(2):
                            if u == 0:
                                pe.wait_ge(f_bank_freed, i * 2 + (part * 8 + n + 1))
                            for k in range(UKT):
                                kb = u * UKT + k
                                w = [unit_ap(r, u)[:, k, n * P:(n + 1) * P] for r in (w_hi, w_lo)]
                                mm = three(ps[:, n, :], *w, h_hi[:, kb, :], h_lo[:, kb, :],
                                           kb == 0, kb == KB - 1)
                            if n == 0 and u == UPP - 1:
                                mm.then_inc(f_bank_done, 1)
                        mm.then_inc(unit_used, 1)
                        if lru is not None and u == 1:
                            j = i + (lru + 1)
                            pe.wait_ge(xc_ready, j)
                            pe.wait_ge(wblk_landed, i * 64 + (lru + 1) * 64)
                            for kind in range(2):
                                mm = nc.tensor.matmul(ps[:, 4 + kind, :], wblk[:, kind, :], lt[0][:],
                                                      start=True, stop=True)
                            mm.then_inc(gates_summed, 1)

            panels(0, U_RNN, 4)
            panels(1, U_RNN + 16, 4)
            panels(2, U_QKV, 4, 0)
            panels(3, U_GA, 4, 4)

            pe.wait_ge(f_bank_freed, 34)
            for u in range(DT_UNITS):
                pe.wait_ge(lo_ready, U_KR + u + 1)
                for k in range(UKT):
                    kb = u * UKT + k
                    w = [unit_ap(r, u, ROPE)[:, k, :] for r in (w_hi, w_lo)]
                    mm = three(ps[0:ROPE, 0, :], *w, h_hi[:, kb, :], h_lo[:, kb, :], kb == 0, kb == KB - 1)
                mm.then_inc(unit_used, 1)
            pe.wait_ge(kr_taken, 1)
            for t in range(NT):
                mm = nc.tensor.transpose(ps[:, 6, t * ROPE:(t + 1) * ROPE], kpt[0:ROPE, t * P:(t + 1) * P],
                                         ident[0:ROPE, 0:ROPE])
            mm.then_inc(kr_turned, 1)

            def sum_latents():
                for part, sq in enumerate(latent_sq):
                    pe.wait_ge(latent_added, part + 1)
                    for t in range(NT):
                        mm = nc.tensor.matmul(ps[:, 4, part * NT + t:part * NT + t + 1],
                                              sq[:, 0, t * P:(t + 1) * P], ones[:, 0:1], start=True, stop=True)
                    mm.then_inc(latent_summed, 1)

            def turn_kpe():
                pe.wait_ge(kpe_ready, 1)
                for t in range(NT):
                    mm = nc.tensor.transpose(ps[:, 5, t * P:(t + 1) * P],
                                             qpe[:, t, :, :].rearrange("p h n -> p (h n)"), ident[:])
                mm.then_inc(kpe_turned, 1)
                pe.sem_inc(pe_turned, 1)

            def score(gp, k):
                h, qb = divmod(k, NT)
                n = (qb + 1) * P
                at = slice(qb * P, n)
                out_ = ps[:, 4 + k % 2, 0:n]
                if k >= 2:
                    pe.wait_ge(exp_ready, gp * 8 + k - 1)
                nc.tensor.matmul(out_, qt[:, h, at], kt[:, h, 0:n], start=True, stop=False)
                rows = slice(h * ROPE, (h + 1) * ROPE)
                nc.tensor.matmul(out_, qpt[rows, at], kpt[rows, 0:n], start=False, stop=False)
                nc.tensor.matmul(ps[:, 4 + k % 2, qb * P:n], ident[:], maskn[:], start=False, stop=True
                                 ).then_inc(scored, 1)

            def turn_prob(gp, j):
                qb = j % 4
                pe.wait_ge(prob_ready, gp * 8 + j + 1)
                if j:
                    pe.wait_ge(pt_ready, gp * 8 + j)
                for kb in range(qb + 1):
                    mm = nc.tensor.transpose(ps[:, 6, kb * P:(kb + 1) * P], prob[:, j % 2, kb * P:(kb + 1) * P],
                                             ident[:])
                mm.then_inc(prob_turned, 1)

            def head_sum(gp, h):
                pe.wait_ge(pt_ready, gp * 8 + 4 * h + 4)
                if h:
                    pe.wait_ge(head_read, gp * 2 + 1)
                for kb in range(NT):
                    mm = nc.tensor.matmul(ps[:, 7, kb * P:], vt[:, kb, h, :], pt[:, kb, kb * P:],
                                          start=kb == 0, stop=kb == NT - 1)
                mm.then_inc(head_summed, 1)

            def pair(g, prev, cur):
                gp = g - 1
                if prev and cur:
                    pe.wait_ge(qk_ready, 2 * g - 1)
                for k in range(10):
                    if cur and k < 4:
                        half = k % 2
                        if k == 2:
                            pe.wait_ge(q_read, g + 1)
                        if not prev:
                            pe.wait_ge(c_lo_ready, (k + 1) * TKT)
                        if k < 2:
                            tok_unit(g * 4 + (U_PAIR + k + 1), k, 2 * QH, blocks((c_hi, c_lo)), half * TKT, half == 0, half == 1)
                        else:
                            tok_unit(g * 4 + (U_PAIR + k + 1), k, TCOL, blocks((c_hi, c_lo)), LORA_KB + half * TKT,
                                     half == 0, half == 1)
                    if not prev and k == 1:
                        sum_latents()
                    if not prev and k == 3:
                        turn_kpe()
                    if prev and k == 0:
                        pe.wait_ge(qk_ready, 2 * g)
                        pe.wait_ge(v_ready, g)
                    if prev and k < 8:
                        score(gp, k)
                    if prev and k == 6:
                        head_sum(gp, 0)
                    if prev and k >= 2:
                        turn_prob(gp, k - 2)
                if cur:
                    pe.wait_ge(nope_normed, g * 2 + 2)
                    for h in range(2):
                        for t in range(NT):
                            at = slice(t * P, (t + 1) * P)
                            nc.tensor.transpose(ps[:, h, at], q_tok[:, t, h, 0:NOPE], ident[:])
                            mm = nc.tensor.transpose(ps[:, 2 + h, at], kv_tok[:, t, h, 0:NOPE], ident[:])
                    mm.then_inc(pair_turned, 1)
                if prev:
                    head_sum(gp, 1)
                if cur:
                    pe.wait_ge(rope_turned, g + 1)
                    if prev:
                        pe.wait_ge(exp_ready, g * 8)
                    for t in range(NT):
                        mm = nc.tensor.transpose(ps[:, 4, t * P:(t + 1) * P],
                                                 qpe[:, t, :, :].rearrange("p h n -> p (h n)"), ident[:])
                    mm.then_inc(pe_turned, 1)

            pair(0, False, True)
            pe.wait_ge(kpt_ready, 1)
            pe.wait_ge(mask_ready, 1)
            with pe.Fori(1, PAIRS) as g:
                pair(g, True, True)
            pair(PAIRS, True, False)

            with pe.Fori(0, OUT_PANELS) as i:
                for u in range(OUT2_UPP):
                    pe.wait_ge(y2_lo_ready, (u + 1) * TKT)
                    tok_unit(i * OUT2_UPP + (U_OUT2 + u + 1), u % RING, TCOL, blocks((y2_hi, y2_lo)), u * TKT,
                             u == 0, u == OUT2_UPP - 1,
                             lambda t: pe.wait_ge(z_bank_freed, i * NT + t + 1), z_bank_done)


_INS = ["x", "ln_g", "final_g", "ssm_w_in", "ssm_conv_w", "ssm_conv_b", "ssm_dt_bias", "ssm_a_log", "ssm_d",
        "ssm_norm_g", "ssm_w_out", "c_2", "positions_2", "w_ada_2", "b_ada_2", "w_in_2", "conv_w_2", "conv_b_2",
        "w_rg_a_2", "b_rg_a_2", "w_rg_x_2", "b_rg_x_2", "lru_lambda_2", "q_a_norm_2", "w_uq_2", "kv_a_norm_2",
        "w_ukv_2", "q_norm_nope_2", "q_norm_rope_2", "k_norm_nope_2", "k_norm_rope_2", "w_out_2"]


def kernel(**inputs):
    import concourse.bacc as _bacc
    from concourse.bass_utils import run_bass_kernel_spmd as _run

    nc = _bacc.Bacc("TRN2", target_bir_lowering=False, num_devices=1)
    arrays = {f"in_{name}_dram": np.ascontiguousarray(inputs[name]) for name in _INS}
    steps = np.arange(0, ROPE, 2, dtype=np.float32) / np.float32(ROPE)
    arrays["in_inv_freq_dram"] = (np.float32(1.0) / np.power(np.float32(10000.0), steps)).astype(np.float32)
    args = [nc.dram_tensor(name, a.shape, mybir.dt.from_np(a.dtype), kind="ExternalInput").ap()
            for name, a in arrays.items()]
    out = nc.dram_tensor("out_0_dram", (1, SEQ, D), F32, kind="ExternalOutput").ap()
    build_program(nc, *args, out)
    r = _run(nc, [arrays], core_ids=[0])
    return r.results[0]["out_0_dram"]
```
